# Optimizing a Trainium2 kernel written in Bass

```python
import math, functools
import jax, jax.numpy as jnp
from jax import lax
import numpy as np

D_MODEL = 2048
BATCH = 1
SEQ = 256
DEPTH = 1
DEC_BATCH = 8
DEC_SEQ = 1
PAST_LEN = 2048
PAGE_SIZE = 128

N_HEADS = 8
HEAD_DIM = 64
V_DIM = 2 * HEAD_DIM
ATTN_QK_WIDTH = N_HEADS * 2 * HEAD_DIM
ATTN_V_WIDTH = N_HEADS * V_DIM
SSM_WIDTH = D_MODEL // 2
SSM_GROUP = 16
N_GROUPS = SSM_WIDTH // SSM_GROUP
STATE_DIM = 64
D_FF = 5504
CONV_W = 3
NUM_BUCKETS = 32
MAX_EXACT = NUM_BUCKETS // 2
MAX_DISTANCE = 128
Q_BLOCK = 128
LN_EPS = 1e-5
NEG_INF = -1e30
Q_END = ATTN_QK_WIDTH
K_END = 2 * ATTN_QK_WIDTH
V_END = K_END + ATTN_V_WIDTH
U_END = V_END + SSM_WIDTH
GA_END = U_END + D_MODEL
IN_WIDTH = GA_END + D_MODEL

kernel_name = 'diffattn_s5_gated_convffn_deepnorm_step'

def layer_norm(x, g, b):
    xf = x.astype(jnp.float32)
    mu = jnp.mean(xf, axis=-1, keepdims=True)
    var = jnp.mean(jnp.square(xf - mu), axis=-1, keepdims=True)
    return ((xf - mu) * lax.rsqrt(var + LN_EPS) * g.astype(jnp.float32) + b.astype(jnp.float32)).astype(x.dtype)

def rms_norm(x, g):
    xf = x.astype(jnp.float32)
    return (xf * lax.rsqrt(jnp.mean(jnp.square(xf), axis=-1, keepdims=True) + LN_EPS) * g.astype(jnp.float32)).astype(x.dtype)

def rel_bucket(q_pos, k_pos):
    n = jnp.maximum(q_pos[:, None] - k_pos[None, :], 0)
    nf = jnp.maximum(n, 1).astype(jnp.float32)
    large = MAX_EXACT + (jnp.log(nf / MAX_EXACT) / math.log(MAX_DISTANCE / MAX_EXACT) * (NUM_BUCKETS - MAX_EXACT)).astype(jnp.int32)
    large = jnp.minimum(large, NUM_BUCKETS - 1)
    return jnp.where(n < MAX_EXACT, n, large)

def diff_attention(q, k, v, q_pos, k_pos, rel_bias, lam):
    s = jnp.einsum('bqhjd,bkhjd->bhjqk', q, k).astype(jnp.float32) * (HEAD_DIM ** -0.5)
    bias = jnp.transpose(rel_bias[rel_bucket(q_pos, k_pos)], (2, 0, 1)).astype(jnp.float32)
    causal = k_pos[None, :] <= q_pos[:, None]
    s = jnp.where(causal, s + bias[None, :, None], NEG_INF)
    p = jax.nn.softmax(s, axis=-1)
    p_diff = p[:, :, 0] - lam * p[:, :, 1]
    return jnp.einsum('bhqk,bkhe->bqhe', p_diff.astype(v.dtype), v)

def prompt_attention(q, k, v, rel_bias, lam):
    b, seq = q.shape[0], q.shape[1]
    n_blocks = seq // Q_BLOCK
    q_blocks = jnp.moveaxis(q.reshape(b, n_blocks, Q_BLOCK, N_HEADS, 2, HEAD_DIM), 1, 0)
    k_pos = jnp.arange(seq, dtype=jnp.int32)

    def one_block(args):
        idx, q_blk = args
        q_pos = idx * Q_BLOCK + jnp.arange(Q_BLOCK, dtype=jnp.int32)
        return diff_attention(q_blk, k, v, q_pos, k_pos, rel_bias, lam)

    out = lax.map(one_block, (jnp.arange(n_blocks, dtype=jnp.int32), q_blocks))
    return jnp.moveaxis(out, 0, 1).reshape(b, seq, N_HEADS, V_DIM)

def sample_attention(k_past, v_past, q, k, v, rel_bias, lam):
    past = k_past.shape[1]
    n_new = q.shape[1]
    k_all = jnp.concatenate([k_past.astype(k.dtype), k], axis=1)
    v_all = jnp.concatenate([v_past.astype(v.dtype), v], axis=1)
    q_pos = past + jnp.arange(n_new, dtype=jnp.int32)
    k_pos = jnp.arange(past + n_new, dtype=jnp.int32)
    return diff_attention(q, k_all, v_all, q_pos, k_pos, rel_bias, lam)

def s5_branch(u, x0_re, x0_im, a_re, a_im, log_dt, b_re, b_im, c_re, c_im, d, w_glu):
    b, seq = u.shape[0], u.shape[1]
    ug = u.reshape(b, seq, N_GROUPS, SSM_GROUP)
    dt = jnp.exp(log_dt)[:, None]
    mag = jnp.exp(a_re * dt)
    ang = a_im * dt
    abar_re = mag * jnp.cos(ang)
    abar_im = mag * jnp.sin(ang)
    den = a_re * a_re + a_im * a_im
    f_re = ((abar_re - 1.0) * a_re + abar_im * a_im) / den
    f_im = (abar_im * a_re - (abar_re - 1.0) * a_im) / den
    bb_re = f_re[..., None] * b_re - f_im[..., None] * b_im
    bb_im = f_re[..., None] * b_im + f_im[..., None] * b_re
    bu_re = jnp.einsum('blgc,gpc->blgp', ug, bb_re)
    bu_im = jnp.einsum('blgc,gpc->blgp', ug, bb_im)
    a_seq_re = jnp.broadcast_to(abar_re, bu_re.shape)
    a_seq_im = jnp.broadcast_to(abar_im, bu_im.shape)

    def combine(e1, e2):
        a1r, a1i, b1r, b1i = e1
        a2r, a2i, b2r, b2i = e2
        return (a2r * a1r - a2i * a1i,
                a2r * a1i + a2i * a1r,
                a2r * b1r - a2i * b1i + b2r,
                a2r * b1i + a2i * b1r + b2i)

    acum_re, acum_im, s_re, s_im = lax.associative_scan(combine, (a_seq_re, a_seq_im, bu_re, bu_im), axis=1)
    x_re = s_re + acum_re * x0_re[:, None] - acum_im * x0_im[:, None]
    x_im = s_im + acum_re * x0_im[:, None] + acum_im * x0_re[:, None]
    y = jnp.einsum('blgp,gcp->blgc', x_re, c_re) - jnp.einsum('blgp,gcp->blgc', x_im, c_im)
    y = y.reshape(b, seq, SSM_WIDTH) + d * u
    g = jax.nn.gelu(y)
    return g * jax.nn.sigmoid(g @ w_glu), x_re[:, -1], x_im[:, -1]

def conv_ffn(h, conv0, w_up, conv_w, conv_b, w_down):
    seq = h.shape[1]
    up = h @ w_up
    padded = jnp.concatenate([conv0.astype(up.dtype), up], axis=1)
    c = conv_b
    for j in range(CONV_W):
        c = c + conv_w[j] * padded[:, j:j + seq]
    gate, val = jnp.split(c, 2, axis=-1)
    return (jax.nn.silu(gate) * val) @ w_down, padded[:, -(CONV_W - 1):]

def decoder_layer(x, attend, ssm_re0, ssm_im0, conv0, layer_idx, rel_bias, layer_weights):
    (w_in, lambda_q1, lambda_k1, lambda_q2, lambda_k2, subln_g, ssm_a_re, ssm_a_im, ssm_log_dt,
     ssm_b_re, ssm_b_im, ssm_c_re, ssm_c_im, ssm_d, w_glu, w_proj_attn, w_proj_ssm, w_out,
     ln1_g, ln1_b, w_up, conv_w, conv_b, w_down, ln2_g, ln2_b) = layer_weights
    b, seq = x.shape[0], x.shape[1]
    alpha = (2.0 * DEPTH) ** 0.25
    lam_init = 0.8 - 0.6 * math.exp(-0.3 * layer_idx)
    z = x @ w_in
    q = z[..., :Q_END].reshape(b, seq, N_HEADS, 2, HEAD_DIM)
    k = z[..., Q_END:K_END].reshape(b, seq, N_HEADS, 2, HEAD_DIM)
    v = z[..., K_END:V_END].reshape(b, seq, N_HEADS, V_DIM)
    u = z[..., V_END:U_END]
    gate_a = jax.nn.sigmoid(z[..., U_END:GA_END])
    gate_s = jax.nn.sigmoid(z[..., GA_END:])
    lam = (jnp.exp(jnp.sum(lambda_q1.astype(jnp.float32) * lambda_k1.astype(jnp.float32)))
           - jnp.exp(jnp.sum(lambda_q2.astype(jnp.float32) * lambda_k2.astype(jnp.float32))) + lam_init)
    attn = rms_norm(attend(q, k, v, rel_bias, lam), subln_g) * (1.0 - lam_init)
    attn = attn.reshape(b, seq, ATTN_V_WIDTH)
    ssm, s_re, s_im = s5_branch(u, ssm_re0, ssm_im0, ssm_a_re, ssm_a_im, ssm_log_dt,
                                ssm_b_re, ssm_b_im, ssm_c_re, ssm_c_im, ssm_d, w_glu)
    merged = gate_a * (attn @ w_proj_attn) + gate_s * (ssm @ w_proj_ssm)
    h = layer_norm(alpha * x + merged @ w_out, ln1_g, ln1_b)
    ffn, conv_new = conv_ffn(h, conv0, w_up, conv_w, conv_b, w_down)
    y = layer_norm(alpha * h + ffn, ln2_g, ln2_b)
    return y, k, v, s_re, s_im, conv_new

def setup_inputs(seed: int = 0) -> dict:
    key = jax.random.key(seed)
    ks = jax.random.split(key, 40)
    f32 = jnp.float32
    beta = (8.0 * DEPTH) ** -0.25
    n_pages = PAST_LEN // PAGE_SIZE
    n_used = DEC_BATCH * n_pages
    n_pool = (n_used * 5) // 4

    def nrm(k, shape, scale=1.0):
        return jax.random.normal(k, shape, f32) * scale

    col_scale = jnp.concatenate([jnp.ones((K_END,), f32),
                                 jnp.full((ATTN_V_WIDTH + SSM_WIDTH,), beta, f32),
                                 jnp.ones((2 * D_MODEL,), f32)])
    page_table = jax.random.permutation(ks[5], n_pool)[:n_used].reshape(DEC_BATCH, n_pages).astype(jnp.int32)
    a_im_init = jnp.pi * jnp.arange(STATE_DIM, dtype=f32)
    return {
        'x_prompt': nrm(ks[0], (BATCH, SEQ, D_MODEL)),
        'x_sample': nrm(ks[1], (DEC_BATCH, DEC_SEQ, D_MODEL)),
        'cache_k': nrm(ks[2], (DEPTH, n_pool, PAGE_SIZE, N_HEADS, 2, HEAD_DIM)),
        'cache_v': nrm(ks[3], (DEPTH, n_pool, PAGE_SIZE, N_HEADS, V_DIM), beta),
        'state_ssm_re': nrm(ks[4], (DEPTH, DEC_BATCH, N_GROUPS, STATE_DIM), 0.3),
        'state_ssm_im': nrm(ks[6], (DEPTH, DEC_BATCH, N_GROUPS, STATE_DIM), 0.3),
        'state_conv': nrm(ks[7], (DEPTH, DEC_BATCH, CONV_W - 1, 2 * D_FF), beta),
        'page_table': page_table,
        'rel_bias': nrm(ks[8], (NUM_BUCKETS, N_HEADS), 0.5),
        'w_in': nrm(ks[9], (DEPTH, D_MODEL, IN_WIDTH), D_MODEL ** -0.5) * col_scale,
        'lambda_q1': nrm(ks[10], (DEPTH, HEAD_DIM), 0.1),
        'lambda_k1': nrm(ks[11], (DEPTH, HEAD_DIM), 0.1),
        'lambda_q2': nrm(ks[12], (DEPTH, HEAD_DIM), 0.1),
        'lambda_k2': nrm(ks[13], (DEPTH, HEAD_DIM), 0.1),
        'subln_g': 1.0 + nrm(ks[14], (DEPTH, V_DIM), 0.02),
        'ssm_a_re': -0.5 + nrm(ks[15], (DEPTH, N_GROUPS, STATE_DIM), 0.02),
        'ssm_a_im': a_im_init + nrm(ks[16], (DEPTH, N_GROUPS, STATE_DIM), 0.02),
        'ssm_log_dt': jax.random.uniform(ks[17], (DEPTH, N_GROUPS), f32, minval=math.log(1e-3), maxval=math.log(1e-1)),
        'ssm_b_re': nrm(ks[18], (DEPTH, N_GROUPS, STATE_DIM, SSM_GROUP), (2 * SSM_GROUP) ** -0.5),
        'ssm_b_im': nrm(ks[19], (DEPTH, N_GROUPS, STATE_DIM, SSM_GROUP), (2 * SSM_GROUP) ** -0.5),
        'ssm_c_re': nrm(ks[20], (DEPTH, N_GROUPS, SSM_GROUP, STATE_DIM), (2 * STATE_DIM) ** -0.5),
        'ssm_c_im': nrm(ks[21], (DEPTH, N_GROUPS, SSM_GROUP, STATE_DIM), (2 * STATE_DIM) ** -0.5),
        'ssm_d': nrm(ks[22], (DEPTH, SSM_WIDTH)),
        'w_glu': nrm(ks[23], (DEPTH, SSM_WIDTH, SSM_WIDTH), SSM_WIDTH ** -0.5),
        'w_proj_attn': nrm(ks[24], (DEPTH, ATTN_V_WIDTH, D_MODEL), beta * ATTN_V_WIDTH ** -0.5),
        'w_proj_ssm': nrm(ks[25], (DEPTH, SSM_WIDTH, D_MODEL), beta * SSM_WIDTH ** -0.5),
        'w_out': nrm(ks[26], (DEPTH, D_MODEL, D_MODEL), beta * D_MODEL ** -0.5),
        'ln1_g': 1.0 + nrm(ks[27], (DEPTH, D_MODEL), 0.02),
        'ln1_b': nrm(ks[28], (DEPTH, D_MODEL), 0.02),
        'w_up': nrm(ks[29], (DEPTH, D_MODEL, 2 * D_FF), beta * D_MODEL ** -0.5),
        'conv_w': nrm(ks[30], (DEPTH, CONV_W, 2 * D_FF), CONV_W ** -0.5),
        'conv_b': nrm(ks[31], (DEPTH, 2 * D_FF), 0.02),
        'w_down': nrm(ks[32], (DEPTH, D_FF, D_MODEL), beta * D_FF ** -0.5),
        'ln2_g': 1.0 + nrm(ks[33], (DEPTH, D_MODEL), 0.02),
        'ln2_b': nrm(ks[34], (DEPTH, D_MODEL), 0.02),
    }

def reference(x_prompt, x_sample, cache_k, cache_v, state_ssm_re, state_ssm_im, state_conv, page_table,
              rel_bias, w_in, lambda_q1, lambda_k1, lambda_q2, lambda_k2, subln_g, ssm_a_re, ssm_a_im,
              ssm_log_dt, ssm_b_re, ssm_b_im, ssm_c_re, ssm_c_im, ssm_d, w_glu, w_proj_attn, w_proj_ssm,
              w_out, ln1_g, ln1_b, w_up, conv_w, conv_b, w_down, ln2_g, ln2_b):
    bp = x_prompt.shape[0]
    bs = x_sample.shape[0]
    n_pages = page_table.shape[1]
    h_p = x_prompt
    h_s = x_sample
    kp_l, vp_l, rep_l, imp_l, cp_l = [], [], [], [], []
    ks_l, vs_l, res_l, ims_l, cs_l = [], [], [], [], []
    for l in range(DEPTH):
        lw = (w_in[l], lambda_q1[l], lambda_k1[l], lambda_q2[l], lambda_k2[l], subln_g[l], ssm_a_re[l],
              ssm_a_im[l], ssm_log_dt[l], ssm_b_re[l], ssm_b_im[l], ssm_c_re[l], ssm_c_im[l], ssm_d[l],
              w_glu[l], w_proj_attn[l], w_proj_ssm[l], w_out[l], ln1_g[l], ln1_b[l], w_up[l], conv_w[l],
              conv_b[l], w_down[l], ln2_g[l], ln2_b[l])
        zero_ssm = jnp.zeros((bp, N_GROUPS, STATE_DIM), x_prompt.dtype)
        zero_conv = jnp.zeros((bp, CONV_W - 1, 2 * D_FF), x_prompt.dtype)
        h_p, k_p, v_p, re_p, im_p, c_p = decoder_layer(h_p, prompt_attention, zero_ssm, zero_ssm, zero_conv,
                                                       l, rel_bias, lw)
        k_past = cache_k[l][page_table].reshape(bs, n_pages * PAGE_SIZE, N_HEADS, 2, HEAD_DIM)
        v_past = cache_v[l][page_table].reshape(bs, n_pages * PAGE_SIZE, N_HEADS, V_DIM)
        h_s, k_s, v_s, re_s, im_s, c_s = decoder_layer(h_s, functools.partial(sample_attention, k_past, v_past),
                                                       state_ssm_re[l], state_ssm_im[l], state_conv[l],
                                                       l, rel_bias, lw)
        kp_l.append(k_p); vp_l.append(v_p); rep_l.append(re_p); imp_l.append(im_p); cp_l.append(c_p)
        ks_l.append(k_s); vs_l.append(v_s); res_l.append(re_s); ims_l.append(im_s); cs_l.append(c_s)
    new_k_prompt = jnp.stack(kp_l, axis=0)
    new_v_prompt = jnp.stack(vp_l, axis=0)
    new_ssm_re_prompt = jnp.stack(rep_l, axis=0)
    new_ssm_im_prompt = jnp.stack(imp_l, axis=0)
    new_conv_prompt = jnp.stack(cp_l, axis=0)
    new_k_sample = jnp.stack(ks_l, axis=0)
    new_v_sample = jnp.stack(vs_l, axis=0)
    new_ssm_re_sample = jnp.stack(res_l, axis=0)
    new_ssm_im_sample = jnp.stack(ims_l, axis=0)
    new_conv_sample = jnp.stack(cs_l, axis=0)
    return (h_p, h_s, new_k_prompt, new_v_prompt, new_ssm_re_prompt, new_ssm_im_prompt, new_conv_prompt,
            new_k_sample, new_v_sample, new_ssm_re_sample, new_ssm_im_sample, new_conv_sample)


_drawn_inputs = setup_inputs


def setup_inputs(seed=0):
    import zlib

    import numpy as np

    out = dict(_drawn_inputs(seed))
    spreads = {}
    factors = {'lambda_q1': 200.0,
     'lambda_q2': 47.248,
     'lambda_k2': 21.888,
     'subln_g': 30.384,
     'ssm_c_re': 5.455,
     'ssm_c_im': 5.489,
     'w_glu': 8.0,
     'ln1_g': 7.473,
     'ln1_b': 16.84,
     'conv_b': 8.0,
     'ln2_g': 22.65,
     'ln2_b': 22.923,
     'ssm_d': 3.903}
    for name, (base, spread) in spreads.items():
        noise = np.random.default_rng([zlib.crc32(name.encode()), seed]).standard_normal(out[name].shape)
        drawn = base * np.exp(spread * noise) if base else spread * noise
        out[name] = __import__('jax').numpy.asarray(drawn.astype(out[name].dtype))
    for name, factor in factors.items():
        out[name] = (out[name] * factor).astype(out[name].dtype)
    return out
```

```python
from contextlib import ExitStack

import numpy as np

import concourse.bass as bass
from concourse import mybir

ALU = mybir.AluOpType
ACT = mybir.ActivationFunctionType
AX = mybir.AxisListType
F32 = mybir.dt.float32
I32 = mybir.dt.int32

P = 128
D = 2048
T = 256
B = 8
N = T + B
H = 8
HD = 64
PAGES = 16
POOL_PAGES = 160
KW = H * 2 * HD
SW = 1024
G = 64
S = 64
C = 16
PAIRS = G // 2
FF = 5504
FT = FF // P
KT = D // P
HT = SW // P
NB = 32
SLOTS = 4
DOWN_A = 22
DOWN_B = FT - DOWN_A
ALPHA = 2.0 ** 0.25
EPS = 1e-5
LAM_INIT = 0.2
MASK = -1e30
PI = float(np.pi)
TWO_PI_DOWN = 6.2831845
MEAN_SHIFT = 1.0 / D

TOEP = 383
OH_TOEP, OH_PAGE, OH_NEW = 0, 384, 384 + PAGES * P
OH_COLS = OH_NEW + B * P


def bucket_table():
    def bucket(n):
        n = np.maximum(n, 0)
        large = 16 + (np.log(np.maximum(n, 1).astype(np.float32) / np.float32(16)) / np.float32(np.log(8.0))
                      * np.float32(16)).astype(np.int32)
        return np.where(n < 16, n, np.minimum(large, NB - 1))

    table = np.zeros((NB + 1, OH_COLS), np.float32)

    def mark(cols, dist):
        row = np.where(dist < 0, NB, bucket(dist))
        table[row, cols] = 1.0

    y = np.arange(TOEP)
    mark(OH_TOEP + y, 255 - y)
    k = np.arange(PAGES * P)
    mark(OH_PAGE + k, PAGES * P - k)
    for b in range(B):
        r = np.arange(P)
        mark(OH_NEW + b * P + r, np.where(r == b, 0, -1))
    return table


def wait(eng, sem, value):
    if isinstance(value, int) and value <= 0:
        return
    eng.wait_ge(sem, value)


class Chain:

    def __init__(self, eng, sem):
        self.eng, self.sem, self.base, self.n = eng, sem, 0, 0

    def did(self, ins):
        ins.then_inc(self.sem, 1)
        self.n += 1
        return self.n

    def wait(self, n=None):
        wait(self.eng, self.sem, self.base + (self.n if n is None else n))

    def enter(self, i, first, per):
        self.outer, self.per = self.base + self.n, per
        self.base, self.n = self.outer + (i - first) * per, 0

    def leave(self, turns):
        assert self.n == self.per, (self.n, self.per)
        self.base, self.n = self.outer + turns * self.per, 0


def build(nc, a, out, scratch):
    with ExitStack() as ctx:
        def sb(name, cols, dt=F32, rows=P):
            return ctx.enter_context(nc.sbuf_tensor(name, [rows, cols], dt))

        def sem(name):
            return ctx.enter_context(nc.semaphore(name))

        w_in, w_glu, w_pa, w_ps, w_out, w_up, w_down = (
            a[name][0] for name in ("w_in", "w_glu", "w_proj_attn", "w_proj_ssm", "w_out", "w_up", "w_down"))

        ring = sb("weight_ring", SLOTS * KT * P)
        xt = sb("x_t", KT * N)
        big = sb("big", FT * N)
        gd = sb("gates_or_down", SLOTS * DOWN_A * P)
        mm = sb("matrices_or_merged", KT * N)
        att = sb("att", H * N)
        yg = sb("ssm_y", HT * N)
        c_rows = sb("c_rows", 2 * HT * P)
        conv_state = sb("conv_state_t", 2 * FT * 2 * B)
        conv_par = sb("conv_par", 4 * 2 * FT)
        par_rows = sb("parameter_rows", 4 * P)
        ln_par = sb("ln_par", 4 * KT)
        kv_new = sb("kv_new", 2 * KW)
        q_s = sb("q_sample", H * B)
        x0_rows = sb("x0_rows", 4 * P)
        x0 = sb("x0", 4 * P)
        xf = sb("x_final", 2 * 9 * PAIRS)
        ln_rows = xf[:, 0:4 * P]
        ident = sb("ident", P)
        ones = sb("ones", P)
        mean_w = sb("mean_w", P)
        v_mean_w = sb("v_mean_w", P)
        small = sb("small", 592)
        bias_pg = sb("bias_pages", PAGES * H)
        bias_nw = sb("bias_new", B * H)
        scan_par = sb("scan_par", 7 * PAIRS)
        score, prob = mm[:, KW:KW + 272], mm[:, KW + 272:KW + 544]
        page_no = sb("page_numbers", B * PAGES, I32, rows=1)
        multiples_i = q_s[:, 0:32].bitcast(I32)

        bank = [ctx.enter_context(nc.psum_tensor(f"bank{i}", [P, 512], F32)) for i in range(8)]

        def slot(j, kt):
            return ring[:, (j * KT + kt) * P:(j * KT + kt + 1) * P]

        def slot3(j, k0, k1):
            return ring[:, (j * KT + k0) * P:(j * KT + k1) * P].rearrange("p (k m) -> p k m", m=P)

        def down_slot(j, kt):
            return gd[:, (j * DOWN_A + kt) * P:(j * DOWN_A + kt + 1) * P]

        def xtile(k):
            return xt[:, k * N:(k + 1) * N]

        x3 = xt[:, :].rearrange("p (k n) -> p k n", n=N)
        x_rows = big[:, 0:3 * D].rearrange("p (c d) -> p c d", c=3)
        k_ring = [big[:, i * KW:(i + 1) * KW] for i in range(4)]
        v_ring = [big[:, (4 + i) * KW:(5 + i) * KW] for i in range(4)]
        kq = [big[:, (8 + i) * KW:(9 + i) * KW] for i in range(2)]
        q_all = big[:, 10 * KW:11 * KW]
        st_rows = gd[0:2 * B, 0:2 * FF]
        k_new, v_new = kv_new[:, 0:KW], kv_new[:, KW:2 * KW]
        gate = gd[:, 0:2 * KT * N]
        merged = mm
        diag_q = mm[:, 0:KW]
        hid = big

        def cutter(tensor, start, end):
            at = [start]

            def cut(cols):
                at[0] += cols
                assert at[0] <= end
                return tensor[:, at[0] - cols:at[0]]
            return cut

        gcut = cutter(gd, 0, SLOTS * DOWN_A * P)
        bias = gcut(H * 384)
        u_all = gcut(HT * N)
        q_t, k_t, v_t, u_t = gcut(N), gcut(N), gcut(N), gcut(N)
        s_sb, p_sb = gcut(768), gcut(768)
        p_diff, p_diff_t = gcut(384), gcut(384)
        v_rows, k_rows = gcut(256), gcut(256)
        toep_rows = gcut(384)
        bcut = cutter(big, 4 * KW, FT * N)
        tab = [bcut(512) for _ in range(2)]
        rot = [bcut(256) for _ in range(4)]
        z_re, z_im, y_re, y_im = bcut(256), bcut(256), bcut(256), bcut(256)
        x_st = [bcut(2 * N) for _ in range(2)]
        ptmp = c_rows[:, 0:1024]
        mst = bcut(512)
        ang = bcut(2048)
        MT = mm[:, 0:HT * 512].rearrange("p (t c) -> p t c", t=HT)
        fcut = cutter(att, 0, H * N)
        acc = [fcut(N) for _ in range(4)]
        th = [fcut(N) for _ in range(2)]
        up10 = fcut(40)
        up_rows = yg[0:10, 0:512]
        cent_sq = c_rows[:, 0:4 * N]
        std_sb = yg[:, 512:512 + N]

        def sems(*names):
            return [sem(n) for n in names]

        ring_in = sems(*(f"weights_in{j}" for j in range(SLOTS)))
        down_in = sems(*(f"down_in{j}" for j in range(4)))
        k_in = sems(*(f"k_in{j}" for j in range(4)))
        v_in = sems(*(f"v_in{j}" for j in range(4)))
        xs_in, tab_in, par_in, st_in = sems("x_in", "table_in", "params_in", "state_in")
        rows_in, b_in, c_in, x0_in, page_in = sems("scan_rows_in", "b_in", "c_in", "x0_in", "pages_in")
        toep_out, toep_in = sems("toeplitz_out", "toeplitz_in")
        kv_stored, out_stored, upr_stored, y_stored = sems("kv_stored", "out_stored", "up_rows_stored", "y_stored")
        x_zero, rel_ready, const_ready, mt_zero = sems("x_rows_zeroed", "rel_ready", "constants_ready", "matrices_zeroed")
        bpad_zero, mult_ready = sems("b_padding_zeroed", "angle_multiples")
        tr, tr_used = sems("setup_transposed", "setup_copied")
        s5_tr, s5_used, s5_act, s5_dve = sems("s5_transposed", "s5_copied", "s5_act_steps", "s5_dve_steps")
        kv_zero, lam_exp = sems("kv_new_zeroed", "lambda_exp")
        pool_c, dve_c, act_c = sems("pool_chain", "dve_chain", "act_chain")
        slot_done, z_read, zv_read = sems("m_tiles_done", "m_tiles_read_by_act", "m_tiles_read_by_dve")
        kt_done, kt_read, vt_done, vt_read = sems("k_transposed", "k_rows_copied", "v_transposed", "v_rows_copied")
        sc_done, max_ready, exp_done = sems("scores_done", "max_ready", "exp_done")
        pd_ready, pdt_done, pdt_read, pv_done, pv_read = sems(
            "p_diff_ready", "p_diff_transposed", "p_diff_copied", "pv_done", "pv_read")
        mst_ready, tab_ready, b_done, b_read, xs_ready, c_done, xf_read, y_ready = sems(
            "matrices_staged", "rotation_ready", "bu_done", "bu_read", "states_ready", "y_sums_done",
            "final_states_read", "y_ready")
        xft, xft_read = sems("final_states_transposed", "final_states_copied")
        dq_ready, qb_done, qb_ready, kq_ready, kq_read = sems(
            "diag_q_ready", "q_broadcast", "q_broadcast_copied", "kq_ready", "kq_reduced")
        smax_ready, gmax_ready, ssub_ready, sexp_ready, lsum_ready, lsum_done, spv_done, v_used, o_read = sems(
            "page_max_ready", "global_max_ready", "shifted_ready", "sample_exp_ready", "page_sum_ready",
            "denominator_ready", "sample_pv_done", "v_pages_used", "sample_out_read")
        gelu_act, gelu_dve = sems("gelu_act", "gelu_dve")
        sq_ready, ms_done, root_ready, att_ready, glu_t, ssm_ready, merged_ready, r_ready = sems(
            "squares_ready", "mean_squares", "roots_ready", "att_ready", "glu_tanh", "ssm_ready", "merged_ready",
            "residual_ready")
        mean_done, cent_ready, csq_ready, var_done, std_ready, norm_ready, h_ready = sems(
            "mean_done", "centred", "centred_squares", "var_done", "std_ready", "normalised", "h_ready")
        tap0, tap_done, th_ready, th_used, hid_ready = sems("tap0", "taps_done", "tanh_ready", "tanh_used", "hidden_ready")
        upt_done, upt_read, down_used, yt_done, yt_read = sems(
            "up_rows_transposed", "up_rows_copied", "down_slots_used", "y_transposed", "y_copied")
        block = ctx.enter_context(nc.Block())

        L1, L2 = 4 * H, 8 * H
        GLU, PROJ, OUT = L2 + HT, L2 + HT + KT, L2 + HT + 2 * KT
        UP = OUT + 2 * FT

        @block.sync
        def _(sp):
            def load_slot(n, j, *parts):
                wait(sp, slot_done, n - SLOTS + 1)
                k0 = 0
                for w, rows, col in parts:
                    src = w[0:rows, bass.ds(col, P)].rearrange("(k p) m -> p k m", p=P)
                    sp.dma_start(slot3(j, k0, k0 + rows // P), src).then_inc(ring_in[j], 16)
                    k0 += rows // P

            def load_head(i):
                for j in range(4):
                    load_slot(4 * i + j, j, (w_in, D, i * P + j * SW))

            sp.dma_start(x_rows[:, 0:2, :], a["x_prompt"][0].rearrange("(c p) d -> p c d", p=P)).then_inc(xs_in, 16)
            sp.wait_ge(x_zero, 1)
            sp.dma_start(x_rows[0:B, 2, :], a["x_sample"].rearrange("b o d -> (b o) d")).then_inc(xs_in, 16)
            for n, name in enumerate(("ssm_a_re", "ssm_a_im")):
                sp.dma_start(yg[0:PAIRS, n * P:(n + 1) * P],
                             a[name][0].rearrange("(q g) s -> q (g s)", g=2)).then_inc(rows_in, 16)
            sp.dma_start(small[0:PAIRS, 0:2],
                         a["ssm_log_dt"].rearrange("o (q g) -> (o q) g", g=2)).then_inc(rows_in, 16)
            load_slot(0, 0, (w_in, D, 0))
            for n, name in enumerate(("ssm_c_re", "ssm_c_im")):
                rows = c_rows[:, n * 1024:(n + 1) * 1024].rearrange("p (t e s) -> p t e s", t=HT, e=2)
                src = a[name][0].rearrange("(t g) c s -> (g c) t s", t=HT)
                for e in range(2):
                    sp.dma_start(rows[:, :, e, :], src).then_inc(c_in, 16)
            for n, name in enumerate(("ssm_b_re", "ssm_b_im")):
                sp.dma_start(att[:, n * 512:(n + 1) * 512].rearrange("p (q c) -> p q c", c=C),
                             a[name][0].rearrange("(q g) s c -> (g s) q c", g=2)).then_inc(b_in, 16)
            for r, name in enumerate(("state_ssm_re", "state_ssm_im")):
                for h in range(2):
                    sp.dma_start(x0_rows[:, (2 * r + h) * P:(2 * r + h + 1) * P],
                                 a[name][0, 4 * h:4 * h + 4].rearrange("b (q g) s -> (b q) (g s)", g=2)
                                 ).then_inc(x0_in, 16)
            load_slot(1, 1, (w_in, D, SW))
            sp.dma_start(par_rows[0:2 * FT, 0:3 * P].rearrange("t (w p) -> t w p", w=3),
                         a["conv_w"][0].rearrange("w (t p) -> t w p", p=P)).then_inc(par_in, 16)
            sp.dma_start(par_rows[0:2 * FT, 3 * P:4 * P],
                         a["conv_b"].rearrange("o (t p) -> (o t) p", p=P)).then_inc(par_in, 16)
            for n, name in enumerate(("ln1_g", "ln1_b", "ln2_g", "ln2_b")):
                sp.dma_start(ln_rows[0:KT, n * P:(n + 1) * P],
                             a[name].rearrange("o (t p) -> (o t) p", p=P)).then_inc(par_in, 16)
            for n, name in enumerate(("lambda_q1", "lambda_k1", "lambda_q2", "lambda_k2")):
                sp.dma_start(small[:, 64 + n * HD:64 + (n + 1) * HD],
                             a[name].to_broadcast([P, HD])).then_inc(par_in, 16)
            with nc.allow_non_contiguous_dma("one column each"):
                sp.dma_start(small[:, 16:24], a["ssm_d"].rearrange("o (t p) -> p (o t)", p=P)).then_inc(par_in, 16)
                sp.dma_start(small[:, 24:25], a["subln_g"].rearrange("o p -> p o")).then_inc(par_in, 16)
            sp.dma_start(st_rows, a["state_conv"][0].rearrange("b i f -> (b i) f")).then_inc(st_in, 16)
            sp.dma_start(mm[0:NB + 1, 0:OH_COLS], a["buckets"]).then_inc(tab_in, 16)
            sp.wait_ge(rel_ready, 1)
            sp.dma_start(small[0:NB, 32:32 + H], a["rel_bias"]).then_inc(tab_in, 16)
            sp.dma_start(page_no[0:1, :], a["page_table"].rearrange("(o b) g -> o (b g)", o=1)).then_inc(page_in, 16)
            sp.dma_start(out["conv_sample"][0, :, 0, :], a["state_conv"][0, :, 1, :]).then_inc(out_stored, 16)
            load_slot(2, 2, (w_in, D, 2 * SW))
            load_slot(3, 3, (w_in, D, 3 * SW))
            sp.wait_ge(tr_used, 22)
            sp.dma_start(scratch, toep_rows[0:H, :].unsqueeze(1).to_broadcast([H, P, 384])).then_inc(toep_out, 16)
            sp.wait_ge(toep_out, 16)
            b3 = bias.rearrange("p (h x) -> p h x", h=H)
            sp.dma_start(b3[:, :, 0:256],
                         bass.AP(scratch.tensor, P - 1, [[383, P], [384 * P, H], [1, 256]])).then_inc(toep_in, 16)
            sp.dma_start(b3[:, :, 256:384],
                         bass.AP(scratch.tensor, 2 * P - 1, [[383, P], [384 * P, H], [1, P]])).then_inc(toep_in, 16)

            def store_head(i):
                sp.wait_ge(kt_read, i + 1)
                sp.wait_ge(vt_read, i + 1)
                for rows, name in ((k_rows, "k_prompt"), (v_rows, "v_prompt")):
                    sp.dma_start(out[name].rearrange("(c p) k -> p c k", p=P)[:, :, bass.ds(i * P, P)],
                                 rows.rearrange("p (c d) -> p c d", c=2)).then_inc(kv_stored, 16)

            with sp.Fori(1, H) as i:
                load_head(i)
                store_head(i - 1)

            ck = a["cache_k"][0].rearrange("n p h j d -> n p (h j d)")
            cv = a["cache_v"][0].rearrange("n p h e -> n p (h e)")

            def load_page(cache, ring4, arrived, b, p):
                page = sp.value_load(page_no[0:1, bass.ds(b * PAGES + p, 1)], min_val=0, max_val=POOL_PAGES - 1)
                sp.dma_start(ring4[p % 4], cache[bass.ds(page, 1)].rearrange("o p k -> (o p) k")
                             ).then_inc(arrived[p % 4], 16)

            def load_batch(b, keys, values):
                for p in range(PAGES):
                    if keys:
                        wait(sp, kq_ready, 17 * b + p - 3 if p >= 4 else 17 * (b - 1) + 12 + p + 1)
                        load_page(ck, k_ring, k_in, b, p)
                    if values:
                        wait(sp, v_used, PAGES * (b - 1) + p - 3)
                        load_page(cv, v_ring, v_in, b - 1, p)
                    if keys and p % 4 == 3:
                        r = p // 4
                        load_slot(L1 + 4 * b + r, r, (w_in, D, 4 * SW + b * 4 * P + r * P))

            sp.wait_ge(page_in, 16)
            load_batch(0, True, False)
            store_head(H - 1)
            sp.wait_ge(xft_read, 2)
            for r, name in enumerate(("ssm_re_prompt", "ssm_im_prompt")):
                sp.dma_start(out[name], par_rows[0:PAIRS, r * P:(r + 1) * P]).then_inc(out_stored, 16)
            for r, name in enumerate(("ssm_re_sample", "ssm_im_sample")):
                for h in range(2):
                    sp.dma_start(out[name][h * P:(h + 1) * P, :],
                                 x0_rows[:, (2 * r + h) * P:(2 * r + h + 1) * P]).then_inc(out_stored, 16)
            sp.dma_start(out["k_sample"], k_new[0:B, :]).then_inc(out_stored, 16)
            sp.dma_start(out["v_sample"], v_new[0:B, :]).then_inc(out_stored, 16)
            load_batch(1, True, True)
            with sp.Fori(2, B) as b:
                load_batch(b, True, True)
            load_batch(B, False, True)
            with sp.Fori(0, HT // 4) as i:
                for j in range(4):
                    load_slot(L2 + 4 * i + j, j, (w_glu, SW, i * 4 * P + j * P))
            with sp.Fori(0, KT // 4) as i:
                for j in range(4):
                    load_slot(GLU + 4 * i + j, j, (w_pa, SW, i * 4 * P + j * P), (w_ps, SW, i * 4 * P + j * P))
            with sp.Fori(0, KT // 4) as i:
                for j in range(4):
                    load_slot(PROJ + 4 * i + j, j, (w_out, D, i * 4 * P + j * P))

            def load_up(n, pairs):
                for q in range(pairs):
                    load_slot(OUT + 4 * n + 2 * q, 2 * q, (w_up, D, n * 2 * P + q * P))
                    load_slot(OUT + 4 * n + 2 * q + 1, 2 * q + 1, (w_up, D, FF + n * 2 * P + q * P))

            def store_up(n, pairs):
                sp.wait_ge(upt_read, n + 1)
                for v in range(2):
                    rows = up_rows.rearrange("r (q v m) -> r v q m", q=2, v=2)[:, v, 0:pairs, :]
                    cols = bass.ds(v * FF + n * 2 * P, pairs * P)
                    sp.dma_start(out["conv_prompt"][:, cols].rearrange("r (q m) -> r q m", m=P),
                                 rows[0:2]).then_inc(upr_stored, 16)
                    sp.dma_start(out["conv_sample"][0, :, 1, cols].rearrange("r (q m) -> r q m", m=P),
                                 rows[2:10]).then_inc(upr_stored, 16)

            load_up(0, 2)
            with sp.Fori(1, FT // 2) as n:
                load_up(n, 2)
                store_up(n - 1, 2)
            load_up(FT // 2, 1)
            store_up(FT // 2 - 1, 2)

            def load_down(n):
                for m in range(2):
                    for h, (k0, k1) in enumerate(((0, DOWN_A), (DOWN_A, FT))):
                        j = 2 * m + h
                        wait(sp, down_used, 4 * n + j - 3)
                        dst = gd[:, j * DOWN_A * P:(j * DOWN_A + k1 - k0) * P].rearrange("p (k m) -> p k m", m=P)
                        src = w_down[k0 * P:k1 * P, bass.ds(n * 2 * P + m * P, P)].rearrange("(k p) m -> p k m", p=P)
                        sp.dma_start(dst, src).then_inc(down_in[j], 16)

            load_down(0)
            store_up(FT // 2, 1)
            with sp.Fori(1, KT // 2) as n:
                load_down(n)
            for c in range(3):
                sp.wait_ge(yt_read, 4 * c + 4)
                rows = big[:, c * D:(c + 1) * D]
                if c < 2:
                    sp.dma_start(out["y_prompt"][c * P:(c + 1) * P, :], rows).then_inc(y_stored, 16)
                else:
                    sp.dma_start(out["y_sample"], rows[0:B]).then_inc(y_stored, 16)
            sp.wait_ge(y_stored, 3 * 16)
            sp.wait_ge(kv_stored, 2 * H * 16)
            sp.wait_ge(out_stored, 9 * 16)
            sp.wait_ge(upr_stored, 4 * (FT // 2 + 1) * 16)

        @block.gpsimd
        def _(pool):
            ch = Chain(pool, pool_c)
            pool.memset(x_rows[:, 2, :], 0.0).then_inc(x_zero, 1)
            ch.did(pool.memset(ident[:, :], 0.0))
            ch.wait()
            pool.affine_select(out=ident[:, :], in_=ident[:, :], compare_op=ALU.not_equal, fill=1.0, base=0,
                               pattern=[[-1, P]], channel_multiplier=1).then_inc(const_ready, 1)
            pool.memset(small[0:NB + 1, 32:32 + H], MASK).then_inc(rel_ready, 1)
            for tensor, value in ((ones[:, :], 1.0), (mean_w[:, :], 1.0 / D), (v_mean_w[:, :], 1.0 / P),
                                  (small[:, 4:5], PI / 2), (small[:, 5:6], EPS), (small[:, 6:7], 4 * EPS)):
                pool.memset(tensor, value).then_inc(const_ready, 1)
            ch.did(pool.iota(multiples_i[:, 0:16], pattern=[[1, 16]], base=1, channel_multiplier=0))
            ch.did(pool.iota(multiples_i[:, 16:32], pattern=[[16, 16]], base=0, channel_multiplier=0))
            ch.wait()
            pool.tensor_copy(small[:, 320:352], multiples_i[:, 0:32]).then_inc(mult_ready, 1)
            pool.memset(kv_new[:, :], 0.0).then_inc(bpad_zero, 1)
            pool.wait_ge(tr, 24)
            pool.memset(MT[:, :, 256:512], 0.0).then_inc(mt_zero, 1)
            pool.wait_ge(s5_tr, 10)
            pool.memset(kv_new[:, :], 0.0).then_inc(kv_zero, 1)
            pool.wait_ge(s5_dve, 7)
            pool.wait_ge(s5_act, 6)
            pool.wait_ge(s5_used, 10)

            ang4 = ang.rearrange("p (r q e) -> p r q e", r=2, q=PAIRS)

            def rotation(t, p):
                n = 4 * t + p

                def fine(r):
                    return ang4[:, r, bass.ds(n, 1), 0:16].to_broadcast([P, 16, 16])

                def coarse(r):
                    return ang4[:, r, bass.ds(n, 1), 16:32].rearrange("p o e -> p e o").to_broadcast([P, 16, 16])

                cos, sin = (tab[p % 2][:, r * 256:(r + 1) * 256].rearrange("p (a b) -> p a b", a=16) for r in range(2))
                t1, t2, t3, t4 = (ptmp[:, k * 256:(k + 1) * 256].rearrange("p (a b) -> p a b", a=16) for k in range(4))
                wait(pool, tab_ready, n)
                ch.did(pool.tensor_tensor(t1, coarse(0), fine(0), ALU.mult))
                ch.did(pool.tensor_tensor(t2, coarse(1), fine(1), ALU.mult))
                ch.did(pool.tensor_tensor(t3, coarse(1), fine(0), ALU.mult))
                ch.did(pool.tensor_tensor(t4, coarse(0), fine(1), ALU.mult))
                wait(pool, xs_ready, n - 1)
                ch.wait()
                ch.did(pool.tensor_tensor(cos, t1, t2, ALU.subtract))
                pool.tensor_tensor(sin, t3, t4, ALU.add).then_inc(tab_ready, 1)

            def s5_tile(t):
                wait(pool, c_done, 4 * t)
                pool.tensor_copy(mst, MT[:, bass.ds(t, 1), :].rearrange("p o c -> p (o c)")).then_inc(mst_ready, 1)
                for p in range(4):
                    rotation(t, p)

            s5_tile(0)
            with pool.Fori(1, HT) as t:
                ch.enter(t, 1, 20)
                s5_tile(t)
            ch.leave(HT - 1)

            pool.wait_ge(c_done, 4 * HT)
            pool.wait_ge(xf_read, 4 * HT)

            def score_products(b):
                for p in range(PAGES + 1):
                    if p < PAGES:
                        pool.wait_ge(k_in[p % 4], 16 * (4 * b + p // 4 + 1))
                    if p == 0:
                        pool.wait_ge(qb_ready, b + 1)
                    wait(pool, kq_read, 17 * b + (p - 1 if p else 0))
                    keys = k_ring[p % 4] if p < PAGES else k_new
                    pool.tensor_tensor(kq[p % 2], keys, q_all, ALU.mult).then_inc(kq_ready, 1)
                pool.wait_ge(smax_ready, b + 1)
                pool.partition_all_reduce(small[:, 528:544], small[:, 512:528], P,
                                          bass.bass_isa.ReduceOp.max).then_inc(gmax_ready, 1)

            for b in range(B):
                score_products(b)

        @block.tensor
        def _(pe):
            def transpose(dst, src):
                k = src.shape[0]
                return pe.transpose(dst, src, ident[0:k, 0:k])

            pe.wait_ge(const_ready, 7)
            pe.wait_ge(xs_in, 32)
            for k in range(KT):
                wait(pe, tr_used, k - 3)
                for c in range(3):
                    last = transpose(bank[k % 4][:, c * P:(c + 1) * P], x_rows[:, c, k * P:(k + 1) * P])
                last.then_inc(tr, 1)
            pe.wait_ge(par_in, 12 * 16)
            pe.wait_ge(tr_used, 13)
            for w in range(4):
                last = transpose(bank[0][:, w * 2 * FT:(w + 1) * 2 * FT], par_rows[0:2 * FT, w * P:(w + 1) * P])
            last.then_inc(tr, 1)
            pe.wait_ge(tr_used, 14)
            for w in range(4):
                last = transpose(bank[1][:, w * KT:(w + 1) * KT], ln_rows[0:KT, w * P:(w + 1) * P])
            last.then_inc(tr, 1)
            pe.wait_ge(st_in, 16)
            for g in range(3):
                pe.wait_ge(tr_used, 15 + g)
                for f in range(32 * g, min(32 * g + 32, 2 * FT)):
                    last = transpose(bank[(18 + g) % 4][:, (f % 32) * 16:(f % 32) * 16 + 16],
                                     st_rows[:, f * P:(f + 1) * P])
                last.then_inc(tr, 1)
            pe.wait_ge(tab_in, 32)
            rel = small[0:NB + 1, 32:32 + H]
            pe.wait_ge(tr_used, 18)
            pe.matmul(bank[1][0:H, 0:384], rel, mm[0:NB + 1, OH_TOEP:OH_TOEP + 384], start=True, stop=True).then_inc(tr, 1)
            pe.wait_ge(tr_used, 19)
            for p in range(PAGES):
                last = pe.matmul(bank[2][:, p * H:(p + 1) * H], mm[0:NB + 1, OH_PAGE + p * P:OH_PAGE + (p + 1) * P],
                                 rel, start=True, stop=True)
            last.then_inc(tr, 1)
            pe.wait_ge(tr_used, 20)
            for b in range(B):
                last = pe.matmul(bank[3][:, b * H:(b + 1) * H], mm[0:NB + 1, OH_NEW + b * P:OH_NEW + (b + 1) * P],
                                 rel, start=True, stop=True)
            last.then_inc(tr, 1)
            pe.wait_ge(x0_in, 64)
            for k in range(4):
                last = transpose(bank[4][:, k * P:(k + 1) * P], x0_rows[:, k * P:(k + 1) * P])
            last.then_inc(s5_tr, 1)
            pe.wait_ge(c_in, 64)
            for k in range(4):
                wait(pe, s5_used, k - 2)
                for t in range(2):
                    for r in range(2):
                        at = r * 1024 + (2 * k + t) * P
                        last = transpose(bank[4 + (1 + k) % 4][:, (2 * t + r) * P:(2 * t + r + 1) * P],
                                         c_rows[:, at:at + P])
                last.then_inc(s5_tr, 1)
            pe.wait_ge(s5_dve, 3)
            pe.wait_ge(s5_used, 2)
            for k in range(7):
                last = transpose(bank[5][:, k * PAIRS:(k + 1) * PAIRS], yg[0:PAIRS, (9 + k) * P:(10 + k) * P])
            last.then_inc(s5_tr, 1)
            pe.wait_ge(s5_dve, 4)
            for k in range(4):
                pe.wait_ge(s5_used, 3 + k)
                for t in range(2):
                    for r in range(2):
                        at = r * 1024 + (2 * k + t) * P
                        last = transpose(bank[4 + (6 + k) % 4][:, (2 * t + r) * P:(2 * t + r + 1) * P],
                                         kv_new[:, at:at + P])
                last.then_inc(s5_tr, 1)

            def m_tile(j, dst, arrived, rhs):
                pe.wait_ge(ring_in[j], arrived)
                k_tiles = len(rhs)
                for k in range(k_tiles):
                    last = pe.matmul(dst[:, 0:N], slot(j, k), rhs[k], start=(k == 0), stop=(k == k_tiles - 1))
                last.then_inc(slot_done, 1)

            x_tiles = [xtile(k) for k in range(KT)]
            pe.wait_ge(tr_used, 24)
            pe.wait_ge(s5_used, 10)

            def z_tile(i, j):
                wait(pe, z_read, 4 * i + j - 1)
                m_tile(j, bank[j % 2], 16 * (i + 1), x_tiles)

            def bu(t, p):
                pe.wait_ge(mst_ready, t + 1)
                pe.wait_ge(z_read, 4 * t + 4)
                wait(pe, b_read, 4 * t + p)
                rows = slice(32 * p, 32 * p + 32)
                pe.matmul(bank[6][:, 0:N], mst[rows, 0:P], u_t[rows, :], start=True, stop=True)
                pe.matmul(bank[7][:, 0:N], mst[rows, P:2 * P], u_t[rows, :], start=True, stop=True).then_inc(b_done, 1)

            def cx(t, p):
                pe.wait_ge(xs_ready, 4 * t + p + 1)
                if p == 0:
                    wait(pe, y_ready, t)
                for r in range(2):
                    last = pe.matmul(bank[3][32 * p:32 * p + 32, 0:N], mst[:, (2 + r) * P + 32 * p:(2 + r) * P + 32 * p + 32],
                                     x_st[p % 2][:, r * N:(r + 1) * N], start=(r == 0), stop=(r == 1))
                last.then_inc(c_done, 1)

            def scores(i):
                pe.wait_ge(z_read, 4 * i + 2)
                wait(pe, pv_read, i)
                wait(pe, max_ready, i)
                for j in range(2):
                    rows = slice(64 * j, 64 * j + 64)
                    pe.matmul(bank[4 + j][:, 0:256], q_t[rows, P:2 * P], k_t[rows, 0:T], start=True, stop=True)
                    last = pe.matmul(bank[4 + j][:, 256:384], q_t[rows, 0:P], k_t[rows, 0:P], start=True, stop=True)
                last.then_inc(sc_done, 1)

            def to_rows(src, done, free, count):
                wait(pe, free, count)
                transpose(bank[2][:, 0:P], src[:, 0:P])
                transpose(bank[2][:, P:2 * P], src[:, P:2 * P])
                transpose(bank[2][0:B, 2 * P:3 * P], src[:, T:N]).then_inc(done, 1)

            def prompt_pv(i):
                pe.wait_ge(pd_ready, i + 1)
                pe.wait_ge(vt_read, i + 1)
                for k, at in enumerate((256, 0, P)):
                    last = transpose(bank[2][:, k * P:(k + 1) * P], p_diff[:, at:at + P])
                last.then_inc(pdt_done, 1)
                pe.wait_ge(pdt_read, i + 1)
                pe.matmul(bank[4][:, 0:T], v_rows[:, 0:P], p_diff_t[:, 0:T], start=True, stop=False)
                pe.matmul(bank[4][:, P:T], v_rows[:, P:2 * P], p_diff_t[:, T:T + P], start=False, stop=True).then_inc(pv_done, 1)

            def head(i, s5):
                t = i - 1
                z_tile(i, 0)
                if s5:
                    bu(t, 0)
                z_tile(i, 1)
                if s5:
                    cx(t, 0)
                    bu(t, 1)
                z_tile(i, 2)
                scores(i)
                if s5:
                    cx(t, 1)
                    bu(t, 2)
                z_tile(i, 3)
                to_rows(k_t, kt_done, pdt_read, i)
                pe.wait_ge(z_read, 4 * i + 3)
                to_rows(v_t, vt_done, kt_read, i + 1)
                if s5:
                    cx(t, 2)
                    bu(t, 3)
                prompt_pv(i)
                if s5:
                    cx(t, 3)

            head(0, False)
            head(1, True)
            with pe.Fori(2, H) as i:
                head(i, True)
            for p in range(4):
                bu(HT - 1, p)
                cx(HT - 1, p)
            pe.wait_ge(xf_read, 4 * HT)
            pe.wait_ge(pdt_read, H)
            xf4 = xf[:, :].rearrange("p (r c q) -> p r c q", r=2, c=9)
            for r in range(2):
                last = transpose(bank[2][0:PAIRS, r * P:(r + 1) * P], xf4[:, r, 0, :])
            last.then_inc(xft, 1)
            pe.wait_ge(max_ready, H)
            for r in range(2):
                for h in range(2):
                    at = r * 9 * PAIRS + (1 + 4 * h) * PAIRS
                    last = transpose(bank[5][:, (2 * r + h) * P:(2 * r + h + 1) * P], xf[:, at:at + P])
            last.then_inc(xft, 1)
            pe.wait_ge(xft_read, 2)
            pe.wait_ge(y_ready, HT)
            pe.wait_ge(pv_read, H)

            def broadcast_q(b):
                pe.wait_ge(dq_ready, b + 1)
                wait(pe, qb_ready, b)
                pe.matmul(bank[2][:, :], ones[:, :], diag_q[:, 0:512], start=True, stop=True)
                pe.matmul(bank[3][:, :], ones[:, :], diag_q[:, 512:1024], start=True, stop=True).then_inc(qb_done, 1)

            def gate_tile(b, r):
                pe.wait_ge(z_read, L1 + 4 * b + r - 1)
                m_tile(r, bank[r % 2], 16 * (H + b + 1), x_tiles)

            def denominators(b):
                pe.wait_ge(lsum_ready, b + 1)
                wait(pe, o_read, b)
                pe.matmul(bank[5][:, 0:16], ones[:, :], small[:, 544:560], start=True, stop=True).then_inc(lsum_done, 1)

            def page_pv(b, p):
                if p < PAGES:
                    pe.wait_ge(v_in[p % 4], 16 * (4 * b + p // 4 + 1))
                values = v_ring[p % 4] if p < PAGES else v_new
                for h in range(H):
                    last = pe.matmul(bank[4][:, 2 * h:2 * h + 2], values[:, h * P:(h + 1) * P],
                                     prob[:, p * 16 + 2 * h:p * 16 + 2 * h + 2], start=(p == 0 and h == 0),
                                     stop=(p == PAGES and h == H - 1), skip_group_check=True)
                last.then_inc(v_used if p < PAGES else spv_done, 1)

            def decode(b, scored, summed):
                if scored:
                    broadcast_q(b)
                if summed:
                    denominators(b - 1)
                for r in range(4):
                    if scored:
                        gate_tile(b, r)
                    if summed:
                        for p in range(4 * r, 4 * r + 4):
                            page_pv(b - 1, p)
                if summed:
                    page_pv(b - 1, PAGES)

            decode(0, True, False)
            decode(1, True, True)
            with pe.Fori(2, B) as b:
                decode(b, True, True)
            decode(B, False, True)

            sq = big[:, 2 * KW + 64:2 * KW + 64 + H * N]
            pe.wait_ge(sq_ready, 1)
            pe.wait_ge(o_read, B)
            for h in range(H):
                wait(pe, root_ready, h - 3)
                pe.matmul(bank[4 + h % 4][:, 0:N], v_mean_w[:, :], sq[:, h * N:(h + 1) * N],
                          start=True, stop=True).then_inc(ms_done, 1)

            y_tiles = [yg[:, k * N:(k + 1) * N] for k in range(HT)]
            pe.wait_ge(gelu_dve, 2)
            with pe.Fori(0, 2) as i:
                for j in range(4):
                    pe.wait_ge(z_read, L2 + 4 * i + j - 1)
                    m_tile(j, bank[j % 2], 16 * (2 * H + i + 1), y_tiles)

            branch_tiles = ([att[:, k * N:(k + 1) * N] for k in range(HT)], [big[:, k * N:(k + 1) * N] for k in range(HT)])
            pe.wait_ge(z_read, GLU)
            pe.wait_ge(att_ready, 1)
            pe.wait_ge(ssm_ready, HT)

            def proj(i):
                for j in range(4):
                    wait(pe, zv_read, 4 * i + j - 1)
                    pe.wait_ge(ring_in[j], 16 * (2 * H + 2) + 32 * (i + 1))
                    for s in range(2):
                        for k in range(HT):
                            last = pe.matmul(bank[2 * s + j % 2][:, 0:N], slot(j, s * HT + k), branch_tiles[s][k],
                                             start=(k == 0), stop=(k == HT - 1))
                    last.then_inc(slot_done, 1)

            proj(0)
            with pe.Fori(1, 4) as i:
                proj(i)

            def mean_tile(n):
                return pe.matmul(bank[6][:, 0:N], mean_w[:, :], xtile(n), start=(n == 0), stop=(n == KT - 1))

            out_base = 16 * (2 * H + 2) + 32 * 4
            for n in range(KT):
                j = n % 4
                pe.wait_ge(zv_read, KT + n - 1)
                pe.wait_ge(ring_in[j], out_base + 16 * (n // 4 + 1))
                for k in range(KT):
                    if n == 0:
                        pe.wait_ge(merged_ready, k + 1)
                    last = pe.matmul(bank[n % 2][:, 0:N], slot(j, k), merged[:, k * N:(k + 1) * N],
                                     start=(k == 0), stop=(k == KT - 1))
                last.then_inc(slot_done, 1)
                if n:
                    pe.wait_ge(zv_read, KT + n)
                    mean_tile(n - 1)
            pe.wait_ge(zv_read, 2 * KT)
            mean_tile(KT - 1).then_inc(mean_done, 1)

            def variance(ln):
                for n in range(KT):
                    if n % 4 == 0:
                        pe.wait_ge(csq_ready, 4 * ln + n // 4 + 1)
                    last = pe.matmul(bank[7][:, 0:N], mean_w[:, :], big[:, n * N:(n + 1) * N], start=(n == 0),
                                     stop=(n == KT - 1))
                last.then_inc(var_done, 1)

            variance(0)
            up_base = out_base + 16 * 4

            def up_rows_out(n, pairs):
                pe.wait_ge(tap0, 4 * n + 2 * pairs)
                wait(pe, upt_read, n)
                for t in range(2 * pairs):
                    last = transpose(bank[4][0:10, t * P:(t + 1) * P], up10[:, t * 10:(t + 1) * 10])
                last.then_inc(upt_done, 1)

            def up(n, pairs, first=False):
                for t in range(2 * pairs):
                    pe.wait_ge(zv_read, 2 * KT + (0 if first else 4 * (n - 1) + t + 1))
                    pe.wait_ge(ring_in[t], up_base + 16 * (n + 1))
                    for k in range(KT):
                        if first and t == 0:
                            pe.wait_ge(h_ready, k + 1)
                        last = pe.matmul(bank[t][:, 0:N], slot(t, k), xtile(k), start=(k == 0), stop=(k == KT - 1))
                    last.then_inc(slot_done, 1)
                    if t == 0 and not first:
                        up_rows_out(n - 1, 2)

            up(0, 2, True)
            with pe.Fori(1, FT // 2) as n:
                up(n, 2)
            up(FT // 2, 1)

            down_base = 2 * KT + 2 * FT

            for n in range(KT):
                i, m = n // 2, n % 2
                pe.wait_ge(zv_read, down_base + max(0, n - 1))
                for h, (k0, k1) in enumerate(((0, DOWN_A), (DOWN_A, FT))):
                    pe.wait_ge(down_in[2 * m + h], 16 * (i + 1))
                    for k in range(k0, k1):
                        if n == 0:
                            pe.wait_ge(hid_ready, k + 1)
                        last = pe.matmul(bank[n % 2][:, 0:N], down_slot(2 * m + h, k - k0), hid[:, k * N:(k + 1) * N],
                                         start=(k == 0), stop=(k == FT - 1))
                    last.then_inc(down_used, 1)
                if n == 0:
                    up_rows_out(FT // 2, 1)
                if n:
                    pe.wait_ge(zv_read, down_base + n)
                    mean_tile(n - 1)
            pe.wait_ge(zv_read, down_base + KT)
            mean_tile(KT - 1).then_inc(mean_done, 1)
            variance(1)
            for c in range(3):
                for g in range(4):
                    n = 4 * c + g
                    wait(pe, yt_read, n - 3)
                    for k in range(4):
                        if c == 0:
                            pe.wait_ge(h_ready, KT + 4 * g + k + 1)
                        tile = xtile(4 * g + k)[:, c * P:min(N, (c + 1) * P)]
                        last = transpose(bank[n % 4][0:tile.shape[1], k * P:(k + 1) * P], tile)
                    last.then_inc(yt_done, 1)

        @block.scalar
        def _(act):
            def copy(dst, src, scale=1.0):
                return act.activation(dst, src, ACT.Copy, scale=scale)

            def row(k):
                return yg[0:PAIRS, k * P:(k + 1) * P]

            act.wait_ge(rows_in, 48)
            act.wait_ge(const_ready, 7)
            act.activation(small[0:PAIRS, 2:4], small[0:PAIRS, 0:2], ACT.Exp).then_inc(s5_act, 1)
            act.wait_ge(s5_dve, 1)
            act.activation(row(9), row(2), ACT.Exp).then_inc(s5_act, 1)
            act.wait_ge(s5_dve, 2)
            act.activation(row(6), row(10), ACT.Sin, scale=TWO_PI_DOWN).then_inc(s5_act, 1)
            act.activation(row(7), row(5), ACT.Sin, scale=-TWO_PI_DOWN, bias=small[0:PAIRS, 4:5]).then_inc(s5_act, 1)
            for k in range(KT):
                act.wait_ge(tr, k + 1)
                copy(xtile(k), bank[k % 4][:, 0:N]).then_inc(tr_used, 1)
            for n, (dst, rows, cols) in enumerate((
                    (conv_par[:, :], P, 8 * FT), (ln_par[:, :], P, 4 * KT), (conv_state[:, 0:512], P, 512),
                    (conv_state[:, 512:1024], P, 512), (conv_state[:, 1024:2 * FT * 16], P, 2 * FT * 16 - 1024),
                    (toep_rows[0:H, :], H, 384), (bias_pg[:, :], P, PAGES * H), (bias_nw[:, :], P, B * H))):
                act.wait_ge(tr, KT + n + 1)
                copy(dst, bank[n % 4][0:rows, 0:cols]).then_inc(tr_used, 1)
            act.wait_ge(par_in, 12 * 16)
            act.wait_ge(s5_dve, 6)
            act.activation(small[:, 28:30], small[:, 26:28], ACT.Exp).then_inc(lam_exp, 1)
            act.wait_ge(s5_dve, 7)
            for r, src in enumerate((att[:, 1024:2048], att[:, 0:1024])):
                if r == 0:
                    act.activation(ang[:, 0:1024], src, ACT.Sin, scale=-TWO_PI_DOWN, bias=small[:, 4:5]).then_inc(s5_act, 1)
                else:
                    act.activation(ang[:, 1024:2048], src, ACT.Sin, scale=TWO_PI_DOWN).then_inc(s5_act, 1)
            act.wait_ge(kv_zero, 1)

            xf4 = xf[:, :].rearrange("p (r c q) -> p r c q", r=2, c=9)
            q_s3 = q_s[:, :].rearrange("p (h b) -> p h b", h=H)

            def final_states(t, p):
                act.wait_ge(xs_ready, 4 * t + p + 1)
                copy(xf4[:, :, :, bass.ds(4 * t + p, 1)].rearrange("p r c o -> p r (c o)"),
                     x_st[p % 2].rearrange("p (r n) -> p r n", r=2)[:, :, T - 1:N]).then_inc(xf_read, 1)

            def exps(i):
                act.wait_ge(max_ready, i + 1)
                wait(act, pd_ready, i)
                for blk, cols in enumerate((slice(0, 256), slice(256, 384))):
                    for j in range(2):
                        k = 2 * blk + j
                        src = s_sb[:, 384 * j + cols.start:384 * j + cols.stop]
                        dst = p_sb[:, 384 * j + cols.start:384 * j + cols.stop]
                        last = act.activation(dst, src, ACT.Exp, bias=small[:, 420 + k:421 + k],
                                              accum_out=small[:, 424 + k:425 + k])
                last.then_inc(exp_done, 1)

            def head(i, s5):
                t = i - 1
                act.wait_ge(slot_done, 4 * i + 1)
                wait(act, sc_done, i)
                copy(q_t, bank[0][:, 0:N])
                copy(q_s3[:, bass.ds(i, 1), :].rearrange("p o b -> p (o b)"), bank[0][:, T:N]).then_inc(z_read, 1)
                act.wait_ge(slot_done, 4 * i + 2)
                wait(act, kt_done, i)
                copy(k_t, bank[1][:, 0:N]).then_inc(z_read, 1)
                if s5:
                    final_states(t, 0)
                act.wait_ge(slot_done, 4 * i + 3)
                wait(act, vt_done, i)
                copy(v_t, bank[0][:, 0:N]).then_inc(z_read, 1)
                if s5:
                    final_states(t, 1)
                act.wait_ge(kt_done, i + 1)
                wait(act, kv_stored, 32 * i)
                copy(k_rows, bank[2][:, 0:256])
                copy(k_new[0:B, bass.ds(i * P, P)], bank[2][0:B, 256:384]).then_inc(kt_read, 1)
                act.wait_ge(vt_done, i + 1)
                wait(act, pv_done, i)
                copy(v_rows, bank[2][:, 0:256])
                copy(v_new[0:B, bass.ds(i * P, P)], bank[2][0:B, 256:384]).then_inc(vt_read, 1)
                exps(i)
                if s5:
                    final_states(t, 2)
                act.wait_ge(slot_done, 4 * i + 4)
                wait(act, b_done, 4 * i)
                copy(u_t, bank[1][:, 0:N])
                copy(u_all[:, bass.ds(i * N, N)], bank[1][:, 0:N]).then_inc(z_read, 1)
                act.wait_ge(pdt_done, i + 1)
                copy(p_diff_t, bank[2][:, 0:384]).then_inc(pdt_read, 1)
                act.wait_ge(pv_done, i + 1)
                copy(att[:, bass.ds(i * N, T)], bank[4][:, 0:T]).then_inc(pv_read, 1)
                if s5:
                    final_states(t, 3)

            head(0, False)
            with act.Fori(1, H) as i:
                head(i, True)
            for p in range(4):
                final_states(HT - 1, p)
            act.wait_ge(xft, 1)
            copy(par_rows[0:PAIRS, 0:2 * P], bank[2][0:PAIRS, 0:2 * P]).then_inc(xft_read, 1)
            act.wait_ge(xft, 2)
            copy(x0_rows[:, :], bank[5][:, :]).then_inc(xft_read, 1)
            gelu_t = mm[:, H * N:2 * H * N]
            act.wait_ge(y_ready, HT)
            act.wait_ge(mst_ready, HT)
            act.activation(gelu_t, yg[:, :], ACT.Square).then_inc(gelu_act, 1)
            act.wait_ge(gelu_dve, 1)
            act.activation(gelu_t, gelu_t, ACT.Tanh, scale=0.7978845608028654).then_inc(gelu_act, 1)

            def decode(b, first=False):
                act.wait_ge(qb_done, b + 1)
                wait(act, kq_ready, 17 * b)
                copy(q_all[:, 0:512], bank[2][:, :], HD ** -0.5)
                copy(q_all[:, 512:1024], bank[3][:, :], HD ** -0.5).then_inc(qb_ready, 1)
                if first:
                    act.wait_ge(kv_stored, 32 * H)
                for r in range(4):
                    act.wait_ge(slot_done, L1 + 4 * b + r + 1)
                    act.activation(gate[:, bass.ds((4 * b + r) * N, N)], bank[r % 2][:, 0:N], ACT.Tanh,
                                   scale=0.5).then_inc(z_read, 1)
                act.wait_ge(ssub_ready, b + 1)
                wait(act, spv_done, b)
                act.activation(prob, score, ACT.Exp).then_inc(sexp_ready, 1)

            decode(0, True)
            with act.Fori(1, B) as b:
                decode(b)

            sq = big[:, 2 * KW + 64:2 * KW + 64 + H * N]
            act.wait_ge(o_read, B)
            act.activation(sq, att[:, :], ACT.Square).then_inc(sq_ready, 1)
            for h in range(H):
                act.wait_ge(ms_done, h + 1)
                act.activation(sq[:, h * N:(h + 1) * N], bank[4 + h % 4][:, 0:N], ACT.Sqrt,
                               bias=small[:, 5:6]).then_inc(root_ready, 1)
            for j in range(HT):
                act.wait_ge(slot_done, L2 + j + 1)
                wait(act, ssm_ready, j - 1)
                act.activation(big[:, 4352 + (j % 2) * N:4352 + (j % 2 + 1) * N], bank[j % 2][:, 0:N], ACT.Tanh,
                               scale=0.25).then_inc(z_read, 1)

            def norm(ln):
                for g in range(4):
                    act.wait_ge(cent_ready, 4 * ln + g + 1)
                    act.activation(big[:, 4 * g * N:4 * (g + 1) * N], xt[:, 4 * g * N:4 * (g + 1) * N],
                                   ACT.Square).then_inc(csq_ready, 1)
                act.wait_ge(var_done, ln + 1)
                act.activation(std_sb, bank[7][:, 0:N], ACT.Sqrt, bias=small[:, 6:7]).then_inc(std_ready, 1)
                for k in range(KT):
                    act.wait_ge(norm_ready, 4 * ln + k // 4 + 1)
                    act.activation(xtile(k), xtile(k), ACT.Identity, scale=ln_par[:, 32 * ln + k:32 * ln + k + 1],
                                   bias=ln_par[:, 32 * ln + 16 + k:32 * ln + 17 + k]).then_inc(h_ready, 1)

            norm(0)

            def par(w, tile):
                return conv_par[:, bass.ds(w * 2 * FT + tile, 1)]

            def up_rows_copy(n, pairs):
                act.wait_ge(upt_done, n + 1)
                wait(act, upr_stored, 64 * n)
                copy(up_rows[:, 0:2 * pairs * P], bank[4][0:10, 0:2 * pairs * P]).then_inc(upt_read, 1)

            def up(n, pairs, first=False):
                for q in range(pairs):
                    wait(act, hid_ready, 2 * (n - 1) + q + 1)
                    for v in range(2):
                        t = 2 * q + v
                        tile = 2 * n + q + v * FT
                        act.wait_ge(slot_done, OUT + 4 * n + t + 1)
                        act.activation(acc[t], bank[t][:, 0:N], ACT.Identity, scale=par(2, tile), bias=par(3, tile))
                        if t == 0:
                            wait(act, upt_done, n)
                        copy(up10[:, t * 10:(t + 1) * 10], bank[t][:, T - 2:N]).then_inc(tap0, 1)
                    if q == 0 and not first:
                        up_rows_copy(n - 1, 2)
                    act.wait_ge(tap_done, 4 * n + 2 * q + 1)
                    act.activation(th[q], acc[2 * q], ACT.Tanh, scale=0.5).then_inc(th_ready, 1)

            up(0, 2, True)
            with act.Fori(1, FT // 2) as n:
                up(n, 2)
            up(FT // 2, 1)
            up_rows_copy(FT // 2, 1)
            norm(1)

        @block.vector
        def _(dve):
            ch = Chain(dve, dve_c)

            def row(k):
                return yg[0:PAIRS, k * P:(k + 1) * P]

            def link(ins):
                ch.did(ins)
                ch.wait()

            a_re, a_im, t_re, t_im = row(0), row(1), row(2), row(3)
            turns, turns_abs, sin, cos = row(10), row(5), row(6), row(7)
            tmp, inv = row(8), row(4)
            mag, ab_re, ab_im, f_re, f_im, neg_im = row(9), row(11), row(12), row(13), row(14), row(15)
            dve.wait_ge(rows_in, 48)
            dve.wait_ge(s5_act, 1)
            dt = small[0:PAIRS, 2:4].unsqueeze(2).to_broadcast([PAIRS, 2, S])

            def g2(x):
                return x.rearrange("q (g s) -> q g s", g=2)

            ch.did(dve.tensor_tensor(g2(t_im), g2(a_im), dt, ALU.mult))
            dve.tensor_tensor(g2(t_re), g2(a_re), dt, ALU.mult).then_inc(s5_dve, 1)
            ch.wait()
            link(dve.tensor_scalar(t_im, t_im, 1.0 / (2 * PI), None, ALU.mult))
            whole = mm[0:PAIRS, KT * N - P:KT * N].bitcast(I32)
            link(dve.tensor_copy(whole, t_im))
            link(dve.tensor_copy(tmp, whole))
            link(dve.tensor_tensor(turns, t_im, tmp, ALU.subtract))
            dve.scalar_tensor_tensor(turns_abs, turns, -1.0, turns, ALU.mult, ALU.max).then_inc(s5_dve, 1)
            ch.did(dve.tensor_tensor(inv, a_re, a_re, ALU.mult))
            link(dve.tensor_tensor(tmp, a_im, a_im, ALU.mult))
            link(dve.tensor_tensor(inv, inv, tmp, ALU.add))
            link(dve.reciprocal(inv, inv))
            dve.wait_ge(s5_act, 4)
            ch.did(dve.tensor_tensor(ab_re, mag, cos, ALU.mult))
            link(dve.tensor_tensor(ab_im, mag, sin, ALU.mult))
            link(dve.tensor_scalar(t_re, ab_re, -1.0, None, ALU.add))
            ch.did(dve.tensor_tensor(f_re, t_re, a_re, ALU.mult))
            ch.did(dve.tensor_tensor(tmp, ab_im, a_im, ALU.mult))
            ch.did(dve.tensor_tensor(f_im, ab_im, a_re, ALU.mult))
            link(dve.tensor_tensor(t_im, t_re, a_im, ALU.mult))
            ch.did(dve.tensor_tensor(f_re, f_re, tmp, ALU.add))
            link(dve.tensor_tensor(f_im, f_im, t_im, ALU.subtract))
            ch.did(dve.tensor_scalar(neg_im, ab_im, -1.0, None, ALU.mult))
            ch.did(dve.tensor_tensor(f_re, f_re, inv, ALU.mult))
            link(dve.tensor_tensor(f_im, f_im, inv, ALU.mult))
            dve.tensor_copy(small[0:PAIRS, 7:8], small[0:PAIRS, 4:5]).then_inc(s5_dve, 1)

            dve.wait_ge(s5_tr, 1)
            dve.tensor_copy(x0[:, :], bank[4][:, :]).then_inc(s5_used, 1)
            dve.wait_ge(mt_zero, 1)
            for k in range(4):
                dve.wait_ge(s5_tr, 2 + k)
                src = bank[4 + (1 + k) % 4][:, :].rearrange("p (t r q g c) -> p t r q g c", t=2, r=2, q=4, g=2)
                dst = MT[:, 2 * k:2 * k + 2, 256:512].rearrange("p t (r q g c) -> p t r q g c", r=2, q=4, g=2)
                for t in range(2):
                    for g in range(2):
                        rows = slice(64 * g, 64 * g + 64)
                        for r in range(2):
                            last = dve.tensor_scalar(dst[rows, t, r, :, g, :], src[rows, t, r, :, g, :],
                                                     1.0 - 2.0 * r, None, ALU.mult)
                last.then_inc(s5_used, 1)
            dve.wait_ge(s5_tr, 6)
            dve.tensor_copy(scan_par[:, :], bank[5][:, 0:7 * PAIRS]).then_inc(s5_used, 1)
            dve.wait_ge(s5_used, 6)
            dve.wait_ge(b_in, 32)
            dve.wait_ge(bpad_zero, 1)
            b_re, b_im, w0, w1 = (att[:, k * 512:(k + 1) * 512].rearrange("p (q c) -> p q c", c=C) for k in range(4))
            fr, fi = (scan_par[:, k * PAIRS:(k + 1) * PAIRS].unsqueeze(2).to_broadcast([P, PAIRS, C]) for k in (4, 5))
            for r, ((x, y), op) in enumerate((((fr, fi), ALU.subtract), ((fi, fr), ALU.add))):
                ch.did(dve.tensor_tensor(w0, b_re, x, ALU.mult))
                link(dve.tensor_tensor(w1, b_im, y, ALU.mult))
                for g in range(2):
                    rows = slice(64 * g, 64 * g + 64)
                    dst = kv_new[rows, r * 1024:(r + 1) * 1024].rearrange("p (q c) -> p q c", c=2 * C)[:, :, g * C:(g + 1) * C]
                    last = dve.tensor_tensor(dst, w0[rows], w1[rows], op)
                    if r == 1 and g == 1:
                        last.then_inc(s5_dve, 1)
                    else:
                        ch.did(last)
                ch.wait()
            for k in range(4):
                dve.wait_ge(s5_tr, 7 + k)
                dve.tensor_copy(MT[:, 2 * k:2 * k + 2, 0:256],
                                bank[4 + (6 + k) % 4][:, :].rearrange("p (t c) -> p t c", t=2)).then_inc(s5_used, 1)
            dve.wait_ge(par_in, 12 * 16)
            lam = small[:, 64:64 + 4 * HD].rearrange("p (m k d) -> p m k d", m=2, k=2)
            prod = small[:, 352:480].rearrange("p (m d) -> p m d", m=2)
            link(dve.tensor_tensor(prod, lam[:, :, 0, :], lam[:, :, 1, :], ALU.mult))
            dve.tensor_reduce(small[:, 26:28], prod, AX.X, ALU.add).then_inc(s5_dve, 2)
            dve.wait_ge(lam_exp, 1)
            link(dve.tensor_tensor(small[:, 25:26], small[:, 29:30], small[:, 28:29], ALU.subtract))
            link(dve.tensor_scalar(small[:, 25:26], small[:, 25:26], -LAM_INIT, None, ALU.add))
            ch.did(dve.tensor_scalar(small[:, 30:31], small[:, 24:25], 1.0 - LAM_INIT, None, ALU.mult))
            dve.wait_ge(mult_ready, 1)
            dve.wait_ge(s5_dve, 6)
            v, f = att[:, 0:1024], att[:, 1024:2048]
            turn_q = scan_par[:, PAIRS:2 * PAIRS].unsqueeze(2).to_broadcast([P, PAIRS, 32])
            times = small[:, 320:352].unsqueeze(1).to_broadcast([P, PAIRS, 32])
            link(dve.tensor_tensor(v.rearrange("p (q e) -> p q e", e=32), turn_q, times, ALU.mult))
            link(dve.tensor_copy(c_rows[:, 0:1024].bitcast(I32), v))
            link(dve.tensor_copy(f, c_rows[:, 0:1024].bitcast(I32)))
            link(dve.tensor_tensor(v, v, f, ALU.subtract))
            dve.scalar_tensor_tensor(f, v, -1.0, v, ALU.mult, ALU.max).then_inc(s5_dve, 1)

            dve.wait_ge(toep_in, 32)
            bias3 = bias.rearrange("p (h x) -> p h x", h=H)
            x04 = x0[:, :].rearrange("p (r b q) -> p r b q", r=2, b=B)

            def states(t, p):
                n = 4 * t + p
                q = bass.ds(n, 1)

                def par(k):
                    return scan_par[:, bass.ds(k * PAIRS + n, 1)]

                def old(r):
                    return x04[:, r, :, q].rearrange("p b o -> p (b o)")

                cos, sin = tab[p % 2][:, 0:256], tab[p % 2][:, 256:512]
                re, im = bank[6], bank[7]
                x_re, x_im = x_st[p % 2][:, 0:N], x_st[p % 2][:, N:2 * N]
                s_re, s_im = small[:, 400:408], small[:, 408:416]
                dve.wait_ge(tab_ready, n + 1)
                dve.wait_ge(b_done, n + 1)
                wait(dve, xs_ready, n)
                ch.did(dve.tensor_tensor(rot[0], re[:, 0:T], cos, ALU.mult))
                n1 = ch.did(dve.tensor_tensor(rot[1], im[:, 0:T], sin, ALU.mult))
                ch.did(dve.tensor_tensor(rot[2], im[:, 0:T], cos, ALU.mult))
                n2 = ch.did(dve.tensor_tensor(rot[3], re[:, 0:T], sin, ALU.mult))
                ch.did(dve.scalar_tensor_tensor(s_re, old(0), par(2), re[:, T:N], ALU.mult, ALU.add))
                dve.scalar_tensor_tensor(s_im, old(1), par(2), im[:, T:N], ALU.mult, ALU.add).then_inc(b_read, 1)
                ch.wait(n1)
                n1 = ch.did(dve.tensor_tensor(z_re, rot[0], rot[1], ALU.add))
                ch.wait(n2)
                n2 = ch.did(dve.tensor_tensor(z_im, rot[2], rot[3], ALU.subtract))
                decay = par(0).to_broadcast([P, T])
                ch.wait(n1)
                n1 = ch.did(dve.tensor_tensor_scan(y_re, decay, z_re, 0.0, ALU.mult, ALU.add))
                ch.wait(n2)
                n2 = ch.did(dve.tensor_tensor_scan(y_im, decay, z_im, 0.0, ALU.mult, ALU.add))
                wait(dve, c_done, n - 1)
                wait(dve, xf_read, n - 1)
                dve.wait_ge(b_read, n + 1)
                ch.did(dve.scalar_tensor_tensor(x_re[:, T:N], old(1), par(6), s_re, ALU.mult, ALU.add))
                ch.did(dve.scalar_tensor_tensor(x_im[:, T:N], old(0), par(3), s_im, ALU.mult, ALU.add))
                ch.wait(n1)
                ch.did(dve.tensor_tensor(rot[0], y_re, cos, ALU.mult))
                ch.did(dve.tensor_tensor(rot[2], y_re, sin, ALU.mult))
                ch.wait(n2)
                n1 = ch.did(dve.tensor_tensor(rot[1], y_im, sin, ALU.mult))
                n2 = ch.did(dve.tensor_tensor(rot[3], y_im, cos, ALU.mult))
                ch.wait(n1)
                ch.did(dve.tensor_tensor(x_re[:, 0:T], rot[0], rot[1], ALU.subtract))
                ch.wait(n2)
                dve.tensor_tensor(x_im[:, 0:T], rot[2], rot[3], ALU.add).then_inc(xs_ready, 1)

            def maxima(i):
                dve.wait_ge(sc_done, i + 1)
                wait(dve, exp_done, i)
                for j in range(2):
                    n1 = ch.did(dve.scalar_tensor_tensor(
                        s_sb[:, 384 * j:384 * (j + 1)], bank[4 + j][:, 0:384], HD ** -0.5,
                        bias3[:, bass.ds(i, 1), :].rearrange("p o x -> p (o x)"), ALU.mult, ALU.add))
                ch.wait(n1)
                s3 = s_sb.rearrange("p (j x) -> p j x", j=2)
                ch.did(dve.tensor_reduce(small[:, 420:422], s3[:, :, 0:256], AX.X, ALU.max, negate=True))
                dve.tensor_reduce(small[:, 422:424], s3[:, :, 256:384], AX.X, ALU.max, negate=True).then_inc(max_ready, 1)

            def differences(i):
                dve.wait_ge(exp_done, i + 1)
                wait(dve, pdt_done, i)
                link(dve.reciprocal(small[:, 428:432], small[:, 424:428]))
                second = small[:, 428:432].rearrange("p (k j) -> p k j", j=2)[:, :, 1]
                n1 = ch.did(dve.tensor_scalar(second, second, small[:, 25:26], None, ALU.mult))
                ch.did(dve.tensor_scalar(p_diff[:, 0:256], p_sb[:, 0:256], small[:, 428:429], None, ALU.mult))
                n2 = ch.did(dve.tensor_scalar(p_diff[:, 256:384], p_sb[:, 256:384], small[:, 430:431], None, ALU.mult))
                ch.wait(n2)
                ch.did(dve.scalar_tensor_tensor(p_diff[:, 0:256], p_sb[:, 384:640], small[:, 429:430],
                                                p_diff[:, 0:256], ALU.mult, ALU.add))
                dve.scalar_tensor_tensor(p_diff[:, 256:384], p_sb[:, 640:768], small[:, 431:432],
                                         p_diff[:, 256:384], ALU.mult, ALU.add).then_inc(pd_ready, 1)

            def y_out(t):
                dve.wait_ge(c_done, 4 * t + 4)
                dve.scalar_tensor_tensor(yg[:, bass.ds(t * N, N)], u_all[:, bass.ds(t * N, N)],
                                         small[:, bass.ds(16 + t, 1)], bank[3][:, 0:N], ALU.mult, ALU.add
                                         ).then_inc(y_ready, 1)

            def head(i):
                states(i - 1, 0)
                states(i - 1, 1)
                maxima(i)
                states(i - 1, 2)
                differences(i)
                states(i - 1, 3)
                y_out(i - 1)

            maxima(0)
            differences(0)
            head(1)
            with dve.Fori(2, H) as i:
                ch.enter(i, 2, 4 * 16 + 3 + 5)
                head(i)
            ch.leave(H - 2)
            for p in range(4):
                states(HT - 1, p)
            y_out(HT - 1)

            gelu_t = mm[:, H * N:2 * H * N]
            dve.wait_ge(gelu_act, 1)
            link(dve.tensor_scalar(gelu_t, gelu_t, 0.044715, 1.0, ALU.mult, ALU.add))
            dve.tensor_tensor(gelu_t, gelu_t, yg[:, :], ALU.mult).then_inc(gelu_dve, 1)

            def diag(b):
                wait(dve, qb_done, b)
                query = q_s[:, :].rearrange("p (h b) -> p h b", h=H)[:, :, bass.ds(b, 1)].to_broadcast([P, H, P])
                dve.tensor_tensor(diag_q.rearrange("p (h m) -> p h m", h=H),
                                  ident[:, :].unsqueeze(1).to_broadcast([P, H, P]), query, ALU.mult).then_inc(dq_ready, 1)

            def sample_out(b):
                dve.wait_ge(spv_done, b + 1)
                dve.wait_ge(lsum_done, b + 1)
                link(dve.reciprocal(small[:, 560:576], bank[5][:, 0:16]))
                o = bank[4][:, 0:16].rearrange("p (h j) -> p h j", j=2)
                r = small[:, 560:576].rearrange("p (h j) -> p h j", j=2)
                ch.did(dve.tensor_tensor(small[:, 576:584], o[:, :, 0], r[:, :, 0], ALU.mult))
                link(dve.tensor_tensor(small[:, 584:592], o[:, :, 1], r[:, :, 1], ALU.mult))
                dst = att[:, :].rearrange("p (h n) -> p h n", h=H)[:, :, bass.ds(T + b, 1)].rearrange("p h o -> p (h o)")
                dve.scalar_tensor_tensor(dst, small[:, 584:592], small[:, 25:26], small[:, 576:584], ALU.mult,
                                         ALU.add).then_inc(o_read, 1)

            def decode(b, summed):
                diag(b)
                wait(dve, sexp_ready, b)
                for p in range(PAGES + 1):
                    dve.wait_ge(kq_ready, 17 * b + p + 1)
                    dve.tensor_reduce(score[:, p * 16:(p + 1) * 16], kq[p % 2].rearrange("p (m d) -> p m d", d=HD),
                                      AX.X, ALU.add).then_inc(kq_read, 1)
                dve.wait_ge(kq_read, 17 * b + 17)
                s4 = score.rearrange("p (g h j) -> p g h j", h=H, j=2)
                for j in range(2):
                    ch.did(dve.tensor_tensor(s4[:, 0:PAGES, :, j], s4[:, 0:PAGES, :, j],
                                             bias_pg[:, :].rearrange("p (g h) -> p g h", h=H), ALU.add))
                    ch.did(dve.tensor_tensor(s4[:, PAGES, :, j], s4[:, PAGES, :, j],
                                             bias_nw[:, bass.ds(b * H, H)], ALU.add))
                ch.wait()
                dve.tensor_reduce(small[:, 512:528], score.rearrange("p (g c) -> p c g", c=16), AX.X,
                                  ALU.max).then_inc(smax_ready, 1)
                if summed:
                    sample_out(b - 1)
                dve.wait_ge(gmax_ready, b + 1)
                s3 = score.rearrange("p (g c) -> p g c", c=16)
                dve.tensor_tensor(s3, s3, small[:, 528:544].unsqueeze(1).to_broadcast([P, PAGES + 1, 16]),
                                  ALU.subtract).then_inc(ssub_ready, 1)
                dve.wait_ge(sexp_ready, b + 1)
                wait(dve, lsum_done, b)
                dve.tensor_reduce(small[:, 544:560], prob.rearrange("p (g c) -> p c g", c=16), AX.X,
                                  ALU.add).then_inc(lsum_ready, 1)

            dve.wait_ge(mst_ready, HT)
            dve.wait_ge(z_read, L1)
            decode(0, False)
            dve.wait_ge(gelu_act, 2)
            dve.scalar_tensor_tensor(yg[:, :], gelu_t, 1.0, yg[:, :], ALU.add, ALU.mult).then_inc(gelu_dve, 1)
            with dve.Fori(1, B) as b:
                ch.enter(b, 1, 7)
                decode(b, True)
            ch.leave(B - 1)
            sample_out(B - 1)

            sq = big[:, 2 * KW + 64:2 * KW + 64 + H * N]
            dve.wait_ge(root_ready, H)
            link(dve.reciprocal(sq, sq))
            dve.scalar_tensor_tensor(att[:, :], att[:, :], small[:, 30:31], sq, ALU.mult, ALU.mult).then_inc(att_ready, 1)
            for j in range(HT):
                dve.wait_ge(z_read, L2 + j + 1)
                dve.scalar_tensor_tensor(big[:, j * N:(j + 1) * N], big[:, 4352 + (j % 2) * N:4352 + (j % 2 + 1) * N],
                                         1.0, yg[:, j * N:(j + 1) * N], ALU.add, ALU.mult).then_inc(ssm_ready, 1)

            def merge(i):
                for j in range(4):
                    n = 4 * i + j
                    one, two = (big[:, 5000 + k * 2 * N + (j % 2) * N:5000 + k * 2 * N + (j % 2 + 1) * N] for k in range(2))
                    wait(dve, merged_ready, n - 1)
                    dve.wait_ge(slot_done, GLU + n + 1)
                    n1 = ch.did(dve.scalar_tensor_tensor(one, gate[:, bass.ds(n * N, N)], 1.0, bank[j % 2][:, 0:N],
                                                         ALU.add, ALU.mult))
                    dve.scalar_tensor_tensor(two, gate[:, bass.ds((KT + n) * N, N)], 1.0, bank[2 + j % 2][:, 0:N],
                                             ALU.add, ALU.mult).then_inc(zv_read, 1)
                    ch.wait(n1)
                    dve.wait_ge(zv_read, n + 1)
                    dve.scalar_tensor_tensor(merged[:, bass.ds(n * N, N)], two, 0.25, one, ALU.mult, ALU.add
                                             ).then_inc(merged_ready, 1)

            merge(0)
            with dve.Fori(1, 4) as i:
                ch.enter(i, 1, 4)
                merge(i)
            ch.leave(3)

            def residual(n, j, done, count):
                dve.wait_ge(done, count)
                tile = xt[:, bass.ds(n * N, N)]
                dve.scalar_tensor_tensor(tile, tile, 2 * ALPHA, bank[j % 2][:, 0:N], ALU.mult, ALU.add).then_inc(zv_read, 1)

            def norm(ln):
                dve.wait_ge(mean_done, ln + 1)
                for g in range(4):
                    c3 = x3[:, 4 * g:4 * g + 4, :]
                    dve.tensor_tensor(c3, c3, bank[6][:, 0:N].unsqueeze(1).to_broadcast([P, 4, N]),
                                      ALU.subtract).then_inc(cent_ready, 1)
                dve.wait_ge(std_ready, ln + 1)
                link(dve.reciprocal(std_sb, std_sb))
                for g in range(4):
                    c3 = x3[:, 4 * g:4 * g + 4, :]
                    dve.tensor_tensor(c3, c3, std_sb.unsqueeze(1).to_broadcast([P, 4, N]), ALU.mult).then_inc(norm_ready, 1)

            with dve.Fori(0, KT // 4) as n:
                for j in range(4):
                    residual(4 * n + j, j, slot_done, PROJ + 4 * n + j + 1)
            norm(0)

            state3 = conv_state[:, :].rearrange("p (t b i) -> p t b i", b=B, i=2)

            def up(n, pairs):
                for q in range(pairs):
                    for v in range(2):
                        t = 2 * q + v
                        tile = 2 * n + q + v * FT
                        y, ps = acc[t], bank[t]

                        def par(w):
                            return conv_par[:, bass.ds(w * 2 * FT + tile, 1)]

                        def old(i):
                            return state3[:, bass.ds(tile, 1), :, i].rearrange("p o b -> p (o b)")

                        dve.wait_ge(tap0, 4 * n + t + 1)
                        n1 = ch.did(dve.scalar_tensor_tensor(y[:, 1:T], ps[:, 0:T - 1], par(1), y[:, 1:T], ALU.mult, ALU.add))
                        n2 = ch.did(dve.scalar_tensor_tensor(y[:, T:N], old(1), par(1), y[:, T:N], ALU.mult, ALU.add))
                        ch.wait(n1)
                        dve.scalar_tensor_tensor(y[:, 2:T], ps[:, 0:T - 2], par(0), y[:, 2:T], ALU.mult, ALU.add
                                                 ).then_inc(zv_read, 1)
                        ch.wait(n2)
                        dve.scalar_tensor_tensor(y[:, T:N], old(0), par(0), y[:, T:N], ALU.mult, ALU.add
                                                 ).then_inc(tap_done, 1)
                    dve.wait_ge(th_ready, 2 * n + q + 1)
                    link(dve.scalar_tensor_tensor(th[q], th[q], 1.0, acc[2 * q], ALU.add, ALU.mult))
                    dve.wait_ge(tap_done, 4 * n + 2 * q + 2)
                    dve.tensor_tensor(hid[:, bass.ds((2 * n + q) * N, N)], th[q], acc[2 * q + 1], ALU.mult
                                      ).then_inc(hid_ready, 1)

            up(0, 2)
            with dve.Fori(1, FT // 2) as n:
                ch.enter(n, 1, 10)
                up(n, 2)
            ch.leave(FT // 2 - 1)
            up(FT // 2, 1)
            with dve.Fori(0, KT // 4) as n:
                for j in range(4):
                    residual(4 * n + j, j, down_used, 8 * n + 2 * j + 2)
            norm(1)
            for c in range(3):
                rows = min(P, N - c * P)
                for g in range(4):
                    n = 4 * c + g
                    dve.wait_ge(yt_done, n + 1)
                    dve.tensor_copy(big[0:rows, c * D + g * 512:c * D + (g + 1) * 512], bank[n % 4][0:rows, :]
                                    ).then_inc(yt_read, 1)


_OUTS = [
    ("y_prompt", (T, D), (1, T, D)),
    ("y_sample", (B, D), (B, 1, D)),
    ("k_prompt", (T, KW), (1, 1, T, H, 2, HD)),
    ("v_prompt", (T, SW), (1, 1, T, H, P)),
    ("ssm_re_prompt", (PAIRS, P), (1, 1, G, S)),
    ("ssm_im_prompt", (PAIRS, P), (1, 1, G, S)),
    ("conv_prompt", (2, 2 * FF), (1, 1, 2, 2 * FF)),
    ("k_sample", (B, KW), (1, B, 1, H, 2, HD)),
    ("v_sample", (B, SW), (1, B, 1, H, P)),
    ("ssm_re_sample", (B * PAIRS, P), (1, B, G, S)),
    ("ssm_im_sample", (B * PAIRS, P), (1, B, G, S)),
    ("conv_sample", (1, B, 2, 2 * FF), (1, B, 2, 2 * FF)),
]


def kernel(**inputs):
    import concourse.bacc as _bacc
    from concourse.bass_utils import run_bass_kernel_spmd as _run

    nc = _bacc.Bacc("TRN2", target_bir_lowering=False, num_devices=1)
    arrays, args, outs = {}, {}, {}
    named = {name: np.ascontiguousarray(array) for name, array in inputs.items()}
    named["buckets"] = bucket_table()
    for name, array in named.items():
        arrays[f"in_{name}"] = array
        args[name] = nc.dram_tensor(f"in_{name}", array.shape, mybir.dt.from_np(array.dtype), kind="ExternalInput").ap()
    for name, shape, _ in _OUTS:
        outs[name] = nc.dram_tensor(f"out_{name}", shape, F32, kind="ExternalOutput").ap()
    scratch = nc.dram_tensor("toeplitz_rows", (H, P, 384), F32, kind="Internal").ap()
    build(nc, args, outs, scratch)
    r = _run(nc, [arrays], core_ids=[0])
    return tuple(np.asarray(r.results[0][f"out_{name}"]).reshape(shape) for name, _, shape in _OUTS)
```

```python
from contextlib import ExitStack

import numpy as np

import concourse.bass as bass
from concourse import mybir

ALU = mybir.AluOpType
ACT = mybir.ActivationFunctionType
AX = mybir.AxisListType
F32 = mybir.dt.float32
I32 = mybir.dt.int32
F32R = mybir.dt.float32r

P = 128
D = 2048
T = 256
B = 8
N = T + B
H = 8
HD = 64
PAGES = 16
POOL_PAGES = 160
KW = H * 2 * HD
SW = 1024
G = 64
S = 64
C = 16
PAIRS = G // 2
FF = 5504
FT = FF // P
KT = D // P
HT = SW // P
NB = 32
SLOTS = 4
DOWN_PARTS = ((0, 16), (16, 32), (32, FT))
ALPHA = 2.0 ** 0.25
EPS = 1e-5
LAM_INIT = 0.2
MASK = -1e30
PI = float(np.pi)
TWO_PI_DOWN = 6.2831845
MEAN_SHIFT = 1.0 / D

TOEP = 383
OH_TOEP, OH_PAGE, OH_NEW = 0, 384, 384 + PAGES * P
OH_COLS = OH_NEW + B * P


def bucket_table():
    def bucket(n):
        n = np.maximum(n, 0)
        large = 16 + (np.log(np.maximum(n, 1).astype(np.float32) / np.float32(16)) / np.float32(np.log(8.0))
                      * np.float32(16)).astype(np.int32)
        return np.where(n < 16, n, np.minimum(large, NB - 1))

    table = np.zeros((NB + 1, OH_COLS), np.float32)

    def mark(cols, dist):
        row = np.where(dist < 0, NB, bucket(dist))
        table[row, cols] = 1.0

    y = np.arange(TOEP)
    mark(OH_TOEP + y, 255 - y)
    k = np.arange(PAGES * P)
    mark(OH_PAGE + k, PAGES * P - k)
    for b in range(B):
        r = np.arange(P)
        mark(OH_NEW + b * P + r, np.where(r == b, 0, -1))
    return table


def wait(eng, sem, value):
    if isinstance(value, int) and value <= 0:
        return
    eng.wait_ge(sem, value)


class Chain:

    def __init__(self, eng, sem):
        self.eng, self.sem, self.base, self.n = eng, sem, 0, 0

    def did(self, ins):
        ins.then_inc(self.sem, 1)
        self.n += 1
        return self.n

    def wait(self, n=None):
        wait(self.eng, self.sem, self.base + (self.n if n is None else n))

    def enter(self, i, first, per):
        self.outer, self.per = self.base + self.n, per
        self.base, self.n = self.outer + (i - first) * per, 0

    def leave(self, turns):
        assert self.n == self.per, (self.n, self.per)
        self.base, self.n = self.outer + turns * self.per, 0


def build(nc, a, out, scratch):
    with ExitStack() as ctx:
        def sb(name, cols, dt=F32, rows=P):
            return ctx.enter_context(nc.sbuf_tensor(name, [rows, cols], dt))

        def sem(name):
            return ctx.enter_context(nc.semaphore(name))

        w_in, w_glu, w_pa, w_ps, w_out, w_up, w_down = (
            a[name][0] for name in ("w_in", "w_glu", "w_proj_attn", "w_proj_ssm", "w_out", "w_up", "w_down"))

        ring = sb("weight_ring", SLOTS * KT * P)
        conv_state = sb("conv_state_t", 2 * FT * 2 * B)
        conv_par = sb("conv_par", 4 * 2 * FT)
        ln_par = sb("ln_par", 4 * KT)
        ident = sb("ident", P)
        ones = sb("ones", P)
        mean_w = sb("mean_w", P)
        v_mean_w = sb("v_mean_w", P)
        small = sb("small", 592)
        page_no = sb("page_numbers", B * PAGES, I32, rows=1)

        def overlay(*parts):
            with ExitStack() as stage:
                placed = [stage.enter_context(nc.sbuf_tensor(name, [P, cols], F32)) for name, cols in parts]
            return [t for t, (name, _) in zip(placed, parts) if not name.startswith("skip")]

        GATES = 2 * KT * N
        s_lo, m_hi, m_lo, a_hi, w_hi, a_lo, w_lo, s_hi = overlay(
            ("skip_x_gates", KT * N + GATES), ("ssm_lo", HT * N), ("skip1", 704), ("merged_hi", KT * N),
            ("merged_lo", KT * N), ("att_hi", HT * N), ("skip2", 888), ("weights_hi", 2 * KT * P), ("skip3", 32),
            ("att_lo", HT * N), ("skip4", HT * N), ("weights_lo", 2 * KT * P), ("ssm_hi", HT * N))
        h_hi, hid_hi, hid_lo, h_lo, late = overlay(
            ("h_hi", KT * N), ("hidden_hi", FT * N), ("hidden_lo", FT * N), ("skip5", 4136), ("h_lo", KT * N),
            ("skip_weights_lo", 2 * KT * P), ("ffn_scratch", 2144))
        xt = sb("x_t", KT * N)
        gd = sb("gates", 11264)
        big = sb("big", FT * N)
        mm = sb("matrices", KT * N)
        att = sb("att", H * N)
        yg = sb("ssm_y", HT * N)
        c_rows = sb("c_rows", 2 * HT * P)
        kv_new = sb("kv_new", 2 * KW)
        par_rows = sb("parameter_rows", 4 * P)
        x0_rows = sb("x0_rows", 4 * P)
        x0 = sb("x0", 4 * P)
        xf = sb("x_final", 2 * 9 * PAIRS)
        q_s = sb("q_sample", H * B)
        scan_par = sb("scan_par", 7 * PAIRS)
        bias_pg = sb("bias_pages", PAGES * H)
        bias_nw = sb("bias_new", B * H)
        ln_rows = xf[:, 0:4 * P]
        score, prob = mm[:, KW:KW + 272], mm[:, KW + 272:KW + 544]
        multiples_i = q_s[:, 0:32].bitcast(I32)

        bank = [ctx.enter_context(nc.psum_tensor(f"bank{i}", [P, 512], F32)) for i in range(8)]

        def slot(j, kt):
            return ring[:, (j * KT + kt) * P:(j * KT + kt + 1) * P]

        def slot3(j, k0, k1):
            return ring[:, (j * KT + k0) * P:(j * KT + k1) * P].rearrange("p (k m) -> p k m", m=P)

        def rounded(t, k, width=N):
            return t[:, k * width:(k + 1) * width].bitcast(F32R)

        def weight(t, m, k):
            return rounded(t, (m % 2) * KT + k, P)

        def xtile(k):
            return xt[:, k * N:(k + 1) * N]

        x3 = xt[:, :].rearrange("p (k n) -> p k n", n=N)
        x_rows = big[:, 0:3 * D].rearrange("p (c d) -> p c d", c=3)
        k_ring = [big[:, i * KW:(i + 1) * KW] for i in range(4)]
        v_ring = [big[:, (4 + i) * KW:(5 + i) * KW] for i in range(4)]
        kq = [big[:, (8 + i) * KW:(9 + i) * KW] for i in range(2)]
        q_all = big[:, 10 * KW:11 * KW]
        st_rows = gd[0:2 * B, 0:2 * FF]
        k_new, v_new = kv_new[:, 0:KW], kv_new[:, KW:2 * KW]
        gate = gd[:, 0:GATES]
        diag_q = mm[:, 0:KW]
        o_rows = c_rows[0:16, 0:KW]

        def cutter(tensor, start, end):
            at = [start]

            def cut(cols):
                at[0] += cols
                assert at[0] <= end
                return tensor[:, at[0] - cols:at[0]]
            return cut

        gcut = cutter(gd, 0, 11264)
        bias = gcut(H * 384)
        u_all = gcut(HT * N)
        q_t, k_t, v_t, u_t = gcut(N), gcut(N), gcut(N), gcut(N)
        s_sb, p_sb = gcut(768), gcut(768)
        p_diff, p_diff_t = gcut(384), gcut(384)
        v_rows, k_rows = gcut(256), gcut(256)
        toep_rows = gcut(384)
        bcut = cutter(big, 4 * KW, FT * N)
        tab = [bcut(512) for _ in range(2)]
        rot = [bcut(256) for _ in range(4)]
        z_re, z_im, y_re, y_im = bcut(256), bcut(256), bcut(256), bcut(256)
        x_st = [bcut(2 * N) for _ in range(2)]
        ptmp = c_rows[:, 0:1024]
        mst = bcut(512)
        ang = bcut(2048)
        MT = mm[:, 0:HT * 512].rearrange("p (t c) -> p t c", t=HT)
        fcut = cutter(late, 0, 2144)
        acc = [fcut(N) for _ in range(4)]
        th = [fcut(N) for _ in range(2)]
        up10 = fcut(40)
        up_rows = fcut(512)[0:10]
        std_sb = acc[0]
        h_tmp = [acc[1], acc[2], acc[3], th[0]]

        def sems(*names):
            return [sem(n) for n in names]

        wh_ready, wh_used, wl_ready, hn_ready = sems("weights_hi_ready", "weights_hi_used", "weights_lo_ready",
                                                     "h_unsplit_ready")
        ring_in = sems(*(f"weights_in{j}" for j in range(SLOTS)))
        k_in = sems(*(f"k_in{j}" for j in range(4)))
        v_in = sems(*(f"v_in{j}" for j in range(4)))
        xs_in, tab_in, par_in, st_in = sems("x_in", "table_in", "params_in", "state_in")
        rows_in, b_in, c_in, x0_in, page_in = sems("scan_rows_in", "b_in", "c_in", "x0_in", "pages_in")
        toep_out, toep_in = sems("toeplitz_out", "toeplitz_in")
        kv_stored, out_stored, upr_stored, y_stored = sems("kv_stored", "out_stored", "up_rows_stored", "y_stored")
        x_zero, rel_ready, const_ready, mt_zero = sems("x_rows_zeroed", "rel_ready", "constants_ready", "matrices_zeroed")
        bpad_zero, mult_ready = sems("b_padding_zeroed", "angle_multiples")
        tr, tr_used = sems("setup_transposed", "setup_copied")
        s5_tr, s5_used, s5_act, s5_dve = sems("s5_transposed", "s5_copied", "s5_act_steps", "s5_dve_steps")
        kv_zero, lam_exp = sems("kv_new_zeroed", "lambda_exp")
        pool_c, dve_c, act_c = sems("pool_chain", "dve_chain", "act_chain")
        slot_done, z_read, zv_read = sems("m_tiles_done", "m_tiles_read_by_act", "m_tiles_read_by_dve")
        kt_done, kt_read, vt_done, vt_read = sems("k_transposed", "k_rows_copied", "v_transposed", "v_rows_copied")
        sc_done, max_ready, exp_done = sems("scores_done", "max_ready", "exp_done")
        pd_ready, pdt_done, pdt_read, pv_done, pv_read = sems(
            "p_diff_ready", "p_diff_transposed", "p_diff_copied", "pv_done", "pv_read")
        mst_ready, tab_ready, b_done, b_read, xs_ready, c_done, xf_read, y_ready = sems(
            "matrices_staged", "rotation_ready", "bu_done", "bu_read", "states_ready", "y_sums_done",
            "final_states_read", "y_ready")
        xft, xft_read = sems("final_states_transposed", "final_states_copied")
        dq_ready, qb_done, qb_ready, kq_ready, kq_read = sems(
            "diag_q_ready", "q_broadcast", "q_broadcast_copied", "kq_ready", "kq_reduced")
        smax_ready, gmax_ready, ssub_ready, sexp_ready, lsum_ready, lsum_done, spv_done, v_used, o_read = sems(
            "page_max_ready", "global_max_ready", "shifted_ready", "sample_exp_ready", "page_sum_ready",
            "denominator_ready", "sample_pv_done", "v_pages_used", "sample_out_read")
        w_ready, o_copied, ocomb_done = sems("map_weights_ready", "sample_pv_copied", "sample_out_done")
        gelu_act, gelu_dve = sems("gelu_act", "gelu_dve")
        sq_ready, ms_done, root_ready, att_ready, glu_t, ssm_ready, merged_ready, r_ready = sems(
            "squares_ready", "mean_squares", "roots_ready", "att_ready", "glu_tanh", "ssm_ready", "merged_ready",
            "residual_ready")
        mean_done, cent_ready, csq_ready, var_done, std_ready, norm_ready, h_ready = sems(
            "mean_done", "centred", "centred_squares", "var_done", "std_ready", "normalised", "h_ready")
        tap0, tap_done, th_ready, th_used, hid_ready = sems("tap0", "taps_done", "tanh_ready", "tanh_used", "hidden_ready")
        upt_done, upt_read, yt_done, yt_read = sems(
            "up_rows_transposed", "up_rows_copied", "y_transposed", "y_copied")
        block = ctx.enter_context(nc.Block())

        L1, L2 = 4 * H, 8 * H
        GLU, PROJ, OUT = L2 + HT, L2 + HT + KT, L2 + HT + 2 * KT
        UP = OUT + 2 * FT
        SPLIT_UP, SPLIT_DOWN = OUT - GLU, UP - GLU

        @block.sync
        def _(sp):
            def load_slot(n, j, *parts, split=False):
                if split:
                    sp.wait_ge(wl_ready, n - SLOTS - GLU + 1)
                else:
                    wait(sp, slot_done, n - SLOTS + 1)
                k0 = 0
                for w, rows, col in parts:
                    src = w[0:rows, bass.ds(col, P)].rearrange("(k p) m -> p k m", p=P)
                    sp.dma_start(slot3(j, k0, k0 + rows // P), src).then_inc(ring_in[j], 16)
                    k0 += rows // P

            def load_head(i):
                for j in range(4):
                    load_slot(4 * i + j, j, (w_in, D, i * P + j * SW))

            sp.dma_start(x_rows[:, 0:2, :], a["x_prompt"][0].rearrange("(c p) d -> p c d", p=P)).then_inc(xs_in, 16)
            sp.wait_ge(x_zero, 1)
            sp.dma_start(x_rows[0:B, 2, :], a["x_sample"].rearrange("b o d -> (b o) d")).then_inc(xs_in, 16)
            for n, name in enumerate(("ssm_a_re", "ssm_a_im")):
                sp.dma_start(yg[0:PAIRS, n * P:(n + 1) * P],
                             a[name][0].rearrange("(q g) s -> q (g s)", g=2)).then_inc(rows_in, 16)
            sp.dma_start(small[0:PAIRS, 0:2],
                         a["ssm_log_dt"].rearrange("o (q g) -> (o q) g", g=2)).then_inc(rows_in, 16)
            load_slot(0, 0, (w_in, D, 0))
            for n, name in enumerate(("ssm_c_re", "ssm_c_im")):
                rows = c_rows[:, n * 1024:(n + 1) * 1024].rearrange("p (t e s) -> p t e s", t=HT, e=2)
                src = a[name][0].rearrange("(t g) c s -> (g c) t s", t=HT)
                for e in range(2):
                    sp.dma_start(rows[:, :, e, :], src).then_inc(c_in, 16)
            for n, name in enumerate(("ssm_b_re", "ssm_b_im")):
                sp.dma_start(att[:, n * 512:(n + 1) * 512].rearrange("p (q c) -> p q c", c=C),
                             a[name][0].rearrange("(q g) s c -> (g s) q c", g=2)).then_inc(b_in, 16)
            for r, name in enumerate(("state_ssm_re", "state_ssm_im")):
                for h in range(2):
                    sp.dma_start(x0_rows[:, (2 * r + h) * P:(2 * r + h + 1) * P],
                                 a[name][0, 4 * h:4 * h + 4].rearrange("b (q g) s -> (b q) (g s)", g=2)
                                 ).then_inc(x0_in, 16)
            load_slot(1, 1, (w_in, D, SW))
            sp.dma_start(par_rows[0:2 * FT, 0:3 * P].rearrange("t (w p) -> t w p", w=3),
                         a["conv_w"][0].rearrange("w (t p) -> t w p", p=P)).then_inc(par_in, 16)
            sp.dma_start(par_rows[0:2 * FT, 3 * P:4 * P],
                         a["conv_b"].rearrange("o (t p) -> (o t) p", p=P)).then_inc(par_in, 16)
            for n, name in enumerate(("ln1_g", "ln1_b", "ln2_g", "ln2_b")):
                sp.dma_start(ln_rows[0:KT, n * P:(n + 1) * P],
                             a[name].rearrange("o (t p) -> (o t) p", p=P)).then_inc(par_in, 16)
            for n, name in enumerate(("lambda_q1", "lambda_k1", "lambda_q2", "lambda_k2")):
                sp.dma_start(small[:, 64 + n * HD:64 + (n + 1) * HD],
                             a[name].to_broadcast([P, HD])).then_inc(par_in, 16)
            with nc.allow_non_contiguous_dma("one column each"):
                sp.dma_start(small[:, 16:24], a["ssm_d"].rearrange("o (t p) -> p (o t)", p=P)).then_inc(par_in, 16)
                sp.dma_start(small[:, 24:25], a["subln_g"].rearrange("o p -> p o")).then_inc(par_in, 16)
            sp.dma_start(st_rows, a["state_conv"][0].rearrange("b i f -> (b i) f")).then_inc(st_in, 16)
            sp.dma_start(mm[0:NB + 1, 0:OH_COLS], a["buckets"]).then_inc(tab_in, 16)
            sp.wait_ge(rel_ready, 1)
            sp.dma_start(small[0:NB, 32:32 + H], a["rel_bias"]).then_inc(tab_in, 16)
            sp.dma_start(page_no[0:1, :], a["page_table"].rearrange("(o b) g -> o (b g)", o=1)).then_inc(page_in, 16)
            sp.dma_start(out["conv_sample"][0, :, 0, :], a["state_conv"][0, :, 1, :]).then_inc(out_stored, 16)
            load_slot(2, 2, (w_in, D, 2 * SW))
            load_slot(3, 3, (w_in, D, 3 * SW))
            sp.wait_ge(tr_used, 22)
            sp.dma_start(scratch, toep_rows[0:H, :].unsqueeze(1).to_broadcast([H, P, 384])).then_inc(toep_out, 16)
            sp.wait_ge(toep_out, 16)
            b3 = bias.rearrange("p (h x) -> p h x", h=H)
            sp.dma_start(b3[:, :, 0:256],
                         bass.AP(scratch.tensor, P - 1, [[383, P], [384 * P, H], [1, 256]])).then_inc(toep_in, 16)
            sp.dma_start(b3[:, :, 256:384],
                         bass.AP(scratch.tensor, 2 * P - 1, [[383, P], [384 * P, H], [1, P]])).then_inc(toep_in, 16)

            def store_head(i):
                sp.wait_ge(kt_read, i + 1)
                sp.wait_ge(vt_read, i + 1)
                for rows, name in ((k_rows, "k_prompt"), (v_rows, "v_prompt")):
                    sp.dma_start(out[name].rearrange("(c p) k -> p c k", p=P)[:, :, bass.ds(i * P, P)],
                                 rows.rearrange("p (c d) -> p c d", c=2)).then_inc(kv_stored, 16)

            with sp.Fori(1, H) as i:
                load_head(i)
                store_head(i - 1)

            ck = a["cache_k"][0].rearrange("n p h j d -> n p (h j d)")
            cv = a["cache_v"][0].rearrange("n p h e -> n p (h e)")

            def load_page(cache, ring4, arrived, b, p):
                page = sp.value_load(page_no[0:1, bass.ds(b * PAGES + p, 1)], min_val=0, max_val=POOL_PAGES - 1)
                sp.dma_start(ring4[p % 4], cache[bass.ds(page, 1)].rearrange("o p k -> (o p) k")
                             ).then_inc(arrived[p % 4], 16)

            def load_batch(b, keys, values):
                for p in range(PAGES):
                    if keys and p % 4 == 0:
                        r = p // 4
                        load_slot(L1 + 4 * b + r, r, (w_in, D, 4 * SW + b * 4 * P + r * P))
                    if keys:
                        wait(sp, kq_ready, 17 * b + p - 3 if p >= 4 else 17 * (b - 1) + 12 + p + 1)
                        load_page(ck, k_ring, k_in, b, p)
                    if values:
                        wait(sp, v_used, PAGES * (b - 1) + p - 3)
                        load_page(cv, v_ring, v_in, b - 1, p)

            sp.wait_ge(page_in, 16)
            load_batch(0, True, False)
            store_head(H - 1)
            sp.wait_ge(xft_read, 2)
            for r, name in enumerate(("ssm_re_prompt", "ssm_im_prompt")):
                sp.dma_start(out[name], par_rows[0:PAIRS, r * P:(r + 1) * P]).then_inc(out_stored, 16)
            for r, name in enumerate(("ssm_re_sample", "ssm_im_sample")):
                for h in range(2):
                    sp.dma_start(out[name][h * P:(h + 1) * P, :],
                                 x0_rows[:, (2 * r + h) * P:(2 * r + h + 1) * P]).then_inc(out_stored, 16)
            sp.dma_start(out["k_sample"], k_new[0:B, :]).then_inc(out_stored, 16)
            sp.dma_start(out["v_sample"], v_new[0:B, :]).then_inc(out_stored, 16)
            load_batch(1, True, True)
            with sp.Fori(2, B) as b:
                load_batch(b, True, True)
            load_batch(B, False, True)
            with sp.Fori(0, HT // 4) as i:
                for j in range(4):
                    load_slot(L2 + 4 * i + j, j, (w_glu, SW, i * 4 * P + j * P))

            def load_proj(i, split=True):
                for j in range(4):
                    load_slot(GLU + 4 * i + j, j, (w_pa, SW, i * 4 * P + j * P), (w_ps, SW, i * 4 * P + j * P),
                              split=split)

            load_proj(0, False)
            with sp.Fori(1, KT // 4) as i:
                load_proj(i)
            with sp.Fori(0, KT // 4) as i:
                for j in range(4):
                    load_slot(PROJ + 4 * i + j, j, (w_out, D, i * 4 * P + j * P), split=True)

            def load_up(n, pairs):
                for q in range(pairs):
                    load_slot(OUT + 4 * n + 2 * q, 2 * q, (w_up, D, n * 2 * P + q * P), split=True)
                    load_slot(OUT + 4 * n + 2 * q + 1, 2 * q + 1, (w_up, D, FF + n * 2 * P + q * P), split=True)

            def store_up(n, pairs):
                sp.wait_ge(upt_read, n + 1)
                for v in range(2):
                    rows = up_rows.rearrange("r (q v m) -> r v q m", q=2, v=2)[:, v, 0:pairs, :]
                    cols = bass.ds(v * FF + n * 2 * P, pairs * P)
                    sp.dma_start(out["conv_prompt"][:, cols].rearrange("r (q m) -> r q m", m=P),
                                 rows[0:2]).then_inc(upr_stored, 16)
                    sp.dma_start(out["conv_sample"][0, :, 1, cols].rearrange("r (q m) -> r q m", m=P),
                                 rows[2:10]).then_inc(upr_stored, 16)

            load_up(0, 2)
            with sp.Fori(1, FT // 2) as n:
                load_up(n, 2)
                store_up(n - 1, 2)
            load_up(FT // 2, 1)

            def load_down(i, o):
                k0, k1 = DOWN_PARTS[o % 3]
                j = (UP + o) % SLOTS
                sp.wait_ge(wl_ready, i * 12 + SPLIT_DOWN + o - SLOTS + 1)
                src = w_down[k0 * P:k1 * P, bass.ds(i * 4 * P + o // 3 * P, P)].rearrange("(k p) m -> p k m", p=P)
                sp.dma_start(slot3(j, 0, k1 - k0), src).then_inc(ring_in[j], 16)

            for o in range(12):
                load_down(0, o)
                if o == 1:
                    store_up(FT // 2 - 1, 2)
            store_up(FT // 2, 1)
            with sp.Fori(1, KT // 4) as i:
                for o in range(12):
                    load_down(i, o)
            for c in range(3):
                sp.wait_ge(yt_read, 4 * c + 4)
                rows = big[:, c * D:(c + 1) * D]
                if c < 2:
                    sp.dma_start(out["y_prompt"][c * P:(c + 1) * P, :], rows).then_inc(y_stored, 16)
                else:
                    sp.dma_start(out["y_sample"], rows[0:B]).then_inc(y_stored, 16)
            sp.wait_ge(y_stored, 3 * 16)
            sp.wait_ge(kv_stored, 2 * H * 16)
            sp.wait_ge(out_stored, 9 * 16)
            sp.wait_ge(upr_stored, 4 * (FT // 2 + 1) * 16)

        @block.gpsimd
        def _(pool):
            ch = Chain(pool, pool_c)
            pool.memset(x_rows[:, 2, :], 0.0).then_inc(x_zero, 1)
            ch.did(pool.memset(ident[:, :], 0.0))
            ch.wait()
            pool.affine_select(out=ident[:, :], in_=ident[:, :], compare_op=ALU.not_equal, fill=1.0, base=0,
                               pattern=[[-1, P]], channel_multiplier=1).then_inc(const_ready, 1)
            pool.memset(small[0:NB + 1, 32:32 + H], MASK).then_inc(rel_ready, 1)
            for tensor, value in ((ones[:, :], 1.0), (mean_w[:, :], 1.0 / D), (v_mean_w[:, :], 1.0 / P),
                                  (small[:, 4:5], PI / 2), (small[:, 5:6], EPS), (small[:, 6:7], 4 * EPS)):
                pool.memset(tensor, value).then_inc(const_ready, 1)
            ch.did(pool.iota(multiples_i[:, 0:16], pattern=[[1, 16]], base=1, channel_multiplier=0))
            ch.did(pool.iota(multiples_i[:, 16:32], pattern=[[16, 16]], base=0, channel_multiplier=0))
            ch.wait()
            pool.tensor_copy(small[:, 320:352], multiples_i[:, 0:32]).then_inc(mult_ready, 1)
            pool.memset(kv_new[:, :], 0.0).then_inc(bpad_zero, 1)
            pool.wait_ge(tr, 24)
            pool.memset(MT[:, :, 256:512], 0.0).then_inc(mt_zero, 1)
            pool.wait_ge(s5_tr, 10)
            pool.memset(kv_new[:, :], 0.0).then_inc(kv_zero, 1)
            pool.wait_ge(s5_dve, 7)
            pool.wait_ge(s5_act, 6)
            pool.wait_ge(s5_used, 10)

            ang4 = ang.rearrange("p (r q e) -> p r q e", r=2, q=PAIRS)

            def rotation(t, p):
                n = 4 * t + p

                def fine(r):
                    return ang4[:, r, bass.ds(n, 1), 0:16].to_broadcast([P, 16, 16])

                def coarse(r):
                    return ang4[:, r, bass.ds(n, 1), 16:32].rearrange("p o e -> p e o").to_broadcast([P, 16, 16])

                cos, sin = (tab[p % 2][:, r * 256:(r + 1) * 256].rearrange("p (a b) -> p a b", a=16) for r in range(2))
                t1, t2, t3, t4 = (ptmp[:, k * 256:(k + 1) * 256].rearrange("p (a b) -> p a b", a=16) for k in range(4))
                wait(pool, tab_ready, n)
                ch.did(pool.tensor_tensor(t1, coarse(0), fine(0), ALU.mult))
                ch.did(pool.tensor_tensor(t2, coarse(1), fine(1), ALU.mult))
                ch.did(pool.tensor_tensor(t3, coarse(1), fine(0), ALU.mult))
                ch.did(pool.tensor_tensor(t4, coarse(0), fine(1), ALU.mult))
                wait(pool, xs_ready, n - 1)
                ch.wait()
                ch.did(pool.tensor_tensor(cos, t1, t2, ALU.subtract))
                pool.tensor_tensor(sin, t3, t4, ALU.add).then_inc(tab_ready, 1)

            def s5_tile(t):
                wait(pool, c_done, 4 * t)
                pool.tensor_copy(mst, MT[:, bass.ds(t, 1), :].rearrange("p o c -> p (o c)")).then_inc(mst_ready, 1)
                for p in range(4):
                    rotation(t, p)

            s5_tile(0)
            with pool.Fori(1, HT) as t:
                ch.enter(t, 1, 20)
                s5_tile(t)
            ch.leave(HT - 1)

            pool.wait_ge(c_done, 4 * HT)
            pool.wait_ge(xf_read, 4 * HT)

            def score_products(b):
                for p in range(PAGES + 1):
                    if p < PAGES:
                        pool.wait_ge(k_in[p % 4], 16 * (4 * b + p // 4 + 1))
                    if p == 0:
                        pool.wait_ge(qb_ready, b + 1)
                    wait(pool, kq_read, 17 * b + (p - 1 if p else 0))
                    keys = k_ring[p % 4] if p < PAGES else k_new
                    pool.tensor_tensor(kq[p % 2], keys, q_all, ALU.mult).then_inc(kq_ready, 1)
                pool.wait_ge(smax_ready, b + 1)
                pool.partition_all_reduce(small[:, 528:544], small[:, 512:528], P,
                                          bass.bass_isa.ReduceOp.max).then_inc(gmax_ready, 1)

            for b in range(B):
                score_products(b)

            def low(m, off, k_tiles):
                pool.wait_ge(wh_ready, m + 1)
                pool.wait_ge(slot_done, GLU + m - 1)
                cols = slice((off % 2) * KT * P, (off % 2) * KT * P + k_tiles * P)
                pool.tensor_tensor(w_lo[:, cols].bitcast(F32R), slot3(off % SLOTS, 0, k_tiles).rearrange("p k m -> p (k m)"),
                                   w_hi[:, cols], ALU.subtract).then_inc(wl_ready, 1)

            with pool.Fori(0, SPLIT_DOWN // 4) as i:
                for j in range(4):
                    low(4 * i + j, j, KT)
            for j in range(SPLIT_DOWN % 4):
                low(SPLIT_DOWN - SPLIT_DOWN % 4 + j, j, KT)
            with pool.Fori(0, KT // 4) as i:
                for o in range(12):
                    k0, k1 = DOWN_PARTS[o % 3]
                    low(12 * i + SPLIT_DOWN + o, SPLIT_DOWN + o, k1 - k0)

        @block.tensor
        def _(pe):
            def transpose(dst, src):
                k = src.shape[0]
                return pe.transpose(dst, src, ident[0:k, 0:k])

            pe.wait_ge(const_ready, 7)
            pe.wait_ge(xs_in, 32)
            for k in range(KT):
                wait(pe, tr_used, k - 3)
                for c in range(3):
                    last = transpose(bank[k % 4][:, c * P:(c + 1) * P], x_rows[:, c, k * P:(k + 1) * P])
                last.then_inc(tr, 1)
            pe.wait_ge(par_in, 12 * 16)
            pe.wait_ge(tr_used, 13)
            for w in range(4):
                last = transpose(bank[0][:, w * 2 * FT:(w + 1) * 2 * FT], par_rows[0:2 * FT, w * P:(w + 1) * P])
            last.then_inc(tr, 1)
            pe.wait_ge(tr_used, 14)
            for w in range(4):
                last = transpose(bank[1][:, w * KT:(w + 1) * KT], ln_rows[0:KT, w * P:(w + 1) * P])
            last.then_inc(tr, 1)
            pe.wait_ge(st_in, 16)
            for g in range(3):
                pe.wait_ge(tr_used, 15 + g)
                for f in range(32 * g, min(32 * g + 32, 2 * FT)):
                    last = transpose(bank[(18 + g) % 4][:, (f % 32) * 16:(f % 32) * 16 + 16],
                                     st_rows[:, f * P:(f + 1) * P])
                last.then_inc(tr, 1)
            pe.wait_ge(tab_in, 32)
            rel = small[0:NB + 1, 32:32 + H]
            pe.wait_ge(tr_used, 18)
            pe.matmul(bank[1][0:H, 0:384], rel, mm[0:NB + 1, OH_TOEP:OH_TOEP + 384], start=True, stop=True).then_inc(tr, 1)
            pe.wait_ge(tr_used, 19)
            for p in range(PAGES):
                last = pe.matmul(bank[2][:, p * H:(p + 1) * H], mm[0:NB + 1, OH_PAGE + p * P:OH_PAGE + (p + 1) * P],
                                 rel, start=True, stop=True)
            last.then_inc(tr, 1)
            pe.wait_ge(tr_used, 20)
            for b in range(B):
                last = pe.matmul(bank[3][:, b * H:(b + 1) * H], mm[0:NB + 1, OH_NEW + b * P:OH_NEW + (b + 1) * P],
                                 rel, start=True, stop=True)
            last.then_inc(tr, 1)
            pe.wait_ge(x0_in, 64)
            for k in range(4):
                last = transpose(bank[4][:, k * P:(k + 1) * P], x0_rows[:, k * P:(k + 1) * P])
            last.then_inc(s5_tr, 1)
            pe.wait_ge(c_in, 64)
            for k in range(4):
                wait(pe, s5_used, k - 2)
                for t in range(2):
                    for r in range(2):
                        at = r * 1024 + (2 * k + t) * P
                        last = transpose(bank[4 + (1 + k) % 4][:, (2 * t + r) * P:(2 * t + r + 1) * P],
                                         c_rows[:, at:at + P])
                last.then_inc(s5_tr, 1)
            pe.wait_ge(s5_dve, 3)
            pe.wait_ge(s5_used, 2)
            for k in range(7):
                last = transpose(bank[5][:, k * PAIRS:(k + 1) * PAIRS], yg[0:PAIRS, (9 + k) * P:(10 + k) * P])
            last.then_inc(s5_tr, 1)
            pe.wait_ge(s5_dve, 4)
            for k in range(4):
                pe.wait_ge(s5_used, 3 + k)
                for t in range(2):
                    for r in range(2):
                        at = r * 1024 + (2 * k + t) * P
                        last = transpose(bank[4 + (6 + k) % 4][:, (2 * t + r) * P:(2 * t + r + 1) * P],
                                         kv_new[:, at:at + P])
                last.then_inc(s5_tr, 1)

            def m_tile(j, dst, arrived, rhs):
                pe.wait_ge(ring_in[j], arrived)
                k_tiles = len(rhs)
                for k in range(k_tiles):
                    last = pe.matmul(dst[:, 0:N], slot(j, k), rhs[k], start=(k == 0), stop=(k == k_tiles - 1))
                last.then_inc(slot_done, 1)

            x_tiles = [xtile(k) for k in range(KT)]
            pe.wait_ge(tr_used, 24)
            pe.wait_ge(s5_used, 10)

            def z_tile(i, j):
                wait(pe, z_read, 4 * i + j - 1)
                m_tile(j, bank[j % 2], 16 * (i + 1), x_tiles)

            def bu(t, p):
                pe.wait_ge(mst_ready, t + 1)
                pe.wait_ge(z_read, 4 * t + 4)
                wait(pe, b_read, 4 * t + p)
                rows = slice(32 * p, 32 * p + 32)
                pe.matmul(bank[6][:, 0:N], mst[rows, 0:P], u_t[rows, :], start=True, stop=True)
                pe.matmul(bank[7][:, 0:N], mst[rows, P:2 * P], u_t[rows, :], start=True, stop=True).then_inc(b_done, 1)

            def cx(t, p):
                pe.wait_ge(xs_ready, 4 * t + p + 1)
                if p == 0:
                    wait(pe, y_ready, t)
                for r in range(2):
                    last = pe.matmul(bank[3][32 * p:32 * p + 32, 0:N], mst[:, (2 + r) * P + 32 * p:(2 + r) * P + 32 * p + 32],
                                     x_st[p % 2][:, r * N:(r + 1) * N], start=(r == 0), stop=(r == 1))
                last.then_inc(c_done, 1)

            def scores(i):
                pe.wait_ge(z_read, 4 * i + 2)
                wait(pe, pv_read, i)
                wait(pe, max_ready, i)
                for j in range(2):
                    rows = slice(64 * j, 64 * j + 64)
                    pe.matmul(bank[4 + j][:, 0:256], q_t[rows, P:2 * P], k_t[rows, 0:T], start=True, stop=True)
                    last = pe.matmul(bank[4 + j][:, 256:384], q_t[rows, 0:P], k_t[rows, 0:P], start=True, stop=True)
                last.then_inc(sc_done, 1)

            def to_rows(src, done, free, count):
                wait(pe, free, count)
                transpose(bank[2][:, 0:P], src[:, 0:P])
                transpose(bank[2][:, P:2 * P], src[:, P:2 * P])
                transpose(bank[2][0:B, 2 * P:3 * P], src[:, T:N]).then_inc(done, 1)

            def prompt_pv(i):
                pe.wait_ge(pd_ready, i + 1)
                pe.wait_ge(vt_read, i + 1)
                for k, at in enumerate((256, 0, P)):
                    last = transpose(bank[2][:, k * P:(k + 1) * P], p_diff[:, at:at + P])
                last.then_inc(pdt_done, 1)
                pe.wait_ge(pdt_read, i + 1)
                pe.matmul(bank[4][:, 0:T], v_rows[:, 0:P], p_diff_t[:, 0:T], start=True, stop=False)
                pe.matmul(bank[4][:, P:T], v_rows[:, P:2 * P], p_diff_t[:, T:T + P], start=False, stop=True).then_inc(pv_done, 1)

            def head(i, s5):
                t = i - 1
                z_tile(i, 0)
                if s5:
                    bu(t, 0)
                z_tile(i, 1)
                if s5:
                    cx(t, 0)
                    bu(t, 1)
                z_tile(i, 2)
                scores(i)
                if s5:
                    cx(t, 1)
                    bu(t, 2)
                z_tile(i, 3)
                to_rows(k_t, kt_done, pdt_read, i)
                pe.wait_ge(z_read, 4 * i + 3)
                to_rows(v_t, vt_done, kt_read, i + 1)
                if s5:
                    cx(t, 2)
                    bu(t, 3)
                prompt_pv(i)
                if s5:
                    cx(t, 3)

            head(0, False)
            head(1, True)
            with pe.Fori(2, H) as i:
                head(i, True)
            for p in range(4):
                bu(HT - 1, p)
                cx(HT - 1, p)
            pe.wait_ge(xf_read, 4 * HT)
            pe.wait_ge(pdt_read, H)
            xf4 = xf[:, :].rearrange("p (r c q) -> p r c q", r=2, c=9)
            for r in range(2):
                last = transpose(bank[2][0:PAIRS, r * P:(r + 1) * P], xf4[:, r, 0, :])
            last.then_inc(xft, 1)
            pe.wait_ge(max_ready, H)
            for r in range(2):
                for h in range(2):
                    at = r * 9 * PAIRS + (1 + 4 * h) * PAIRS
                    last = transpose(bank[5][:, (2 * r + h) * P:(2 * r + h + 1) * P], xf[:, at:at + P])
            last.then_inc(xft, 1)
            pe.wait_ge(xft_read, 2)
            pe.wait_ge(y_ready, HT)
            pe.wait_ge(pv_read, H)

            def broadcast_q(b):
                pe.wait_ge(dq_ready, b + 1)
                wait(pe, qb_ready, b)
                pe.matmul(bank[2][:, :], ones[:, :], diag_q[:, 0:512], start=True, stop=True)
                pe.matmul(bank[3][:, :], ones[:, :], diag_q[:, 512:1024], start=True, stop=True).then_inc(qb_done, 1)

            def gate_part(b, r, c):
                if c == 0:
                    pe.wait_ge(z_read, L1 + 4 * b + r - 1)
                    pe.wait_ge(ring_in[r], 16 * (H + b + 1))
                for k in range(4 * c, 4 * c + 4):
                    last = pe.matmul(bank[r % 2][:, 0:N], slot(r, k), xtile(k), start=(k == 0), stop=(k == KT - 1))
                if c == 3:
                    last.then_inc(slot_done, 1)

            def denominators(b):
                pe.wait_ge(lsum_ready, b + 1)
                wait(pe, w_ready, b)
                pe.matmul(bank[7][0:16, 0:1], small[:, 544:560], ones[:, 0:1], start=True, stop=True).then_inc(lsum_done, 1)

            def page_pv(b, p):
                if p < PAGES:
                    pe.wait_ge(v_in[p % 4], 16 * (4 * b + p // 4 + 1))
                if p == 0:
                    pe.wait_ge(sexp_ready, b + 1)
                    wait(pe, o_copied, b)
                values = v_ring[p % 4] if p < PAGES else v_new
                for g in range(2):
                    last = pe.matmul(bank[4 + g][0:16, :], prob[:, p * 16:(p + 1) * 16], values[:, g * 512:(g + 1) * 512],
                                     start=(p == 0), stop=(p == PAGES))
                last.then_inc(v_used if p < PAGES else spv_done, 1)

            def combine(b):
                pe.wait_ge(o_copied, b + 1)
                pe.wait_ge(w_ready, b + 1)
                wait(pe, o_read, b)
                for h in range(H):
                    last = pe.matmul(bank[6][:, h:h + 1], o_rows[:, h * P:(h + 1) * P], small[0:16, 576 + h:577 + h],
                                     start=True, stop=True)
                last.then_inc(ocomb_done, 1)

            def decode(b, scored, summed, more=True):
                if summed:
                    denominators(b - 1)
                for r in range(4):
                    if scored and more and r == 3:
                        broadcast_q(b + 1)
                    for c in range(4):
                        if scored:
                            gate_part(b, r, c)
                        if summed:
                            page_pv(b - 1, 4 * r + c)
                if summed:
                    page_pv(b - 1, PAGES)
                    combine(b - 1)

            broadcast_q(0)
            decode(0, True, False)
            decode(1, True, True)
            with pe.Fori(2, B - 1) as b:
                decode(b, True, True)
            decode(B - 1, True, True, False)
            decode(B, False, True)

            sq = big[:, 2 * KW + 64:2 * KW + 64 + H * N]
            pe.wait_ge(sq_ready, 1)
            pe.wait_ge(o_read, B)
            for h in range(H):
                wait(pe, root_ready, h - 3)
                pe.matmul(bank[4 + h % 4][:, 0:N], v_mean_w[:, :], sq[:, h * N:(h + 1) * N],
                          start=True, stop=True).then_inc(ms_done, 1)

            y_tiles = [yg[:, k * N:(k + 1) * N] for k in range(HT)]
            pe.wait_ge(gelu_dve, 2)
            with pe.Fori(0, 2) as i:
                for j in range(4):
                    pe.wait_ge(z_read, L2 + 4 * i + j - 1)
                    m_tile(j, bank[j % 2], 16 * (2 * H + i + 1), y_tiles)

            def products(m, off, sums):
                pe.wait_ge(wh_ready, m + 1)
                for dst, k0, highs, lows, start, _, ready in sums:
                    for k in range(len(highs)):
                        if ready is not None:
                            pe.wait_ge(*ready(k))
                        pe.matmul(dst[:, 0:N], weight(w_hi, off, k0 + k), highs[k], start=start and k == 0, stop=False)
                        last = pe.matmul(dst[:, 0:N], weight(w_hi, off, k0 + k), lows[k], start=False, stop=False)
                last.then_inc(wh_used, 1)
                pe.wait_ge(wl_ready, m + 1)
                for dst, k0, highs, _, _, stop, _ in sums:
                    for k in range(len(highs)):
                        last = pe.matmul(dst[:, 0:N], weight(w_lo, off, k0 + k), highs[k], start=False,
                                         stop=stop and k == len(highs) - 1)
                last.then_inc(slot_done, 1)

            def tiles(t, k0, k1):
                return [rounded(t, k) for k in range(k0, k1)]

            branches = [(tiles(a_hi, 0, HT), tiles(a_lo, 0, HT)), (tiles(s_hi, 0, HT), tiles(s_lo, 0, HT))]
            pe.wait_ge(z_read, GLU)
            pe.wait_ge(att_ready, 1)
            pe.wait_ge(ssm_ready, HT)

            def proj(i):
                for j in range(4):
                    wait(pe, zv_read, 4 * i + j - 1)
                    products(4 * i + j, j, [(bank[2 * s + j % 2], s * HT, *branches[s], True, True, None) for s in range(2)])

            proj(0)
            with pe.Fori(1, 4) as i:
                proj(i)

            def mean_tile(n):
                return pe.matmul(bank[6][:, 0:N], mean_w[:, :], xtile(n), start=(n == 0), stop=(n == KT - 1))

            m_parts = tiles(m_hi, 0, KT), tiles(m_lo, 0, KT)
            for n in range(KT):
                pe.wait_ge(zv_read, KT + n - 1)
                products(KT + n, n, [(bank[n % 2], 0, *m_parts, True, True,
                                      (lambda k: (merged_ready, k + 1)) if n == 0 else None)])
                if n:
                    pe.wait_ge(zv_read, KT + n)
                    mean_tile(n - 1)
            pe.wait_ge(zv_read, 2 * KT)
            mean_tile(KT - 1).then_inc(mean_done, 1)

            def variance(ln):
                for n in range(KT):
                    if n % 4 == 0:
                        pe.wait_ge(csq_ready, 4 * ln + n // 4 + 1)
                    last = pe.matmul(bank[7][:, 0:N], mean_w[:, :], big[:, n * N:(n + 1) * N], start=(n == 0),
                                     stop=(n == KT - 1))
                last.then_inc(var_done, 1)

            variance(0)
            h_parts = tiles(h_hi, 0, KT), tiles(h_lo, 0, KT)

            def up_rows_out(n, pairs):
                pe.wait_ge(tap0, 4 * n + 2 * pairs)
                wait(pe, upt_read, n)
                for t in range(2 * pairs):
                    last = transpose(bank[4][0:10, t * P:(t + 1) * P], up10[:, t * 10:(t + 1) * 10])
                last.then_inc(upt_done, 1)

            def up(n, pairs, first=False):
                for t in range(2 * pairs):
                    pe.wait_ge(zv_read, 2 * KT + (0 if first else 4 * (n - 1) + t + 1))
                    products(4 * n + SPLIT_UP + t, t, [(bank[t], 0, *h_parts, True, True,
                                                        (lambda k: (h_ready, k + 1)) if first and t == 0 else None)])
                    if t == 0 and not first:
                        up_rows_out(n - 1, 2)

            up(0, 2, True)
            with pe.Fori(1, FT // 2) as n:
                up(n, 2)
            up(FT // 2, 1)

            down_base = 2 * KT + 2 * FT

            for n in range(KT):
                pe.wait_ge(zv_read, down_base + max(0, n - 1))
                for part, (k0, k1) in enumerate(DOWN_PARTS):
                    m = SPLIT_DOWN + 3 * n + part
                    products(m, m, [(bank[n % 2], 0, tiles(hid_hi, k0, k1), tiles(hid_lo, k0, k1), part == 0, part == 2,
                                     (lambda k: (hid_ready, k0 + k + 1)) if n == 0 else None)])
                    if n == 0 and part == 0:
                        up_rows_out(FT // 2, 1)
                if n:
                    pe.wait_ge(zv_read, down_base + n)
                    mean_tile(n - 1)
            pe.wait_ge(zv_read, down_base + KT)
            mean_tile(KT - 1).then_inc(mean_done, 1)
            variance(1)
            for c in range(3):
                for g in range(4):
                    n = 4 * c + g
                    wait(pe, yt_read, n - 3)
                    for k in range(4):
                        if c == 0:
                            pe.wait_ge(h_ready, KT + 4 * g + k + 1)
                        tile = xtile(4 * g + k)[:, c * P:min(N, (c + 1) * P)]
                        last = transpose(bank[n % 4][0:tile.shape[1], k * P:(k + 1) * P], tile)
                    last.then_inc(yt_done, 1)

        @block.scalar
        def _(act):
            def copy(dst, src, scale=1.0):
                return act.activation(dst, src, ACT.Copy, scale=scale)

            def row(k):
                return yg[0:PAIRS, k * P:(k + 1) * P]

            act.wait_ge(rows_in, 48)
            act.wait_ge(const_ready, 7)
            act.activation(small[0:PAIRS, 2:4], small[0:PAIRS, 0:2], ACT.Exp).then_inc(s5_act, 1)
            act.wait_ge(s5_dve, 1)
            act.activation(row(9), row(2), ACT.Exp).then_inc(s5_act, 1)
            act.wait_ge(s5_dve, 2)
            act.activation(row(6), row(10), ACT.Sin, scale=TWO_PI_DOWN).then_inc(s5_act, 1)
            act.activation(row(7), row(5), ACT.Sin, scale=-TWO_PI_DOWN, bias=small[0:PAIRS, 4:5]).then_inc(s5_act, 1)
            for k in range(KT):
                act.wait_ge(tr, k + 1)
                copy(xtile(k), bank[k % 4][:, 0:N]).then_inc(tr_used, 1)
            for n, (dst, rows, cols) in enumerate((
                    (conv_par[:, :], P, 8 * FT), (ln_par[:, :], P, 4 * KT), (conv_state[:, 0:512], P, 512),
                    (conv_state[:, 512:1024], P, 512), (conv_state[:, 1024:2 * FT * 16], P, 2 * FT * 16 - 1024),
                    (toep_rows[0:H, :], H, 384), (bias_pg[:, :], P, PAGES * H), (bias_nw[:, :], P, B * H))):
                act.wait_ge(tr, KT + n + 1)
                copy(dst, bank[n % 4][0:rows, 0:cols]).then_inc(tr_used, 1)
            act.wait_ge(par_in, 12 * 16)
            act.wait_ge(s5_dve, 6)
            act.activation(small[:, 28:30], small[:, 26:28], ACT.Exp).then_inc(lam_exp, 1)
            act.wait_ge(s5_dve, 7)
            for r, src in enumerate((att[:, 1024:2048], att[:, 0:1024])):
                if r == 0:
                    act.activation(ang[:, 0:1024], src, ACT.Sin, scale=-TWO_PI_DOWN, bias=small[:, 4:5]).then_inc(s5_act, 1)
                else:
                    act.activation(ang[:, 1024:2048], src, ACT.Sin, scale=TWO_PI_DOWN).then_inc(s5_act, 1)
            act.wait_ge(kv_zero, 1)

            xf4 = xf[:, :].rearrange("p (r c q) -> p r c q", r=2, c=9)
            q_s3 = q_s[:, :].rearrange("p (h b) -> p h b", h=H)

            def final_states(t, p):
                act.wait_ge(xs_ready, 4 * t + p + 1)
                copy(xf4[:, :, :, bass.ds(4 * t + p, 1)].rearrange("p r c o -> p r (c o)"),
                     x_st[p % 2].rearrange("p (r n) -> p r n", r=2)[:, :, T - 1:N]).then_inc(xf_read, 1)

            def exps(i):
                act.wait_ge(max_ready, i + 1)
                wait(act, pd_ready, i)
                for blk, cols in enumerate((slice(0, 256), slice(256, 384))):
                    for j in range(2):
                        k = 2 * blk + j
                        src = s_sb[:, 384 * j + cols.start:384 * j + cols.stop]
                        dst = p_sb[:, 384 * j + cols.start:384 * j + cols.stop]
                        last = act.activation(dst, src, ACT.Exp, bias=small[:, 420 + k:421 + k],
                                              accum_out=small[:, 424 + k:425 + k])
                last.then_inc(exp_done, 1)

            def head(i, s5):
                t = i - 1
                act.wait_ge(slot_done, 4 * i + 1)
                wait(act, sc_done, i)
                copy(q_t, bank[0][:, 0:N])
                copy(q_s3[:, bass.ds(i, 1), :].rearrange("p o b -> p (o b)"), bank[0][:, T:N]).then_inc(z_read, 1)
                act.wait_ge(slot_done, 4 * i + 2)
                wait(act, kt_done, i)
                copy(k_t, bank[1][:, 0:N]).then_inc(z_read, 1)
                if s5:
                    final_states(t, 0)
                act.wait_ge(slot_done, 4 * i + 3)
                wait(act, vt_done, i)
                copy(v_t, bank[0][:, 0:N]).then_inc(z_read, 1)
                if s5:
                    final_states(t, 1)
                act.wait_ge(kt_done, i + 1)
                wait(act, kv_stored, 32 * i)
                copy(k_rows, bank[2][:, 0:256])
                copy(k_new[0:B, bass.ds(i * P, P)], bank[2][0:B, 256:384]).then_inc(kt_read, 1)
                act.wait_ge(vt_done, i + 1)
                wait(act, pv_done, i)
                copy(v_rows, bank[2][:, 0:256])
                copy(v_new[0:B, bass.ds(i * P, P)], bank[2][0:B, 256:384]).then_inc(vt_read, 1)
                exps(i)
                if s5:
                    final_states(t, 2)
                act.wait_ge(slot_done, 4 * i + 4)
                wait(act, b_done, 4 * i)
                copy(u_t, bank[1][:, 0:N])
                copy(u_all[:, bass.ds(i * N, N)], bank[1][:, 0:N]).then_inc(z_read, 1)
                act.wait_ge(pdt_done, i + 1)
                copy(p_diff_t, bank[2][:, 0:384]).then_inc(pdt_read, 1)
                act.wait_ge(pv_done, i + 1)
                copy(att[:, bass.ds(i * N, T)], bank[4][:, 0:T]).then_inc(pv_read, 1)
                if s5:
                    final_states(t, 3)

            head(0, False)
            with act.Fori(1, H) as i:
                head(i, True)
            for p in range(4):
                final_states(HT - 1, p)
            act.wait_ge(xft, 1)
            copy(par_rows[0:PAIRS, 0:2 * P], bank[2][0:PAIRS, 0:2 * P]).then_inc(xft_read, 1)
            act.wait_ge(xft, 2)
            copy(x0_rows[:, :], bank[5][:, :]).then_inc(xft_read, 1)
            gelu_t = mm[:, H * N:2 * H * N]
            act.wait_ge(y_ready, HT)
            act.wait_ge(mst_ready, HT)
            act.activation(gelu_t, yg[:, :], ACT.Square).then_inc(gelu_act, 1)
            act.wait_ge(gelu_dve, 1)
            act.activation(gelu_t, gelu_t, ACT.Tanh, scale=0.7978845608028654).then_inc(gelu_act, 1)

            def query(b):
                act.wait_ge(qb_done, b + 1)
                wait(act, kq_ready, 17 * b)
                copy(q_all[:, 0:512], bank[2][:, :], HD ** -0.5)
                copy(q_all[:, 512:1024], bank[3][:, :], HD ** -0.5).then_inc(qb_ready, 1)

            def copy_sums(b):
                act.wait_ge(spv_done, b + 1)
                wait(act, ocomb_done, b)
                copy(o_rows[:, 0:512], bank[4][0:16, :])
                copy(o_rows[:, 512:1024], bank[5][0:16, :]).then_inc(o_copied, 1)

            def decode(b, summed=True, more=True):
                if not summed:
                    act.wait_ge(kv_stored, 32 * H)
                for r in range(4):
                    if r == 3 and more:
                        query(b + 1)
                    act.wait_ge(slot_done, L1 + 4 * b + r + 1)
                    act.activation(gate[:, bass.ds((4 * b + r) * N, N)], bank[r % 2][:, 0:N], ACT.Tanh,
                                   scale=0.5).then_inc(z_read, 1)
                if summed:
                    copy_sums(b - 1)
                act.wait_ge(ssub_ready, b + 1)
                act.activation(prob, score, ACT.Exp).then_inc(sexp_ready, 1)

            query(0)
            decode(0, False)
            with act.Fori(1, B - 1) as b:
                decode(b)
            decode(B - 1, True, False)
            copy_sums(B - 1)

            sq = big[:, 2 * KW + 64:2 * KW + 64 + H * N]
            act.wait_ge(o_read, B)
            act.activation(sq, att[:, :], ACT.Square).then_inc(sq_ready, 1)
            for h in range(H):
                act.wait_ge(ms_done, h + 1)
                act.activation(sq[:, h * N:(h + 1) * N], bank[4 + h % 4][:, 0:N], ACT.Sqrt,
                               bias=small[:, 5:6]).then_inc(root_ready, 1)

            def high(g, off, branch=False, k_tiles=KT):
                g, j = g + off // SLOTS, off % SLOTS
                base = 16 * (2 * H + 2)
                act.wait_ge(ring_in[j], (g + 1) * 32 + base if branch else (g + 1) * 16 + base + 16 * 4)
                wait(act, wh_used, 4 * g + j - 1)
                wait(act, wl_ready, 4 * g + j - 1)
                act.activation(w_hi[:, (j % 2) * KT * P:(j % 2) * KT * P + k_tiles * P].bitcast(F32R),
                               slot3(j, 0, k_tiles).rearrange("p k m -> p (k m)"), ACT.Copy).then_inc(wh_ready, 1)

            for j in range(HT):
                act.wait_ge(slot_done, L2 + j + 1)
                wait(act, ssm_ready, j - 1)
                act.activation(big[:, 4352 + (j % 2) * N:4352 + (j % 2 + 1) * N], bank[j % 2][:, 0:N], ACT.Tanh,
                               scale=0.25).then_inc(z_read, 1)
                if j >= HT - 2:
                    high(0, j - HT + 2, True)

            def norm(ln):
                for g in range(4):
                    act.wait_ge(cent_ready, 4 * ln + g + 1)
                    act.activation(big[:, 4 * g * N:4 * (g + 1) * N], xt[:, 4 * g * N:4 * (g + 1) * N],
                                   ACT.Square).then_inc(csq_ready, 1)
                act.wait_ge(var_done, ln + 1)
                act.activation(std_sb, bank[7][:, 0:N], ACT.Sqrt, bias=small[:, 6:7]).then_inc(std_ready, 1)
                for k in range(KT):
                    act.wait_ge(norm_ready, 4 * ln + k // 4 + 1)
                    if ln == 0:
                        wait(act, h_ready, k - 3)
                    act.activation(xtile(k) if ln else h_tmp[k % 4], xtile(k), ACT.Identity,
                                   scale=ln_par[:, 32 * ln + k:32 * ln + k + 1],
                                   bias=ln_par[:, 32 * ln + 16 + k:32 * ln + 17 + k]).then_inc(h_ready if ln else hn_ready, 1)

            for j in range(2, 4):
                high(0, j, True)
            with act.Fori(1, 4) as g:
                for j in range(4):
                    high(g, j, True)
            with act.Fori(4, 8) as g:
                for j in range(4):
                    high(g, j)
            for j in range(2):
                high(8, j)
            norm(0)

            def par(w, tile):
                return conv_par[:, bass.ds(w * 2 * FT + tile, 1)]

            def up_rows_copy(n, pairs):
                act.wait_ge(upt_done, n + 1)
                wait(act, upr_stored, 64 * n)
                copy(up_rows[:, 0:2 * pairs * P], bank[4][0:10, 0:2 * pairs * P]).then_inc(upt_read, 1)

            def up(n, pairs, first=False):
                for q in range(pairs):
                    wait(act, hid_ready, 2 * (n - 1) + q + 1)
                    for v in range(2):
                        t = 2 * q + v
                        tile = 2 * n + q + v * FT
                        high(n + 8, t + 2)
                        act.wait_ge(slot_done, OUT + 4 * n + t + 1)
                        act.activation(acc[t], bank[t][:, 0:N], ACT.Identity, scale=par(2, tile), bias=par(3, tile))
                        if t == 0:
                            wait(act, upt_done, n)
                        copy(up10[:, t * 10:(t + 1) * 10], bank[t][:, T - 2:N]).then_inc(tap0, 1)
                    if q == 0 and not first:
                        up_rows_copy(n - 1, 2)
                    act.wait_ge(tap_done, 4 * n + 2 * q + 1)
                    act.activation(th[q], acc[2 * q], ACT.Tanh, scale=0.5).then_inc(th_ready, 1)

            up(0, 2, True)
            with act.Fori(1, FT // 2) as n:
                up(n, 2)
            up(FT // 2, 1)
            up_rows_copy(FT // 2, 1)
            first = SPLIT_DOWN // 4

            def high_down(i, o):
                k0, k1 = DOWN_PARTS[o % 3]
                high(3 * i + first, SPLIT_DOWN % 4 + o, k_tiles=k1 - k0)

            with act.Fori(0, KT // 4 - 1) as i:
                for o in range(2, 14):
                    high_down(i, o)
            for o in range(2, 12):
                high_down(KT // 4 - 1, o)
            norm(1)

        @block.vector
        def _(dve):
            ch = Chain(dve, dve_c)

            def row(k):
                return yg[0:PAIRS, k * P:(k + 1) * P]

            def link(ins):
                ch.did(ins)
                ch.wait()

            a_re, a_im, t_re, t_im = row(0), row(1), row(2), row(3)
            turns, turns_abs, sin, cos = row(10), row(5), row(6), row(7)
            tmp, inv = row(8), row(4)
            mag, ab_re, ab_im, f_re, f_im, neg_im = row(9), row(11), row(12), row(13), row(14), row(15)
            dve.wait_ge(rows_in, 48)
            dve.wait_ge(s5_act, 1)
            dt = small[0:PAIRS, 2:4].unsqueeze(2).to_broadcast([PAIRS, 2, S])

            def g2(x):
                return x.rearrange("q (g s) -> q g s", g=2)

            ch.did(dve.tensor_tensor(g2(t_im), g2(a_im), dt, ALU.mult))
            dve.tensor_tensor(g2(t_re), g2(a_re), dt, ALU.mult).then_inc(s5_dve, 1)
            ch.wait()
            link(dve.tensor_scalar(t_im, t_im, 1.0 / (2 * PI), None, ALU.mult))
            whole = mm[0:PAIRS, KT * N - P:KT * N].bitcast(I32)
            link(dve.tensor_copy(whole, t_im))
            link(dve.tensor_copy(tmp, whole))
            link(dve.tensor_tensor(turns, t_im, tmp, ALU.subtract))
            dve.scalar_tensor_tensor(turns_abs, turns, -1.0, turns, ALU.mult, ALU.max).then_inc(s5_dve, 1)
            ch.did(dve.tensor_tensor(inv, a_re, a_re, ALU.mult))
            link(dve.tensor_tensor(tmp, a_im, a_im, ALU.mult))
            link(dve.tensor_tensor(inv, inv, tmp, ALU.add))
            link(dve.reciprocal(inv, inv))
            dve.wait_ge(s5_act, 4)
            ch.did(dve.tensor_tensor(ab_re, mag, cos, ALU.mult))
            link(dve.tensor_tensor(ab_im, mag, sin, ALU.mult))
            link(dve.tensor_scalar(t_re, ab_re, -1.0, None, ALU.add))
            ch.did(dve.tensor_tensor(f_re, t_re, a_re, ALU.mult))
            ch.did(dve.tensor_tensor(tmp, ab_im, a_im, ALU.mult))
            ch.did(dve.tensor_tensor(f_im, ab_im, a_re, ALU.mult))
            link(dve.tensor_tensor(t_im, t_re, a_im, ALU.mult))
            ch.did(dve.tensor_tensor(f_re, f_re, tmp, ALU.add))
            link(dve.tensor_tensor(f_im, f_im, t_im, ALU.subtract))
            ch.did(dve.tensor_scalar(neg_im, ab_im, -1.0, None, ALU.mult))
            ch.did(dve.tensor_tensor(f_re, f_re, inv, ALU.mult))
            link(dve.tensor_tensor(f_im, f_im, inv, ALU.mult))
            dve.tensor_copy(small[0:PAIRS, 7:8], small[0:PAIRS, 4:5]).then_inc(s5_dve, 1)

            dve.wait_ge(s5_tr, 1)
            dve.tensor_copy(x0[:, :], bank[4][:, :]).then_inc(s5_used, 1)
            dve.wait_ge(mt_zero, 1)
            for k in range(4):
                dve.wait_ge(s5_tr, 2 + k)
                src = bank[4 + (1 + k) % 4][:, :].rearrange("p (t r q g c) -> p t r q g c", t=2, r=2, q=4, g=2)
                dst = MT[:, 2 * k:2 * k + 2, 256:512].rearrange("p t (r q g c) -> p t r q g c", r=2, q=4, g=2)
                for t in range(2):
                    for g in range(2):
                        rows = slice(64 * g, 64 * g + 64)
                        for r in range(2):
                            last = dve.tensor_scalar(dst[rows, t, r, :, g, :], src[rows, t, r, :, g, :],
                                                     1.0 - 2.0 * r, None, ALU.mult)
                last.then_inc(s5_used, 1)
            dve.wait_ge(s5_tr, 6)
            dve.tensor_copy(scan_par[:, :], bank[5][:, 0:7 * PAIRS]).then_inc(s5_used, 1)
            dve.wait_ge(s5_used, 6)
            dve.wait_ge(b_in, 32)
            dve.wait_ge(bpad_zero, 1)
            b_re, b_im, w0, w1 = (att[:, k * 512:(k + 1) * 512].rearrange("p (q c) -> p q c", c=C) for k in range(4))
            fr, fi = (scan_par[:, k * PAIRS:(k + 1) * PAIRS].unsqueeze(2).to_broadcast([P, PAIRS, C]) for k in (4, 5))
            for r, ((x, y), op) in enumerate((((fr, fi), ALU.subtract), ((fi, fr), ALU.add))):
                ch.did(dve.tensor_tensor(w0, b_re, x, ALU.mult))
                link(dve.tensor_tensor(w1, b_im, y, ALU.mult))
                for g in range(2):
                    rows = slice(64 * g, 64 * g + 64)
                    dst = kv_new[rows, r * 1024:(r + 1) * 1024].rearrange("p (q c) -> p q c", c=2 * C)[:, :, g * C:(g + 1) * C]
                    last = dve.tensor_tensor(dst, w0[rows], w1[rows], op)
                    if r == 1 and g == 1:
                        last.then_inc(s5_dve, 1)
                    else:
                        ch.did(last)
                ch.wait()
            for k in range(4):
                dve.wait_ge(s5_tr, 7 + k)
                dve.tensor_copy(MT[:, 2 * k:2 * k + 2, 0:256],
                                bank[4 + (6 + k) % 4][:, :].rearrange("p (t c) -> p t c", t=2)).then_inc(s5_used, 1)
            dve.wait_ge(par_in, 12 * 16)
            lam = small[:, 64:64 + 4 * HD].rearrange("p (m k d) -> p m k d", m=2, k=2)
            prod = small[:, 352:480].rearrange("p (m d) -> p m d", m=2)
            link(dve.tensor_tensor(prod, lam[:, :, 0, :], lam[:, :, 1, :], ALU.mult))
            dve.tensor_reduce(small[:, 26:28], prod, AX.X, ALU.add).then_inc(s5_dve, 2)
            dve.wait_ge(lam_exp, 1)
            link(dve.tensor_tensor(small[:, 25:26], small[:, 29:30], small[:, 28:29], ALU.subtract))
            link(dve.tensor_scalar(small[:, 25:26], small[:, 25:26], -LAM_INIT, None, ALU.add))
            ch.did(dve.tensor_scalar(small[:, 30:31], small[:, 24:25], 1.0 - LAM_INIT, None, ALU.mult))
            dve.wait_ge(mult_ready, 1)
            dve.wait_ge(s5_dve, 6)
            v, f = att[:, 0:1024], att[:, 1024:2048]
            turn_q = scan_par[:, PAIRS:2 * PAIRS].unsqueeze(2).to_broadcast([P, PAIRS, 32])
            times = small[:, 320:352].unsqueeze(1).to_broadcast([P, PAIRS, 32])
            link(dve.tensor_tensor(v.rearrange("p (q e) -> p q e", e=32), turn_q, times, ALU.mult))
            link(dve.tensor_copy(c_rows[:, 0:1024].bitcast(I32), v))
            link(dve.tensor_copy(f, c_rows[:, 0:1024].bitcast(I32)))
            link(dve.tensor_tensor(v, v, f, ALU.subtract))
            dve.scalar_tensor_tensor(f, v, -1.0, v, ALU.mult, ALU.max).then_inc(s5_dve, 1)

            dve.wait_ge(toep_in, 32)
            bias3 = bias.rearrange("p (h x) -> p h x", h=H)
            x04 = x0[:, :].rearrange("p (r b q) -> p r b q", r=2, b=B)

            def states(t, p):
                n = 4 * t + p
                q = bass.ds(n, 1)

                def par(k):
                    return scan_par[:, bass.ds(k * PAIRS + n, 1)]

                def old(r):
                    return x04[:, r, :, q].rearrange("p b o -> p (b o)")

                cos, sin = tab[p % 2][:, 0:256], tab[p % 2][:, 256:512]
                re, im = bank[6], bank[7]
                x_re, x_im = x_st[p % 2][:, 0:N], x_st[p % 2][:, N:2 * N]
                s_re, s_im = small[:, 400:408], small[:, 408:416]
                dve.wait_ge(tab_ready, n + 1)
                dve.wait_ge(b_done, n + 1)
                wait(dve, xs_ready, n)
                ch.did(dve.tensor_tensor(rot[0], re[:, 0:T], cos, ALU.mult))
                n1 = ch.did(dve.tensor_tensor(rot[1], im[:, 0:T], sin, ALU.mult))
                ch.did(dve.tensor_tensor(rot[2], im[:, 0:T], cos, ALU.mult))
                n2 = ch.did(dve.tensor_tensor(rot[3], re[:, 0:T], sin, ALU.mult))
                ch.did(dve.scalar_tensor_tensor(s_re, old(0), par(2), re[:, T:N], ALU.mult, ALU.add))
                dve.scalar_tensor_tensor(s_im, old(1), par(2), im[:, T:N], ALU.mult, ALU.add).then_inc(b_read, 1)
                ch.wait(n1)
                n1 = ch.did(dve.tensor_tensor(z_re, rot[0], rot[1], ALU.add))
                ch.wait(n2)
                n2 = ch.did(dve.tensor_tensor(z_im, rot[2], rot[3], ALU.subtract))
                decay = par(0).to_broadcast([P, T])
                ch.wait(n1)
                n1 = ch.did(dve.tensor_tensor_scan(y_re, decay, z_re, 0.0, ALU.mult, ALU.add))
                ch.wait(n2)
                n2 = ch.did(dve.tensor_tensor_scan(y_im, decay, z_im, 0.0, ALU.mult, ALU.add))
                wait(dve, c_done, n - 1)
                wait(dve, xf_read, n - 1)
                dve.wait_ge(b_read, n + 1)
                ch.did(dve.scalar_tensor_tensor(x_re[:, T:N], old(1), par(6), s_re, ALU.mult, ALU.add))
                ch.did(dve.scalar_tensor_tensor(x_im[:, T:N], old(0), par(3), s_im, ALU.mult, ALU.add))
                ch.wait(n1)
                ch.did(dve.tensor_tensor(rot[0], y_re, cos, ALU.mult))
                ch.did(dve.tensor_tensor(rot[2], y_re, sin, ALU.mult))
                ch.wait(n2)
                n1 = ch.did(dve.tensor_tensor(rot[1], y_im, sin, ALU.mult))
                n2 = ch.did(dve.tensor_tensor(rot[3], y_im, cos, ALU.mult))
                ch.wait(n1)
                ch.did(dve.tensor_tensor(x_re[:, 0:T], rot[0], rot[1], ALU.subtract))
                ch.wait(n2)
                dve.tensor_tensor(x_im[:, 0:T], rot[2], rot[3], ALU.add).then_inc(xs_ready, 1)

            def maxima(i):
                dve.wait_ge(sc_done, i + 1)
                wait(dve, exp_done, i)
                for j in range(2):
                    n1 = ch.did(dve.scalar_tensor_tensor(
                        s_sb[:, 384 * j:384 * (j + 1)], bank[4 + j][:, 0:384], HD ** -0.5,
                        bias3[:, bass.ds(i, 1), :].rearrange("p o x -> p (o x)"), ALU.mult, ALU.add))
                ch.wait(n1)
                s3 = s_sb.rearrange("p (j x) -> p j x", j=2)
                ch.did(dve.tensor_reduce(small[:, 420:422], s3[:, :, 0:256], AX.X, ALU.max, negate=True))
                dve.tensor_reduce(small[:, 422:424], s3[:, :, 256:384], AX.X, ALU.max, negate=True).then_inc(max_ready, 1)

            def differences(i):
                dve.wait_ge(exp_done, i + 1)
                wait(dve, pdt_done, i)
                link(dve.reciprocal(small[:, 428:432], small[:, 424:428]))
                second = small[:, 428:432].rearrange("p (k j) -> p k j", j=2)[:, :, 1]
                n1 = ch.did(dve.tensor_scalar(second, second, small[:, 25:26], None, ALU.mult))
                ch.did(dve.tensor_scalar(p_diff[:, 0:256], p_sb[:, 0:256], small[:, 428:429], None, ALU.mult))
                n2 = ch.did(dve.tensor_scalar(p_diff[:, 256:384], p_sb[:, 256:384], small[:, 430:431], None, ALU.mult))
                ch.wait(n2)
                ch.did(dve.scalar_tensor_tensor(p_diff[:, 0:256], p_sb[:, 384:640], small[:, 429:430],
                                                p_diff[:, 0:256], ALU.mult, ALU.add))
                dve.scalar_tensor_tensor(p_diff[:, 256:384], p_sb[:, 640:768], small[:, 431:432],
                                         p_diff[:, 256:384], ALU.mult, ALU.add).then_inc(pd_ready, 1)

            def y_out(t):
                dve.wait_ge(c_done, 4 * t + 4)
                dve.scalar_tensor_tensor(yg[:, bass.ds(t * N, N)], u_all[:, bass.ds(t * N, N)],
                                         small[:, bass.ds(16 + t, 1)], bank[3][:, 0:N], ALU.mult, ALU.add
                                         ).then_inc(y_ready, 1)

            def head(i):
                states(i - 1, 0)
                states(i - 1, 1)
                maxima(i)
                states(i - 1, 2)
                differences(i)
                states(i - 1, 3)
                y_out(i - 1)

            maxima(0)
            differences(0)
            head(1)
            with dve.Fori(2, H) as i:
                ch.enter(i, 2, 4 * 16 + 3 + 5)
                head(i)
            ch.leave(H - 2)
            for p in range(4):
                states(HT - 1, p)
            y_out(HT - 1)

            gelu_t = mm[:, H * N:2 * H * N]
            dve.wait_ge(gelu_act, 1)
            link(dve.tensor_scalar(gelu_t, gelu_t, 0.044715, 1.0, ALU.mult, ALU.add))
            dve.tensor_tensor(gelu_t, gelu_t, yg[:, :], ALU.mult).then_inc(gelu_dve, 1)

            def diag(b):
                wait(dve, qb_done, b)
                query = q_s[:, :].rearrange("p (h b) -> p h b", h=H)[:, :, bass.ds(b, 1)].to_broadcast([P, H, P])
                dve.tensor_tensor(diag_q.rearrange("p (h m) -> p h m", h=H),
                                  ident[:, :].unsqueeze(1).to_broadcast([P, H, P]), query, ALU.mult).then_inc(dq_ready, 1)

            def weights(b):
                dve.wait_ge(lsum_done, b + 1)
                wait(dve, ocomb_done, b)
                link(dve.reciprocal(small[0:16, 560:561], bank[7][0:16, 0:1]))
                dve.tensor_scalar(small[0:16, 576:584], small[0:16, 584:592], small[0:16, 560:561], None,
                                  ALU.mult).then_inc(w_ready, 1)

            def sample_out(b):
                dve.wait_ge(ocomb_done, b + 1)
                dst = att[:, :].rearrange("p (h n) -> p h n", h=H)[:, :, bass.ds(T + b, 1)].rearrange("p h o -> p (h o)")
                dve.tensor_copy(dst, bank[6][:, 0:H]).then_inc(o_read, 1)

            def decode(b, summed, more=True):
                if summed:
                    weights(b - 1)
                if more:
                    diag(b + 1)
                for p in range(PAGES + 1):
                    dve.wait_ge(kq_ready, 17 * b + p + 1)
                    dve.tensor_reduce(score[:, p * 16:(p + 1) * 16], kq[p % 2].rearrange("p (m d) -> p m d", d=HD),
                                      AX.X, ALU.add).then_inc(kq_read, 1)
                dve.wait_ge(kq_read, 17 * b + 17)
                s4 = score.rearrange("p (g h j) -> p g h j", h=H, j=2)
                for j in range(2):
                    ch.did(dve.tensor_tensor(s4[:, 0:PAGES, :, j], s4[:, 0:PAGES, :, j],
                                             bias_pg[:, :].rearrange("p (g h) -> p g h", h=H), ALU.add))
                    ch.did(dve.tensor_tensor(s4[:, PAGES, :, j], s4[:, PAGES, :, j],
                                             bias_nw[:, bass.ds(b * H, H)], ALU.add))
                ch.wait()
                dve.tensor_reduce(small[:, 512:528], score.rearrange("p (g c) -> p c g", c=16), AX.X,
                                  ALU.max).then_inc(smax_ready, 1)
                dve.wait_ge(gmax_ready, b + 1)
                s3 = score.rearrange("p (g c) -> p g c", c=16)
                dve.tensor_tensor(s3, s3, small[:, 528:544].unsqueeze(1).to_broadcast([P, PAGES + 1, 16]),
                                  ALU.subtract).then_inc(ssub_ready, 1)
                if summed:
                    sample_out(b - 1)
                dve.wait_ge(sexp_ready, b + 1)
                wait(dve, lsum_done, b)
                dve.tensor_reduce(small[:, 544:560], prob.rearrange("p (g c) -> p c g", c=16), AX.X,
                                  ALU.add).then_inc(lsum_ready, 1)

            pick = ident[0:16, 0:16].rearrange("p (h j) -> p h j", j=2)
            dve.scalar_tensor_tensor(small[0:16, 584:592], pick[:, :, 1], small[0:16, 25:26], pick[:, :, 0], ALU.mult, ALU.add
                                     ).then_inc(dve_c, 1)
            ch.n += 1
            dve.wait_ge(mst_ready, HT)
            dve.wait_ge(z_read, L1)
            diag(0)
            decode(0, False)
            dve.wait_ge(gelu_act, 2)
            dve.scalar_tensor_tensor(yg[:, :], gelu_t, 1.0, yg[:, :], ALU.add, ALU.mult).then_inc(gelu_dve, 1)
            with dve.Fori(1, B - 1) as b:
                ch.enter(b, 1, 5)
                decode(b, True)
            ch.leave(B - 2)
            decode(B - 1, True, False)
            weights(B - 1)
            sample_out(B - 1)

            sq = big[:, 2 * KW + 64:2 * KW + 64 + H * N]
            dve.wait_ge(root_ready, H)
            link(dve.reciprocal(sq, sq))
            link(dve.scalar_tensor_tensor(att[:, :], att[:, :], small[:, 30:31], sq, ALU.mult, ALU.mult))
            link(dve.tensor_copy(a_hi[:, :].bitcast(F32R), att[:, :]))
            dve.tensor_tensor(a_lo[:, :].bitcast(F32R), att[:, :], a_hi[:, :], ALU.subtract).then_inc(att_ready, 1)
            dve.wait_ge(out_stored, 9 * 16)
            for j in range(HT):
                dve.wait_ge(z_read, L2 + j + 1)
                cols = slice(j * N, (j + 1) * N)
                product = big[:, 4352 + (j % 2) * N:4352 + (j % 2 + 1) * N]
                link(dve.scalar_tensor_tensor(product, product, 1.0, yg[:, cols], ALU.add, ALU.mult))
                link(dve.tensor_copy(s_hi[:, cols].bitcast(F32R), product))
                dve.tensor_tensor(s_lo[:, cols].bitcast(F32R), product, s_hi[:, cols], ALU.subtract).then_inc(ssm_ready, 1)

            def merge(i):
                for j in range(4):
                    n = 4 * i + j
                    one, two = (yg[:, k * 2 * N + (j % 2) * N:k * 2 * N + (j % 2 + 1) * N] for k in range(2))
                    wait(dve, merged_ready, n - 1)
                    dve.wait_ge(slot_done, GLU + n + 1)
                    n1 = ch.did(dve.scalar_tensor_tensor(one, gate[:, bass.ds(n * N, N)], 1.0, bank[j % 2][:, 0:N],
                                                         ALU.add, ALU.mult))
                    dve.scalar_tensor_tensor(two, gate[:, bass.ds((KT + n) * N, N)], 1.0, bank[2 + j % 2][:, 0:N],
                                             ALU.add, ALU.mult).then_inc(zv_read, 1)
                    ch.wait(n1)
                    dve.wait_ge(zv_read, n + 1)
                    link(dve.scalar_tensor_tensor(one, two, 0.25, one, ALU.mult, ALU.add))
                    link(dve.tensor_copy(m_hi[:, bass.ds(n * N, N)].bitcast(F32R), one))
                    dve.tensor_tensor(m_lo[:, bass.ds(n * N, N)].bitcast(F32R), one, m_hi[:, bass.ds(n * N, N)],
                                      ALU.subtract).then_inc(merged_ready, 1)

            merge(0)
            with dve.Fori(1, 4) as i:
                ch.enter(i, 1, 12)
                merge(i)
            ch.leave(3)

            def residual(n, j, count):
                dve.wait_ge(slot_done, count)
                tile = xt[:, bass.ds(n * N, N)]
                dve.scalar_tensor_tensor(tile, tile, 2 * ALPHA, bank[j % 2][:, 0:N], ALU.mult, ALU.add).then_inc(zv_read, 1)

            def norm(ln):
                dve.wait_ge(mean_done, ln + 1)
                for g in range(4):
                    c3 = x3[:, 4 * g:4 * g + 4, :]
                    dve.tensor_tensor(c3, c3, bank[6][:, 0:N].unsqueeze(1).to_broadcast([P, 4, N]),
                                      ALU.subtract).then_inc(cent_ready, 1)
                dve.wait_ge(std_ready, ln + 1)
                link(dve.reciprocal(std_sb, std_sb))
                for g in range(4):
                    c3 = x3[:, 4 * g:4 * g + 4, :]
                    dve.tensor_tensor(c3, c3, std_sb.unsqueeze(1).to_broadcast([P, 4, N]), ALU.mult).then_inc(norm_ready, 1)

            with dve.Fori(0, KT // 4) as n:
                for j in range(4):
                    residual(4 * n + j, j, PROJ + 4 * n + j + 1)
            norm(0)
            for k in range(KT):
                dve.wait_ge(hn_ready, k + 1)
                cols = slice(k * N, (k + 1) * N)
                link(dve.tensor_copy(h_hi[:, cols].bitcast(F32R), h_tmp[k % 4]))
                dve.tensor_tensor(h_lo[:, cols].bitcast(F32R), h_tmp[k % 4], h_hi[:, cols], ALU.subtract).then_inc(h_ready, 1)

            state3 = conv_state[:, :].rearrange("p (t b i) -> p t b i", b=B, i=2)

            def up(n, pairs):
                for q in range(pairs):
                    for v in range(2):
                        t = 2 * q + v
                        tile = 2 * n + q + v * FT
                        y, ps = acc[t], bank[t]

                        def par(w):
                            return conv_par[:, bass.ds(w * 2 * FT + tile, 1)]

                        def old(i):
                            return state3[:, bass.ds(tile, 1), :, i].rearrange("p o b -> p (o b)")

                        dve.wait_ge(tap0, 4 * n + t + 1)
                        n1 = ch.did(dve.scalar_tensor_tensor(y[:, 1:T], ps[:, 0:T - 1], par(1), y[:, 1:T], ALU.mult, ALU.add))
                        n2 = ch.did(dve.scalar_tensor_tensor(y[:, T:N], old(1), par(1), y[:, T:N], ALU.mult, ALU.add))
                        ch.wait(n1)
                        dve.scalar_tensor_tensor(y[:, 2:T], ps[:, 0:T - 2], par(0), y[:, 2:T], ALU.mult, ALU.add
                                                 ).then_inc(zv_read, 1)
                        ch.wait(n2)
                        dve.scalar_tensor_tensor(y[:, T:N], old(0), par(0), y[:, T:N], ALU.mult, ALU.add
                                                 ).then_inc(tap_done, 1)
                    dve.wait_ge(th_ready, 2 * n + q + 1)
                    link(dve.scalar_tensor_tensor(th[q], th[q], 1.0, acc[2 * q], ALU.add, ALU.mult))
                    dve.wait_ge(tap_done, 4 * n + 2 * q + 2)
                    hidden = bass.ds((2 * n + q) * N, N)
                    link(dve.tensor_tensor(th[q], th[q], acc[2 * q + 1], ALU.mult))
                    link(dve.tensor_copy(hid_hi[:, hidden].bitcast(F32R), th[q]))
                    dve.tensor_tensor(hid_lo[:, hidden].bitcast(F32R), th[q], hid_hi[:, hidden], ALU.subtract
                                      ).then_inc(hid_ready, 1)

            up(0, 2)
            with dve.Fori(1, FT // 2) as n:
                ch.enter(n, 1, 14)
                up(n, 2)
            ch.leave(FT // 2 - 1)
            up(FT // 2, 1)
            with dve.Fori(0, KT // 4) as n:
                ch.enter(n, 0, 4)
                for j in range(4):
                    tile = bass.ds(4 * n * N + j * N, N)
                    dve.wait_ge(slot_done, 12 * n + UP + 3 * j + 3)
                    link(dve.scalar_tensor_tensor(xt[:, tile], h_hi[:, tile], 2 * ALPHA, bank[j % 2][:, 0:N], ALU.mult, ALU.add))
                    dve.scalar_tensor_tensor(xt[:, tile], h_lo[:, tile], 2 * ALPHA, xt[:, tile], ALU.mult, ALU.add
                                             ).then_inc(zv_read, 1)
            ch.leave(KT // 4)
            norm(1)
            for c in range(3):
                rows = min(P, N - c * P)
                for g in range(4):
                    n = 4 * c + g
                    dve.wait_ge(yt_done, n + 1)
                    dve.tensor_copy(big[0:rows, c * D + g * 512:c * D + (g + 1) * 512], bank[n % 4][0:rows, :]
                                    ).then_inc(yt_read, 1)


_OUTS = [
    ("y_prompt", (T, D), (1, T, D)),
    ("y_sample", (B, D), (B, 1, D)),
    ("k_prompt", (T, KW), (1, 1, T, H, 2, HD)),
    ("v_prompt", (T, SW), (1, 1, T, H, P)),
    ("ssm_re_prompt", (PAIRS, P), (1, 1, G, S)),
    ("ssm_im_prompt", (PAIRS, P), (1, 1, G, S)),
    ("conv_prompt", (2, 2 * FF), (1, 1, 2, 2 * FF)),
    ("k_sample", (B, KW), (1, B, 1, H, 2, HD)),
    ("v_sample", (B, SW), (1, B, 1, H, P)),
    ("ssm_re_sample", (B * PAIRS, P), (1, B, G, S)),
    ("ssm_im_sample", (B * PAIRS, P), (1, B, G, S)),
    ("conv_sample", (1, B, 2, 2 * FF), (1, B, 2, 2 * FF)),
]


def kernel(**inputs):
    import concourse.bacc as _bacc
    from concourse.bass_utils import run_bass_kernel_spmd as _run

    nc = _bacc.Bacc("TRN2", target_bir_lowering=False, num_devices=1)
    arrays, args, outs = {}, {}, {}
    named = {name: np.ascontiguousarray(array) for name, array in inputs.items()}
    named["buckets"] = bucket_table()
    for name, array in named.items():
        arrays[f"in_{name}"] = array
        args[name] = nc.dram_tensor(f"in_{name}", array.shape, mybir.dt.from_np(array.dtype), kind="ExternalInput").ap()
    for name, shape, _ in _OUTS:
        outs[name] = nc.dram_tensor(f"out_{name}", shape, F32, kind="ExternalOutput").ap()
    scratch = nc.dram_tensor("toeplitz_rows", (H, P, 384), F32, kind="Internal").ap()
    build(nc, args, outs, scratch)
    r = _run(nc, [arrays], core_ids=[0])
    return tuple(np.asarray(r.results[0][f"out_{name}"]).reshape(shape) for name, _, shape in _OUTS)
```

```python
from contextlib import ExitStack

import numpy as np

import concourse.bass as bass
from concourse import mybir

ALU = mybir.AluOpType
ACT = mybir.ActivationFunctionType
AX = mybir.AxisListType
F32 = mybir.dt.float32
I32 = mybir.dt.int32
F32R = mybir.dt.float32r

P = 128
D = 2048
T = 256
B = 8
N = T + B
H = 8
HD = 64
PAGES = 16
POOL_PAGES = 160
KW = H * 2 * HD
SW = 1024
G = 64
S = 64
C = 16
PAIRS = G // 2
FF = 5504
FT = FF // P
KT = D // P
HT = SW // P
NB = 32
SLOTS = 4
DOWN_PARTS = ((0, 16), (16, 32), (32, FT))
ALPHA = 2.0 ** 0.25
EPS = 1e-5
LAM_INIT = 0.2
MASK = -1e30
PI = float(np.pi)
TWO_PI_DOWN = 6.2831845

TOEP = 383
OH_TOEP, OH_PAGE, OH_NEW = 0, 384, 384 + PAGES * P
OH_COLS = OH_NEW + B * P


def bucket_table():
    def bucket(n):
        n = np.maximum(n, 0)
        large = 16 + (np.log(np.maximum(n, 1).astype(np.float32) / np.float32(16)) / np.float32(np.log(8.0))
                      * np.float32(16)).astype(np.int32)
        return np.where(n < 16, n, np.minimum(large, NB - 1))

    table = np.zeros((NB + 1, OH_COLS), np.float32)

    def mark(cols, dist):
        row = np.where(dist < 0, NB, bucket(dist))
        table[row, cols] = 1.0

    y = np.arange(TOEP)
    mark(OH_TOEP + y, 255 - y)
    k = np.arange(PAGES * P)
    mark(OH_PAGE + k, PAGES * P - k)
    for b in range(B):
        r = np.arange(P)
        mark(OH_NEW + b * P + r, np.where(r == b, 0, -1))
    return table


def wait(eng, sem, value):
    if isinstance(value, int) and value <= 0:
        return
    eng.wait_ge(sem, value)


class Chain:

    def __init__(self, eng, sem):
        self.eng, self.sem, self.base, self.n = eng, sem, 0, 0

    def did(self, ins):
        ins.then_inc(self.sem, 1)
        self.n += 1
        return self.n

    def wait(self, n=None):
        wait(self.eng, self.sem, self.base + (self.n if n is None else n))

    def enter(self, i, first, per):
        self.outer, self.per = self.base + self.n, per
        self.base, self.n = self.outer + (i - first) * per, 0

    def leave(self, turns):
        assert self.n == self.per, (self.n, self.per)
        self.base, self.n = self.outer + turns * self.per, 0


def build(nc, a, out, scratch):
    with ExitStack() as ctx:
        def sb(name, cols, dt=F32, rows=P):
            return ctx.enter_context(nc.sbuf_tensor(name, [rows, cols], dt))

        def sem(name):
            return ctx.enter_context(nc.semaphore(name))

        w_in, w_glu, w_pa, w_ps, w_out, w_up, w_down = (
            a[name][0] for name in ("w_in", "w_glu", "w_proj_attn", "w_proj_ssm", "w_out", "w_up", "w_down"))

        ring = sb("weight_ring", SLOTS * KT * P)
        conv_state = sb("conv_state_t", 2 * FT * 2 * B)
        conv_par = sb("conv_par", 4 * 2 * FT)
        ln_par = sb("ln_par", 4 * KT)
        ident = sb("ident", P)
        ones = sb("ones", P)
        mean_w = sb("mean_w", P)
        v_mean_w = sb("v_mean_w", P)
        small = sb("small", 592)
        page_no = sb("page_numbers", B * PAGES, I32, rows=1)

        def overlay(*parts):
            with ExitStack() as stage:
                placed = [stage.enter_context(nc.sbuf_tensor(name, [P, cols], F32)) for name, cols in parts]
            return [t for t, (name, _) in zip(placed, parts) if not name.startswith("skip")]

        GATES = 2 * KT * N
        s_lo, m_hi, m_lo, a_hi, w_hi, a_lo, w_lo, s_hi = overlay(
            ("skip_x_gates", KT * N + GATES), ("ssm_lo", HT * N), ("skip1", 704), ("merged_hi", KT * N),
            ("merged_lo", KT * N), ("att_hi", HT * N), ("skip2", 888), ("weights_hi", 2 * KT * P), ("skip3", 32),
            ("att_lo", HT * N), ("skip4", HT * N), ("weights_lo", 2 * KT * P), ("ssm_hi", HT * N))
        h_hi, hid_hi, hid_lo, h_lo, late = overlay(
            ("h_hi", KT * N), ("hidden_hi", FT * N), ("hidden_lo", FT * N), ("skip5", 4136), ("h_lo", KT * N),
            ("skip_weights_lo", 2 * KT * P), ("ffn_scratch", 2144))
        xt = sb("x_t", KT * N)
        gd = sb("gates", 11264)
        big = sb("big", FT * N)
        mm = sb("matrices", KT * N)
        att = sb("att", H * N)
        yg = sb("ssm_y", HT * N)
        c_rows = sb("c_rows", 2 * HT * P)
        kv_new = sb("kv_new", 2 * KW)
        par_rows = sb("parameter_rows", 4 * P)
        x0_rows = sb("x0_rows", 4 * P)
        x0 = sb("x0", 4 * P)
        xf = sb("x_final", 2 * 9 * PAIRS)
        q_s = sb("q_sample", H * B)
        scan_par = sb("scan_par", 7 * PAIRS)
        bias_pg = sb("bias_pages", PAGES * H)
        bias_nw = sb("bias_new", B * H)
        ln_rows = xf[:, 0:4 * P]
        score, prob = mm[:, KW:KW + 272], mm[:, KW + 272:KW + 544]
        multiples_i = q_s[:, 0:32].bitcast(I32)

        bank = [ctx.enter_context(nc.psum_tensor(f"bank{i}", [P, 512], F32)) for i in range(8)]

        def slot(j, kt):
            return ring[:, (j * KT + kt) * P:(j * KT + kt + 1) * P]

        def slot3(j, k0, k1):
            return ring[:, (j * KT + k0) * P:(j * KT + k1) * P].rearrange("p (k m) -> p k m", m=P)

        def rounded(t, k, width=N):
            return t[:, k * width:(k + 1) * width].bitcast(F32R)

        def weight(t, m, k):
            return rounded(t, (m % 2) * KT + k, P)

        def xtile(k):
            return xt[:, k * N:(k + 1) * N]

        x3 = xt[:, :].rearrange("p (k n) -> p k n", n=N)
        x_rows = big[:, 0:3 * D].rearrange("p (c d) -> p c d", c=3)
        k_ring = [big[:, i * KW:(i + 1) * KW] for i in range(4)]
        v_ring = [big[:, (4 + i) * KW:(5 + i) * KW] for i in range(4)]
        kq = [big[:, (8 + i) * KW:(9 + i) * KW] for i in range(2)]
        q_all = big[:, 10 * KW:11 * KW]
        st_rows = gd[0:2 * B, 0:2 * FF]
        k_new, v_new = kv_new[:, 0:KW], kv_new[:, KW:2 * KW]
        gate = gd[:, 0:GATES]
        diag_q = mm[:, 0:KW]
        sq_prompt = c_rows[:, 0:H * T]
        sq_sample, root_sample = scan_par[:, 0:H * B], scan_par[:, H * B:2 * H * B]
        att3 = att[:, :].rearrange("p (h n) -> p h n", h=H)
        glu = gd[:, GATES:GATES + HT * N]
        o_rows = c_rows[:, 0:2 * P]

        def cutter(tensor, start, end):
            at = [start]

            def cut(cols):
                at[0] += cols
                assert at[0] <= end
                return tensor[:, at[0] - cols:at[0]]
            return cut

        gcut = cutter(gd, 0, 11264)
        bias = gcut(H * 384)
        u_all = gcut(HT * N)
        q_t, k_t, v_t, u_t = gcut(N), gcut(N), gcut(N), gcut(N)
        s_sb, p_sb = gcut(768), gcut(768)
        p_diff, p_diff_t = gcut(384), gcut(384)
        v_rows, k_rows = gcut(256), gcut(256)
        toep_rows = gcut(384)
        bcut = cutter(big, 4 * KW, FT * N)
        tab = [bcut(512) for _ in range(2)]
        rot = [bcut(256) for _ in range(4)]
        z_re, z_im, y_re, y_im = bcut(256), bcut(256), bcut(256), bcut(256)
        x_st = [bcut(2 * N) for _ in range(2)]
        ptmp = c_rows[:, 0:1024]
        mst = bcut(512)
        ang = bcut(2048)
        MT = mm[:, 0:HT * 512].rearrange("p (t c) -> p t c", t=HT)
        fcut = cutter(late, 0, 2144)
        acc = [fcut(N) for _ in range(4)]
        th = [fcut(N) for _ in range(2)]
        up10 = fcut(40)
        up_rows = fcut(512)[0:10]
        std_sb = acc[0]
        h_tmp = [acc[1], acc[2], acc[3], th[0]]

        def sems(*names):
            return [sem(n) for n in names]

        wh_ready, wh_used, wl_ready, hn_ready = sems("weights_hi_ready", "weights_hi_used", "weights_lo_ready",
                                                     "h_unsplit_ready")
        ring_in = sems(*(f"weights_in{j}" for j in range(SLOTS)))
        k_in = sems(*(f"k_in{j}" for j in range(4)))
        v_in = sems(*(f"v_in{j}" for j in range(4)))
        xs_in, tab_in, par_in, st_in = sems("x_in", "table_in", "params_in", "state_in")
        rows_in, b_in, c_in, x0_in, page_in = sems("scan_rows_in", "b_in", "c_in", "x0_in", "pages_in")
        toep_out, toep_in = sems("toeplitz_out", "toeplitz_in")
        kv_stored, out_stored, upr_stored, y_stored = sems("kv_stored", "out_stored", "up_rows_stored", "y_stored")
        x_zero, rel_ready, const_ready, mt_zero = sems("x_rows_zeroed", "rel_ready", "constants_ready", "matrices_zeroed")
        bpad_zero, mult_ready = sems("b_padding_zeroed", "angle_multiples")
        tr, tr_used = sems("setup_transposed", "setup_copied")
        s5_tr, s5_used, s5_act, s5_dve = sems("s5_transposed", "s5_copied", "s5_act_steps", "s5_dve_steps")
        kv_zero, lam_exp = sems("kv_new_zeroed", "lambda_exp")
        pool_c, dve_c = sems("pool_chain", "dve_chain")
        slot_done, z_read, zv_read = sems("m_tiles_done", "m_tiles_read_by_act", "m_tiles_read_by_dve")
        kt_done, kt_read, vt_done, vt_read = sems("k_transposed", "k_rows_copied", "v_transposed", "v_rows_copied")
        sc_done, max_ready, exp_done = sems("scores_done", "max_ready", "exp_done")
        pd_ready, pdt_done, pdt_read, pv_done, pv_read = sems(
            "p_diff_ready", "p_diff_transposed", "p_diff_copied", "pv_done", "pv_read")
        mstb_ready, mst_ready, tab_ready, b_done, b_read, xs_ready, c_done, xf_read, y_ready = sems(
            "matrices_b_staged", "matrices_c_staged", "rotation_ready", "bu_done", "bu_read", "states_ready", "y_sums_done",
            "final_states_read", "y_ready")
        xft, xft_read = sems("final_states_transposed", "final_states_copied")
        dq_ready, qb_done, qb_ready, kq_ready, kq_read = sems(
            "diag_q_ready", "q_broadcast", "q_broadcast_copied", "kq_ready", "kq_reduced")
        smax_ready, gmax_ready, ssub_ready, sexp_ready, lsum_ready, lsum_done, spv_done, v_used, o_read = sems(
            "page_max_ready", "global_max_ready", "shifted_ready", "sample_exp_ready", "page_sum_ready",
            "denominator_ready", "sample_pv_done", "v_pages_used", "sample_out_read")
        w_ready, o_copied, ocomb_done = sems("map_weights_ready", "sample_pv_copied", "sample_out_done")
        gelu_act, gelu_dve = sems("gelu_act", "gelu_dve")
        sq_ready, ms_done, root_ready, att_ready, ssm_ready, merged_ready = sems(
            "squares_ready", "mean_squares", "roots_ready", "att_ready", "ssm_ready", "merged_ready")
        mean_done, cent_ready, csq_ready, var_done, std_ready, norm_ready, h_ready = sems(
            "mean_done", "centred", "centred_squares", "var_done", "std_ready", "normalised", "h_ready")
        tap0, tap_done, th_ready, hid_ready = sems("tap0", "taps_done", "tanh_ready", "hidden_ready")
        upt_done, upt_read, yt_done, yt_read = sems(
            "up_rows_transposed", "up_rows_copied", "y_transposed", "y_copied")
        block = ctx.enter_context(nc.Block())

        L1 = 4 * H
        GLU = L1 + 4
        PROJ0 = 8 * H + HT
        PROJ, OUT = PROJ0 + KT, PROJ0 + 2 * KT

        def gates_at(b):
            return L1 if isinstance(b, int) and b == 0 else 4 * b + (L1 + HT)
        UP = OUT + 2 * FT
        SPLIT_UP, SPLIT_DOWN = OUT - PROJ0, UP - PROJ0

        @block.sync
        def _(sp):
            def load_slot(n, j, *parts, split=False):
                if split:
                    sp.wait_ge(wl_ready, n - SLOTS - PROJ0 + 1)
                else:
                    wait(sp, slot_done, n - SLOTS + 1)
                k0 = 0
                for w, rows, col in parts:
                    src = w[0:rows, bass.ds(col, P)].rearrange("(k p) m -> p k m", p=P)
                    sp.dma_start(slot3(j, k0, k0 + rows // P), src).then_inc(ring_in[j], 16)
                    k0 += rows // P

            def load_head(i):
                for j in range(4):
                    load_slot(4 * i + j, j, (w_in, D, i * P + j * SW))

            sp.dma_start(x_rows[:, 0:2, :], a["x_prompt"][0].rearrange("(c p) d -> p c d", p=P)).then_inc(xs_in, 16)
            sp.wait_ge(x_zero, 1)
            sp.dma_start(x_rows[0:B, 2, :], a["x_sample"].rearrange("b o d -> (b o) d")).then_inc(xs_in, 16)
            for n, name in enumerate(("ssm_a_re", "ssm_a_im")):
                sp.dma_start(yg[0:PAIRS, n * P:(n + 1) * P],
                             a[name][0].rearrange("(q g) s -> q (g s)", g=2)).then_inc(rows_in, 16)
            sp.dma_start(small[0:PAIRS, 0:2],
                         a["ssm_log_dt"].rearrange("o (q g) -> (o q) g", g=2)).then_inc(rows_in, 16)
            load_slot(0, 0, (w_in, D, 0))
            for n, name in enumerate(("ssm_c_re", "ssm_c_im")):
                rows = c_rows[:, n * 1024:(n + 1) * 1024].rearrange("p (t e s) -> p t e s", t=HT, e=2)
                src = a[name][0].rearrange("(t g) c s -> (g c) t s", t=HT)
                for e in range(2):
                    sp.dma_start(rows[:, :, e, :], src).then_inc(c_in, 16)
            for n, name in enumerate(("ssm_b_re", "ssm_b_im")):
                sp.dma_start(att[:, n * 512:(n + 1) * 512].rearrange("p (q c) -> p q c", c=C),
                             a[name][0].rearrange("(q g) s c -> (g s) q c", g=2)).then_inc(b_in, 16)
            for r, name in enumerate(("state_ssm_re", "state_ssm_im")):
                for h in range(2):
                    sp.dma_start(x0_rows[:, (2 * r + h) * P:(2 * r + h + 1) * P],
                                 a[name][0, 4 * h:4 * h + 4].rearrange("b (q g) s -> (b q) (g s)", g=2)
                                 ).then_inc(x0_in, 16)
            load_slot(1, 1, (w_in, D, SW))
            sp.dma_start(par_rows[0:2 * FT, 0:3 * P].rearrange("t (w p) -> t w p", w=3),
                         a["conv_w"][0].rearrange("w (t p) -> t w p", p=P)).then_inc(par_in, 16)
            sp.dma_start(par_rows[0:2 * FT, 3 * P:4 * P],
                         a["conv_b"].rearrange("o (t p) -> (o t) p", p=P)).then_inc(par_in, 16)
            for n, name in enumerate(("ln1_g", "ln1_b", "ln2_g", "ln2_b")):
                sp.dma_start(ln_rows[0:KT, n * P:(n + 1) * P],
                             a[name].rearrange("o (t p) -> (o t) p", p=P)).then_inc(par_in, 16)
            for n, name in enumerate(("lambda_q1", "lambda_k1", "lambda_q2", "lambda_k2")):
                sp.dma_start(small[:, 64 + n * HD:64 + (n + 1) * HD],
                             a[name].to_broadcast([P, HD])).then_inc(par_in, 16)
            with nc.allow_non_contiguous_dma("one column each"):
                sp.dma_start(small[:, 16:24], a["ssm_d"].rearrange("o (t p) -> p (o t)", p=P)).then_inc(par_in, 16)
                sp.dma_start(small[:, 24:25], a["subln_g"].rearrange("o p -> p o")).then_inc(par_in, 16)
            sp.dma_start(st_rows, a["state_conv"][0].rearrange("b i f -> (b i) f")).then_inc(st_in, 16)
            sp.dma_start(mm[0:NB + 1, 0:OH_COLS], a["buckets"]).then_inc(tab_in, 16)
            sp.wait_ge(rel_ready, 1)
            sp.dma_start(small[0:NB, 32:32 + H], a["rel_bias"]).then_inc(tab_in, 16)
            sp.dma_start(page_no[0:1, :], a["page_table"].rearrange("(o b) g -> o (b g)", o=1)).then_inc(page_in, 16)
            sp.dma_start(out["conv_sample"][0, :, 0, :], a["state_conv"][0, :, 1, :]).then_inc(out_stored, 16)
            load_slot(2, 2, (w_in, D, 2 * SW))
            load_slot(3, 3, (w_in, D, 3 * SW))
            sp.wait_ge(tr_used, 22)
            sp.dma_start(scratch, toep_rows[0:H, :].unsqueeze(1).to_broadcast([H, P, 384])).then_inc(toep_out, 16)
            sp.wait_ge(toep_out, 16)
            b3 = bias.rearrange("p (h x) -> p h x", h=H)
            sp.dma_start(b3[:, :, 0:256],
                         bass.AP(scratch.tensor, P - 1, [[383, P], [384 * P, H], [1, 256]])).then_inc(toep_in, 16)
            sp.dma_start(b3[:, :, 256:384],
                         bass.AP(scratch.tensor, 2 * P - 1, [[383, P], [384 * P, H], [1, P]])).then_inc(toep_in, 16)

            def store_head(i):
                for rows, name, copied in ((k_rows, "k_prompt", kt_read), (v_rows, "v_prompt", vt_read)):
                    sp.wait_ge(copied, i + 1)
                    sp.dma_start(out[name].rearrange("(c p) k -> p c k", p=P)[:, :, bass.ds(i * P, P)],
                                 rows.rearrange("p (c d) -> p c d", c=2)).then_inc(kv_stored, 16)

            def load_gate(b, r):
                load_slot(gates_at(b) + r, r, (w_in, D, 4 * SW + b * 4 * P + r * P))

            def load_glu(j):
                load_slot(GLU + j, j % 4, (w_glu, SW, j * P))

            with sp.Fori(1, H) as i:
                load_head(i)
                store_head(i - 1)
            for r in range(4):
                load_gate(0, r)

            ck = a["cache_k"][0].rearrange("n p h j d -> n p (h j d)")
            cv = a["cache_v"][0].rearrange("n p h e -> n p (h e)")

            def load_page(cache, ring4, arrived, b, p):
                page = sp.value_load(page_no[0:1, bass.ds(b * PAGES + p, 1)], min_val=0, max_val=POOL_PAGES - 1)
                sp.dma_start(ring4[p % 4], cache[bass.ds(page, 1)].rearrange("o p k -> (o p) k")
                             ).then_inc(arrived[p % 4], 16)

            def load_batch(b, keys, values, gates=True):
                for p in range(0 if gates or not keys else 4, PAGES):
                    if keys and gates and p % 4 == 0:
                        load_gate(b, p // 4)
                    if keys and not gates and p >= 6 and p % 2 == 0 and p < 14:
                        load_glu(4 + (p - 6) // 2)
                    if keys:
                        wait(sp, kq_ready, 17 * b + p - 3 if p >= 4 else 17 * (b - 1) + 12 + p + 1)
                        load_page(ck, k_ring, k_in, b, p)
                    if values:
                        wait(sp, v_used, PAGES * (b - 1) + p - 3)
                        load_page(cv, v_ring, v_in, b - 1, p)

            sp.wait_ge(page_in, 16)
            for p in range(4):
                load_page(ck, k_ring, k_in, 0, p)
            store_head(H - 1)
            for j in range(4):
                load_glu(j)
            load_batch(0, True, False, gates=False)
            sp.wait_ge(xft_read, 2)
            for r, name in enumerate(("ssm_re_prompt", "ssm_im_prompt")):
                sp.dma_start(out[name], par_rows[0:PAIRS, r * P:(r + 1) * P]).then_inc(out_stored, 16)
            for r, name in enumerate(("ssm_re_sample", "ssm_im_sample")):
                for h in range(2):
                    sp.dma_start(out[name][h * P:(h + 1) * P, :],
                                 x0_rows[:, (2 * r + h) * P:(2 * r + h + 1) * P]).then_inc(out_stored, 16)
            sp.dma_start(out["k_sample"], k_new[0:B, :]).then_inc(out_stored, 16)
            sp.dma_start(out["v_sample"], v_new[0:B, :]).then_inc(out_stored, 16)
            load_batch(1, True, True)
            with sp.Fori(2, B) as b:
                load_batch(b, True, True)
            load_batch(B, False, True)

            def load_proj(i, split=True):
                for j in range(4):
                    load_slot(PROJ0 + 4 * i + j, j, (w_pa, SW, i * 4 * P + j * P), (w_ps, SW, i * 4 * P + j * P),
                              split=split)

            load_proj(0, False)
            with sp.Fori(1, KT // 4) as i:
                load_proj(i)
            with sp.Fori(0, KT // 4) as i:
                for j in range(4):
                    load_slot(PROJ + 4 * i + j, j, (w_out, D, i * 4 * P + j * P), split=True)

            def store_up(n, pairs):
                sp.wait_ge(upt_read, n + 1)
                for v in range(2):
                    rows = up_rows.rearrange("r (q v m) -> r v q m", q=2, v=2)[:, v, 0:pairs, :]
                    cols = bass.ds(v * FF + n * 2 * P, pairs * P)
                    sp.dma_start(out["conv_prompt"][:, cols].rearrange("r (q m) -> r q m", m=P),
                                 rows[0:2]).then_inc(upr_stored, 16)
                    sp.dma_start(out["conv_sample"][0, :, 1, cols].rearrange("r (q m) -> r q m", m=P),
                                 rows[2:10]).then_inc(upr_stored, 16)

            def load_up(n, pairs):
                for q in range(pairs):
                    if q == 1 or pairs == 1:
                        if not isinstance(n, int) or n >= 2:
                            store_up(n - 2, 2)
                    for v in range(2):
                        load_slot(OUT + 4 * n + 2 * q + v, 2 * q + v, (w_up, D, v * FF + n * 2 * P + q * P), split=True)

            load_up(0, 2)
            load_up(1, 2)
            with sp.Fori(2, FT // 2) as n:
                load_up(n, 2)
            load_up(FT // 2, 1)

            def load_down(i, o):
                k0, k1 = DOWN_PARTS[o % 3]
                j = (UP + o) % SLOTS
                sp.wait_ge(wl_ready, i * 12 + SPLIT_DOWN + o - SLOTS + 1)
                src = w_down[k0 * P:k1 * P, bass.ds(i * 4 * P + o // 3 * P, P)].rearrange("(k p) m -> p k m", p=P)
                sp.dma_start(slot3(j, 0, k1 - k0), src).then_inc(ring_in[j], 16)

            for o in range(12):
                load_down(0, o)
                if o == 1:
                    store_up(FT // 2 - 1, 2)
            store_up(FT // 2, 1)
            with sp.Fori(1, KT // 4) as i:
                for o in range(12):
                    load_down(i, o)
            for c in range(3):
                sp.wait_ge(yt_read, 4 * c + 4)
                rows = big[:, c * D:(c + 1) * D]
                if c < 2:
                    sp.dma_start(out["y_prompt"][c * P:(c + 1) * P, :], rows).then_inc(y_stored, 16)
                else:
                    sp.dma_start(out["y_sample"], rows[0:B]).then_inc(y_stored, 16)
            sp.wait_ge(y_stored, 3 * 16)
            sp.wait_ge(kv_stored, 2 * H * 16)
            sp.wait_ge(out_stored, 9 * 16)
            sp.wait_ge(upr_stored, 4 * (FT // 2 + 1) * 16)

        @block.gpsimd
        def _(pool):
            ch = Chain(pool, pool_c)
            pool.memset(x_rows[:, 2, :], 0.0).then_inc(x_zero, 1)
            ch.did(pool.memset(ident[:, :], 0.0))
            ch.wait()
            pool.affine_select(out=ident[:, :], in_=ident[:, :], compare_op=ALU.not_equal, fill=1.0, base=0,
                               pattern=[[-1, P]], channel_multiplier=1).then_inc(const_ready, 1)
            pool.memset(small[0:NB + 1, 32:32 + H], MASK).then_inc(rel_ready, 1)
            for tensor, value in ((ones[:, :], 1.0), (mean_w[:, :], 1.0 / D), (v_mean_w[:, :], 1.0 / P),
                                  (small[:, 4:5], PI / 2), (small[:, 5:6], EPS), (small[:, 6:7], 4 * EPS)):
                pool.memset(tensor, value).then_inc(const_ready, 1)
            ch.did(pool.iota(multiples_i[:, 0:16], pattern=[[1, 16]], base=1, channel_multiplier=0))
            ch.did(pool.iota(multiples_i[:, 16:32], pattern=[[16, 16]], base=0, channel_multiplier=0))
            ch.wait()
            pool.tensor_copy(small[:, 320:352], multiples_i[:, 0:32]).then_inc(mult_ready, 1)
            pool.memset(kv_new[:, :], 0.0).then_inc(bpad_zero, 1)
            pool.wait_ge(tr, 24)
            pool.memset(MT[:, :, 256:512], 0.0).then_inc(mt_zero, 1)
            pool.wait_ge(s5_tr, 10)
            pool.memset(kv_new[:, :], 0.0).then_inc(kv_zero, 1)
            pool.wait_ge(s5_dve, 7)
            pool.wait_ge(s5_act, 6)
            pool.wait_ge(s5_used, 10)

            ang4 = ang.rearrange("p (r q e) -> p r q e", r=2, q=PAIRS)

            def rotation(t, p):
                n = 4 * t + p

                def fine(r):
                    return ang4[:, r, bass.ds(n, 1), 0:16].to_broadcast([P, 16, 16])

                def coarse(r):
                    return ang4[:, r, bass.ds(n, 1), 16:32].rearrange("p o e -> p e o").to_broadcast([P, 16, 16])

                cos, sin = (tab[p % 2][:, r * 256:(r + 1) * 256].rearrange("p (a b) -> p a b", a=16) for r in range(2))
                t1, t2, t3, t4 = (ptmp[:, k * 256:(k + 1) * 256].rearrange("p (a b) -> p a b", a=16) for k in range(4))
                wait(pool, tab_ready, n)
                ch.did(pool.tensor_tensor(t1, coarse(0), fine(0), ALU.mult))
                ch.did(pool.tensor_tensor(t2, coarse(1), fine(1), ALU.mult))
                ch.did(pool.tensor_tensor(t3, coarse(1), fine(0), ALU.mult))
                ch.did(pool.tensor_tensor(t4, coarse(0), fine(1), ALU.mult))
                wait(pool, xs_ready, n - 1)
                ch.wait()
                ch.did(pool.tensor_tensor(cos, t1, t2, ALU.subtract))
                pool.tensor_tensor(sin, t3, t4, ALU.add).then_inc(tab_ready, 1)

            def s5_tile(t):
                wait(pool, b_done, 4 * t)
                pool.tensor_copy(mst[:, 0:256], MT[:, bass.ds(t, 1), 0:256].rearrange("p o c -> p (o c)")
                                 ).then_inc(mstb_ready, 1)
                rotation(t, 0)
                wait(pool, c_done, 4 * t)
                pool.tensor_copy(mst[:, 256:512], MT[:, bass.ds(t, 1), 256:512].rearrange("p o c -> p (o c)")
                                 ).then_inc(mst_ready, 1)
                for p in range(1, 4):
                    rotation(t, p)

            s5_tile(0)
            with pool.Fori(1, HT) as t:
                ch.enter(t, 1, 20)
                s5_tile(t)
            ch.leave(HT - 1)

            pool.wait_ge(c_done, 4 * HT)
            pool.wait_ge(xf_read, 4 * HT)

            def score_products(b):
                for p in range(PAGES + 1):
                    if p < PAGES:
                        pool.wait_ge(k_in[p % 4], 16 * (4 * b + p // 4 + 1))
                    if p == 0:
                        pool.wait_ge(qb_ready, b + 1)
                    wait(pool, kq_read, 17 * b + (p - 1 if p else 0))
                    keys = k_ring[p % 4] if p < PAGES else k_new
                    pool.tensor_tensor(kq[p % 2], keys, q_all, ALU.mult).then_inc(kq_ready, 1)
                pool.wait_ge(smax_ready, b + 1)
                pool.partition_all_reduce(small[:, 528:544], small[:, 512:528], P,
                                          bass.bass_isa.ReduceOp.max).then_inc(gmax_ready, 1)

            for b in range(B):
                score_products(b)

            pool.wait_ge(ocomb_done, B)
            def low(m, off, k_tiles):
                pool.wait_ge(wh_ready, m + 1)
                pool.wait_ge(slot_done, PROJ0 + m - 1)
                cols = slice((off % 2) * KT * P, (off % 2) * KT * P + k_tiles * P)
                pool.tensor_tensor(w_lo[:, cols].bitcast(F32R), slot3(off % SLOTS, 0, k_tiles).rearrange("p k m -> p (k m)"),
                                   w_hi[:, cols], ALU.subtract).then_inc(wl_ready, 1)

            with pool.Fori(0, SPLIT_DOWN // 4) as i:
                for j in range(4):
                    low(4 * i + j, j, KT)
            for j in range(SPLIT_DOWN % 4):
                low(SPLIT_DOWN - SPLIT_DOWN % 4 + j, j, KT)
            with pool.Fori(0, KT // 4) as i:
                for o in range(12):
                    k0, k1 = DOWN_PARTS[o % 3]
                    low(12 * i + SPLIT_DOWN + o, SPLIT_DOWN + o, k1 - k0)

        @block.tensor
        def _(pe):
            def transpose(dst, src):
                k = src.shape[0]
                return pe.transpose(dst, src, ident[0:k, 0:k])

            pe.wait_ge(const_ready, 7)
            pe.wait_ge(xs_in, 32)
            for k in range(KT):
                wait(pe, tr_used, k - 3)
                for c in range(3):
                    last = transpose(bank[k % 4][:, c * P:(c + 1) * P], x_rows[:, c, k * P:(k + 1) * P])
                last.then_inc(tr, 1)
            def m_tile(j, dst, arrived, rhs):
                pe.wait_ge(ring_in[j], arrived)
                k_tiles = len(rhs)
                for k in range(k_tiles):
                    last = pe.matmul(dst[:, 0:N], slot(j, k), rhs[k], start=(k == 0), stop=(k == k_tiles - 1))
                last.then_inc(slot_done, 1)

            x_tiles = [xtile(k) for k in range(KT)]

            def z_tile(i, j):
                wait(pe, z_read, 4 * i + j - 1)
                m_tile(j, bank[j % 2], 16 * (i + 1), x_tiles)

            pe.wait_ge(tr_used, KT)
            z_tile(0, 0)
            z_tile(0, 1)
            pe.wait_ge(par_in, 12 * 16)
            for w in range(4):
                last = transpose(bank[4][:, w * 2 * FT:(w + 1) * 2 * FT], par_rows[0:2 * FT, w * P:(w + 1) * P])
            last.then_inc(tr, 1)
            for w in range(4):
                last = transpose(bank[5][:, w * KT:(w + 1) * KT], ln_rows[0:KT, w * P:(w + 1) * P])
            last.then_inc(tr, 1)
            pe.wait_ge(st_in, 16)
            for g in range(3):
                if g == 2:
                    pe.wait_ge(tr_used, KT + 1)
                for f in range(32 * g, min(32 * g + 32, 2 * FT)):
                    last = transpose(bank[4 + (18 + g) % 4][:, (f % 32) * 16:(f % 32) * 16 + 16],
                                     st_rows[:, f * P:(f + 1) * P])
                last.then_inc(tr, 1)
            pe.wait_ge(tab_in, 32)
            rel = small[0:NB + 1, 32:32 + H]
            pe.wait_ge(tr_used, 18)
            pe.matmul(bank[5][0:H, 0:384], rel, mm[0:NB + 1, OH_TOEP:OH_TOEP + 384], start=True, stop=True).then_inc(tr, 1)
            pe.wait_ge(tr_used, 19)
            for p in range(PAGES):
                last = pe.matmul(bank[6][:, p * H:(p + 1) * H], mm[0:NB + 1, OH_PAGE + p * P:OH_PAGE + (p + 1) * P],
                                 rel, start=True, stop=True)
            last.then_inc(tr, 1)
            pe.wait_ge(tr_used, 20)
            for b in range(B):
                last = pe.matmul(bank[7][:, b * H:(b + 1) * H], mm[0:NB + 1, OH_NEW + b * P:OH_NEW + (b + 1) * P],
                                 rel, start=True, stop=True)
            last.then_inc(tr, 1)
            z_tile(0, 2)
            pe.wait_ge(tr_used, 24)
            pe.wait_ge(x0_in, 64)
            for k in range(4):
                last = transpose(bank[4][:, k * P:(k + 1) * P], x0_rows[:, k * P:(k + 1) * P])
            last.then_inc(s5_tr, 1)
            pe.wait_ge(c_in, 64)
            for k in range(4):
                wait(pe, s5_used, k - 2)
                for t in range(2):
                    for r in range(2):
                        at = r * 1024 + (2 * k + t) * P
                        last = transpose(bank[4 + (1 + k) % 4][:, (2 * t + r) * P:(2 * t + r + 1) * P],
                                         c_rows[:, at:at + P])
                last.then_inc(s5_tr, 1)
            z_tile(0, 3)
            pe.wait_ge(s5_dve, 3)
            pe.wait_ge(s5_used, 2)
            for k in range(7):
                last = transpose(bank[5][:, k * PAIRS:(k + 1) * PAIRS], yg[0:PAIRS, (9 + k) * P:(10 + k) * P])
            last.then_inc(s5_tr, 1)
            pe.wait_ge(s5_dve, 4)
            for k in range(4):
                pe.wait_ge(s5_used, 3 + k)
                for t in range(2):
                    for r in range(2):
                        at = r * 1024 + (2 * k + t) * P
                        last = transpose(bank[4 + (6 + k) % 4][:, (2 * t + r) * P:(2 * t + r + 1) * P],
                                         kv_new[:, at:at + P])
                last.then_inc(s5_tr, 1)

            def bu(t, p):
                pe.wait_ge(mstb_ready, t + 1)
                pe.wait_ge(z_read, 4 * t + 4)
                wait(pe, b_read, 4 * t + p)
                rows = slice(32 * p, 32 * p + 32)
                pe.matmul(bank[6][:, 0:N], mst[rows, 0:P], u_t[rows, :], start=True, stop=True)
                pe.matmul(bank[7][:, 0:N], mst[rows, P:2 * P], u_t[rows, :], start=True, stop=True).then_inc(b_done, 1)

            def cx(t, p):
                pe.wait_ge(xs_ready, 4 * t + p + 1)
                if p == 0:
                    pe.wait_ge(mst_ready, t + 1)
                    wait(pe, y_ready, t)
                for r in range(2):
                    last = pe.matmul(bank[3][32 * p:32 * p + 32, 0:N], mst[:, (2 + r) * P + 32 * p:(2 + r) * P + 32 * p + 32],
                                     x_st[p % 2][:, r * N:(r + 1) * N], start=(r == 0), stop=(r == 1))
                last.then_inc(c_done, 1)

            def scores(i):
                pe.wait_ge(z_read, 4 * i + 2)
                wait(pe, pv_read, i)
                wait(pe, max_ready, i)
                for j in range(2):
                    rows = slice(64 * j, 64 * j + 64)
                    pe.matmul(bank[4 + j][:, 0:256], q_t[rows, P:2 * P], k_t[rows, 0:T], start=True, stop=True)
                    last = pe.matmul(bank[4 + j][:, 256:384], q_t[rows, 0:P], k_t[rows, 0:P], start=True, stop=True)
                last.then_inc(sc_done, 1)

            def to_rows(src, done, free, count):
                wait(pe, free, count)
                transpose(bank[2][:, 0:P], src[:, 0:P])
                transpose(bank[2][:, P:2 * P], src[:, P:2 * P])
                transpose(bank[2][0:B, 2 * P:3 * P], src[:, T:N]).then_inc(done, 1)

            def keys_to_rows(i):
                to_rows(k_t, kt_done, pdt_read, i)

            def values_to_rows(i):
                pe.wait_ge(z_read, 4 * i + 3)
                to_rows(v_t, vt_done, kt_read, i + 1)

            def p_diff_rows(i):
                pe.wait_ge(pd_ready, i + 1)
                pe.wait_ge(vt_read, i + 1)
                for k, at in enumerate((256, 0, P)):
                    last = transpose(bank[2][:, k * P:(k + 1) * P], p_diff[:, at:at + P])
                last.then_inc(pdt_done, 1)

            def prompt_pv(i):
                pe.wait_ge(pdt_read, i + 1)
                pe.matmul(bank[4][:, 0:T], v_rows[:, 0:P], p_diff_t[:, 0:T], start=True, stop=False)
                pe.matmul(bank[4][:, P:T], v_rows[:, P:2 * P], p_diff_t[:, T:T + P], start=False, stop=True).then_inc(pv_done, 1)

            def head(i, first=False, last=False):
                t = i - 1
                z_tile(i, 0)
                if not first:
                    cx(t - 1, 3)
                values_to_rows(i - 1)
                bu(t, 0)
                for j in range(1, 4):
                    z_tile(i, j)
                    if j == 3:
                        p_diff_rows(i - 1)
                    cx(t, j - 1)
                    bu(t, j)
                prompt_pv(i - 1)
                if not last:
                    keys_to_rows(i)
                    scores(i)

            pe.wait_ge(s5_used, 10)
            keys_to_rows(0)
            scores(0)
            head(1, first=True)
            with pe.Fori(2, H) as i:
                head(i)
            head(H, last=True)
            cx(HT - 1, 3)

            def broadcast_q(b):
                pe.wait_ge(dq_ready, b + 1)
                wait(pe, qb_ready, b)
                pe.matmul(bank[2][:, :], ones[:, :], diag_q[:, 0:512], start=True, stop=True)
                pe.matmul(bank[3][:, :], ones[:, :], diag_q[:, 512:1024], start=True, stop=True).then_inc(qb_done, 1)

            pe.wait_ge(y_ready, HT)
            pe.wait_ge(pdt_read, H)
            broadcast_q(0)
            pe.wait_ge(xf_read, 4 * HT)
            pe.wait_ge(b_read, 4 * HT)
            xf4 = xf[:, :].rearrange("p (r c q) -> p r c q", r=2, c=9)
            for r in range(2):
                last = transpose(bank[6][0:PAIRS, r * P:(r + 1) * P], xf4[:, r, 0, :])
            last.then_inc(xft, 1)
            pe.wait_ge(max_ready, H)
            for r in range(2):
                for h in range(2):
                    at = r * 9 * PAIRS + (1 + 4 * h) * PAIRS
                    last = transpose(bank[5][:, (2 * r + h) * P:(2 * r + h + 1) * P], xf[:, at:at + P])
            last.then_inc(xft, 1)
            pe.wait_ge(xft_read, 2)
            pe.wait_ge(pv_read, H)
            pe.wait_ge(sq_ready, 1)
            for c in range(4):
                pe.matmul(bank[4 + c][:, :], v_mean_w[:, :], sq_prompt[:, c * 512:(c + 1) * 512],
                          start=True, stop=True).then_inc(ms_done, 1)
            y_tiles = [yg[:, k * N:(k + 1) * N] for k in range(HT)]
            pe.wait_ge(gelu_dve, 2)
            with pe.Fori(0, 2) as i:
                for j in range(4):
                    pe.wait_ge(z_read, GLU + 4 * i + j - 1)
                    m_tile(j, bank[j % 2], 16 * (H + 1 + i + 1), y_tiles)

            def gate_part(b, r, c):
                if c == 0:
                    pe.wait_ge(z_read, gates_at(b) + r - 1)
                    pe.wait_ge(ring_in[r], 16 * (H + b + 3))
                for k in range(4 * c, 4 * c + 4):
                    last = pe.matmul(bank[r % 2][:, 0:N], slot(r, k), xtile(k), start=(k == 0), stop=(k == KT - 1))
                if c == 3:
                    last.then_inc(slot_done, 1)

            def denominators(b):
                pe.wait_ge(lsum_ready, b + 1)
                wait(pe, w_ready, b)
                pe.matmul(bank[7][:, 0:16], ones[:, :], small[:, 544:560], start=True, stop=True).then_inc(lsum_done, 1)

            def page_pv(b, p):
                if p < PAGES:
                    pe.wait_ge(v_in[p % 4], 16 * (4 * b + p // 4 + 1))
                if p == 0:
                    pe.wait_ge(sexp_ready, b + 1)
                    wait(pe, o_copied, b)
                values = v_ring[p % 4] if p < PAGES else v_new
                for g in range(4):
                    last = pe.matmul(bank[4][32 * g:32 * g + 16, 0:2 * P], prob[:, p * 16:(p + 1) * 16],
                                     values[:, g * 2 * P:(g + 1) * 2 * P], start=(p == 0), stop=(p == PAGES))
                last.then_inc(v_used if p < PAGES else spv_done, 1)

            def combine(b):
                pe.wait_ge(o_copied, b + 1)
                pe.wait_ge(w_ready, b + 1)
                wait(pe, o_read, b)
                for h in range(H):
                    last = pe.matmul(bank[6][:, h:h + 1], o_rows[:, h % 2 * P:(h % 2 + 1) * P], small[:, 576 + h:577 + h],
                                     start=True, stop=True)
                last.then_inc(ocomb_done, 1)

            def decode(b, scored, summed, more=True):
                if summed:
                    denominators(b - 1)
                for r in range(4):
                    if scored and more and r == 3:
                        broadcast_q(b + 1)
                    for c in range(4):
                        if scored and summed:
                            gate_part(b, r, c)
                        if summed:
                            page_pv(b - 1, 4 * r + c)
                if summed:
                    page_pv(b - 1, PAGES)
                    combine(b - 1)

            decode(0, True, False)
            pe.wait_ge(root_ready, 4)
            decode(1, True, True)
            with pe.Fori(2, B - 1) as b:
                decode(b, True, True)
            decode(B - 1, True, True, False)
            decode(B, False, True)

            pe.wait_ge(sq_ready, 2)
            pe.matmul(bank[4][:, 0:H * B], v_mean_w[:, :], sq_sample, start=True, stop=True).then_inc(ms_done, 1)

            def products(m, off, sums):
                pe.wait_ge(wh_ready, m + 1)
                for dst, k0, highs, lows, start, _, ready in sums:
                    for k in range(len(highs)):
                        if ready is not None:
                            pe.wait_ge(*ready(k))
                        pe.matmul(dst[:, 0:N], weight(w_hi, off, k0 + k), highs[k], start=start and k == 0, stop=False)
                        last = pe.matmul(dst[:, 0:N], weight(w_hi, off, k0 + k), lows[k], start=False, stop=False)
                last.then_inc(wh_used, 1)
                pe.wait_ge(wl_ready, m + 1)
                for dst, k0, highs, _, _, stop, _ in sums:
                    for k in range(len(highs)):
                        last = pe.matmul(dst[:, 0:N], weight(w_lo, off, k0 + k), highs[k], start=False,
                                         stop=stop and k == len(highs) - 1)
                last.then_inc(slot_done, 1)

            def tiles(t, k0, k1):
                return [rounded(t, k) for k in range(k0, k1)]

            branches = [(tiles(a_hi, 0, HT), tiles(a_lo, 0, HT)), (tiles(s_hi, 0, HT), tiles(s_lo, 0, HT))]
            pe.wait_ge(z_read, PROJ0)
            pe.wait_ge(att_ready, 2)
            pe.wait_ge(ssm_ready, 1)

            def proj(i):
                for j in range(4):
                    wait(pe, zv_read, 4 * i + j - 1)
                    products(4 * i + j, j, [(bank[2 * s + j % 2], s * HT, *branches[s], True, True, None) for s in range(2)])

            proj(0)
            with pe.Fori(1, 4) as i:
                proj(i)

            def mean_tile(n):
                return pe.matmul(bank[6][:, 0:N], mean_w[:, :], xtile(n), start=(n == 0), stop=(n == KT - 1))

            m_parts = tiles(m_hi, 0, KT), tiles(m_lo, 0, KT)
            for n in range(KT):
                pe.wait_ge(zv_read, KT + n - 1)
                products(KT + n, n, [(bank[n % 2], 0, *m_parts, True, True,
                                      (lambda k: (merged_ready, k + 1)) if n == 0 else None)])
                if n:
                    pe.wait_ge(zv_read, KT + n)
                    mean_tile(n - 1)
            pe.wait_ge(zv_read, 2 * KT)
            mean_tile(KT - 1).then_inc(mean_done, 1)

            def variance(ln):
                for n in range(KT):
                    if n % 4 == 0:
                        pe.wait_ge(csq_ready, 4 * ln + n // 4 + 1)
                    last = pe.matmul(bank[7][:, 0:N], mean_w[:, :], big[:, n * N:(n + 1) * N], start=(n == 0),
                                     stop=(n == KT - 1))
                last.then_inc(var_done, 1)

            variance(0)
            h_parts = tiles(h_hi, 0, KT), tiles(h_lo, 0, KT)

            def up_rows_out(n, pairs):
                pe.wait_ge(tap0, 4 * n + 2 * pairs)
                wait(pe, upt_read, n)
                for t in range(2 * pairs):
                    last = transpose(bank[4][0:10, t * P:(t + 1) * P], up10[:, t * 10:(t + 1) * 10])
                last.then_inc(upt_done, 1)

            def up(n, pairs, first=False):
                for t in range(2 * pairs):
                    pe.wait_ge(zv_read, 2 * KT + (0 if first else 4 * (n - 1) + t + 1))
                    products(4 * n + SPLIT_UP + t, t, [(bank[t], 0, *h_parts, True, True,
                                                        (lambda k: (h_ready, k + 1)) if first and t == 0 else None)])
                    if t == 0 and not first:
                        up_rows_out(n - 1, 2)

            up(0, 2, True)
            with pe.Fori(1, FT // 2) as n:
                up(n, 2)
            up(FT // 2, 1)

            down_base = 2 * KT + 2 * FT

            for n in range(KT):
                pe.wait_ge(zv_read, down_base + max(0, n - 1))
                for part, (k0, k1) in enumerate(DOWN_PARTS):
                    m = SPLIT_DOWN + 3 * n + part
                    products(m, m, [(bank[n % 2], 0, tiles(hid_hi, k0, k1), tiles(hid_lo, k0, k1), part == 0, part == 2,
                                     (lambda k: (hid_ready, k0 + k + 1)) if n == 0 else None)])
                    if n == 0 and part == 0:
                        up_rows_out(FT // 2, 1)
                if n:
                    pe.wait_ge(zv_read, down_base + n)
                    mean_tile(n - 1)
            pe.wait_ge(zv_read, down_base + KT)
            mean_tile(KT - 1).then_inc(mean_done, 1)
            variance(1)
            for c in range(3):
                for g in range(4):
                    n = 4 * c + g
                    wait(pe, yt_read, n - 3)
                    for k in range(4):
                        if c == 0:
                            pe.wait_ge(h_ready, KT + 4 * g + k + 1)
                        tile = xtile(4 * g + k)[:, c * P:min(N, (c + 1) * P)]
                        last = transpose(bank[n % 4][0:tile.shape[1], k * P:(k + 1) * P], tile)
                    last.then_inc(yt_done, 1)

        @block.scalar
        def _(act):
            def copy(dst, src, scale=1.0):
                return act.activation(dst, src, ACT.Copy, scale=scale)

            def row(k):
                return yg[0:PAIRS, k * P:(k + 1) * P]

            act.wait_ge(rows_in, 48)
            act.wait_ge(const_ready, 7)
            act.activation(small[0:PAIRS, 2:4], small[0:PAIRS, 0:2], ACT.Exp).then_inc(s5_act, 1)
            act.wait_ge(s5_dve, 1)
            act.activation(row(9), row(2), ACT.Exp).then_inc(s5_act, 1)
            act.wait_ge(s5_dve, 2)
            act.activation(row(6), row(10), ACT.Sin, scale=TWO_PI_DOWN).then_inc(s5_act, 1)
            act.activation(row(7), row(5), ACT.Sin, scale=-TWO_PI_DOWN, bias=small[0:PAIRS, 4:5]).then_inc(s5_act, 1)
            for k in range(KT):
                act.wait_ge(tr, k + 1)
                copy(xtile(k), bank[k % 4][:, 0:N]).then_inc(tr_used, 1)
            q_s3 = q_s[:, :].rearrange("p (h b) -> p h b", h=H)

            def copy_q(i):
                act.wait_ge(slot_done, 4 * i + 1)
                wait(act, sc_done, i)
                copy(q_t, bank[0][:, 0:N])
                copy(q_s3[:, bass.ds(i, 1), :].rearrange("p o b -> p (o b)"), bank[0][:, T:N]).then_inc(z_read, 1)

            def copy_k(i):
                act.wait_ge(slot_done, 4 * i + 2)
                wait(act, kt_done, i)
                copy(k_t, bank[1][:, 0:N]).then_inc(z_read, 1)

            def copy_v(i):
                act.wait_ge(slot_done, 4 * i + 3)
                wait(act, vt_done, i)
                copy(v_t, bank[0][:, 0:N]).then_inc(z_read, 1)

            def copy_u(i):
                act.wait_ge(slot_done, 4 * i + 4)
                wait(act, b_done, 4 * i)
                copy(u_t, bank[1][:, 0:N])
                copy(u_all[:, bass.ds(i * N, N)], bank[1][:, 0:N]).then_inc(z_read, 1)

            for n, (dst, rows, cols) in enumerate((
                    (conv_par[:, :], P, 8 * FT), (ln_par[:, :], P, 4 * KT), (conv_state[:, 0:512], P, 512),
                    (conv_state[:, 512:1024], P, 512), (conv_state[:, 1024:2 * FT * 16], P, 2 * FT * 16 - 1024),
                    (toep_rows[0:H, :], H, 384), (bias_pg[:, :], P, PAGES * H), (bias_nw[:, :], P, B * H))):
                act.wait_ge(tr, KT + n + 1)
                copy(dst, bank[4 + n % 4][0:rows, 0:cols]).then_inc(tr_used, 1)
                if n == 4:
                    act.wait_ge(mult_ready, 1)
                    copy_q(0)
                    copy_k(0)
            copy_v(0)
            copy_u(0)
            act.wait_ge(par_in, 12 * 16)
            act.wait_ge(s5_dve, 6)
            act.activation(small[:, 28:30], small[:, 26:28], ACT.Exp).then_inc(lam_exp, 1)
            act.wait_ge(s5_dve, 7)
            for r, src in enumerate((att[:, 1024:2048], att[:, 0:1024])):
                if r == 0:
                    act.activation(ang[:, 0:1024], src, ACT.Sin, scale=-TWO_PI_DOWN, bias=small[:, 4:5]).then_inc(s5_act, 1)
                else:
                    act.activation(ang[:, 1024:2048], src, ACT.Sin, scale=TWO_PI_DOWN).then_inc(s5_act, 1)
            act.wait_ge(kv_zero, 1)

            xf4 = xf[:, :].rearrange("p (r c q) -> p r c q", r=2, c=9)

            def final_states(t, p):
                act.wait_ge(xs_ready, 4 * t + p + 1)
                copy(xf4[:, :, :, bass.ds(4 * t + p, 1)].rearrange("p r c o -> p r (c o)"),
                     x_st[p % 2].rearrange("p (r n) -> p r n", r=2)[:, :, T - 1:N]).then_inc(xf_read, 1)

            def exps(i):
                act.wait_ge(max_ready, i + 1)
                wait(act, pd_ready, i)
                for blk, cols in enumerate((slice(0, 256), slice(256, 384))):
                    for j in range(2):
                        k = 2 * blk + j
                        src = s_sb[:, 384 * j + cols.start:384 * j + cols.stop]
                        dst = p_sb[:, 384 * j + cols.start:384 * j + cols.stop]
                        last = act.activation(dst, src, ACT.Exp, bias=small[:, 420 + k:421 + k],
                                              accum_out=small[:, 424 + k:425 + k])
                last.then_inc(exp_done, 1)

            def first_gate(r):
                act.wait_ge(slot_done, L1 + r + 1)
                act.activation(gate[:, r * N:(r + 1) * N], bank[r % 2][:, 0:N], ACT.Tanh, scale=0.5).then_inc(z_read, 1)

            def key_rows(i):
                act.wait_ge(kt_done, i + 1)
                wait(act, kv_stored, 32 * i)
                copy(k_rows, bank[2][:, 0:256])
                copy(k_new[0:B, bass.ds(i * P, P)], bank[2][0:B, 256:384]).then_inc(kt_read, 1)

            def value_rows(i):
                act.wait_ge(vt_done, i + 1)
                wait(act, pv_done, i)
                act.wait_ge(kv_stored, 32 * i + 16)
                copy(v_rows, bank[2][:, 0:256])
                copy(v_new[0:B, bass.ds(i * P, P)], bank[2][0:B, 256:384]).then_inc(vt_read, 1)

            def head(i, first=False, last=False):
                t = i - 1
                first_gate(0) if last else copy_q(i)
                if not first:
                    final_states(t - 1, 3)
                value_rows(i - 1)
                first_gate(1) if last else copy_k(i)
                final_states(t, 0)
                exps(i - 1)
                first_gate(2) if last else copy_v(i)
                final_states(t, 1)
                act.wait_ge(pdt_done, i)
                copy(p_diff_t, bank[2][:, 0:384]).then_inc(pdt_read, 1)
                final_states(t, 2)
                first_gate(3) if last else copy_u(i)
                act.wait_ge(pv_done, i)
                copy(att[:, bass.ds((i - 1) * N, T)], bank[4][:, 0:T]).then_inc(pv_read, 1)
                if not last:
                    key_rows(i)

            key_rows(0)
            head(1, first=True)
            with act.Fori(2, H) as i:
                head(i)
            head(H, last=True)
            final_states(HT - 1, 3)

            def query(b):
                act.wait_ge(qb_done, b + 1)
                wait(act, kq_ready, 17 * b)
                copy(q_all[:, 0:512], bank[2][:, :], HD ** -0.5)
                copy(q_all[:, 512:1024], bank[3][:, :], HD ** -0.5).then_inc(qb_ready, 1)

            query(0)
            act.wait_ge(xft, 1)
            copy(par_rows[0:PAIRS, 0:2 * P], bank[6][0:PAIRS, 0:2 * P]).then_inc(xft_read, 1)
            act.wait_ge(xft, 2)
            copy(x0_rows[:, :], bank[5][:, :]).then_inc(xft_read, 1)
            gelu_t = mm[:, H * N:2 * H * N]
            act.wait_ge(y_ready, HT)
            act.wait_ge(mst_ready, HT)
            act.activation(gelu_t, yg[:, :], ACT.Square).then_inc(gelu_act, 1)
            act.activation(sq_prompt.rearrange("p (h n) -> p h n", h=H), att3[:, :, 0:T], ACT.Square).then_inc(sq_ready, 1)
            act.wait_ge(gelu_dve, 1)
            act.activation(gelu_t, gelu_t, ACT.Tanh, scale=0.7978845608028654).then_inc(gelu_act, 1)
            for c in range(4):
                act.wait_ge(ms_done, c + 1)
                act.activation(sq_prompt[:, c * 512:(c + 1) * 512], bank[4 + c][:, :], ACT.Sqrt,
                               bias=small[:, 5:6]).then_inc(root_ready, 1)
            act.wait_ge(kv_stored, 32 * H)
            for j in range(HT):
                act.wait_ge(slot_done, GLU + j + 1)
                act.activation(glu[:, j * N:(j + 1) * N], bank[j % 2][:, 0:N], ACT.Tanh, scale=0.25).then_inc(z_read, 1)

            def copy_sums(b):
                act.wait_ge(spv_done, b + 1)
                wait(act, ocomb_done, b)
                for g in range(4):
                    last = copy(o_rows[32 * g:32 * g + 16, :], bank[4][32 * g:32 * g + 16, 0:2 * P])
                last.then_inc(o_copied, 1)

            def decode(b, summed=True, more=True):
                if not summed:
                    query(1)
                for r in range(4 if summed else 0):
                    if r == 3 and more:
                        query(b + 1)
                    act.wait_ge(slot_done, gates_at(b) + r + 1)
                    act.activation(gate[:, bass.ds((4 * b + r) * N, N)], bank[r % 2][:, 0:N], ACT.Tanh,
                                   scale=0.5).then_inc(z_read, 1)
                if summed:
                    copy_sums(b - 1)
                act.wait_ge(ssub_ready, b + 1)
                act.activation(prob, score, ACT.Exp).then_inc(sexp_ready, 1)

            decode(0, False)
            act.wait_ge(att_ready, 1)
            with act.Fori(1, B - 1) as b:
                decode(b)
            decode(B - 1, True, False)
            copy_sums(B - 1)

            def high(g, off, branch=False, k_tiles=KT):
                g, j = g + off // SLOTS, off % SLOTS
                base = 16 * (2 * H + 2)
                act.wait_ge(ring_in[j], (g + 1) * 32 + base if branch else (g + 1) * 16 + base + 16 * 4)
                wait(act, wh_used, 4 * g + j - 1)
                wait(act, wl_ready, 4 * g + j - 1)
                act.activation(w_hi[:, (j % 2) * KT * P:(j % 2) * KT * P + k_tiles * P].bitcast(F32R),
                               slot3(j, 0, k_tiles).rearrange("p k m -> p (k m)"), ACT.Copy).then_inc(wh_ready, 1)

            high(0, 0, True)
            act.wait_ge(o_read, B)
            act.activation(sq_sample.rearrange("p (h b) -> p h b", h=H), att3[:, :, T:N], ACT.Square).then_inc(sq_ready, 1)
            act.wait_ge(ms_done, 5)
            act.activation(root_sample, bank[4][:, 0:H * B], ACT.Sqrt, bias=small[:, 5:6]).then_inc(root_ready, 1)
            high(0, 1, True)

            def norm(ln):
                for g in range(4):
                    act.wait_ge(cent_ready, 4 * ln + g + 1)
                    act.activation(big[:, 4 * g * N:4 * (g + 1) * N], xt[:, 4 * g * N:4 * (g + 1) * N],
                                   ACT.Square).then_inc(csq_ready, 1)
                act.wait_ge(var_done, ln + 1)
                act.activation(std_sb, bank[7][:, 0:N], ACT.Sqrt, bias=small[:, 6:7]).then_inc(std_ready, 1)
                for k in range(KT):
                    act.wait_ge(norm_ready, 4 * ln + k // 4 + 1)
                    if ln == 0:
                        wait(act, h_ready, k - 3)
                    act.activation(xtile(k) if ln else h_tmp[k % 4], xtile(k), ACT.Identity,
                                   scale=ln_par[:, 32 * ln + k:32 * ln + k + 1],
                                   bias=ln_par[:, 32 * ln + 16 + k:32 * ln + 17 + k]).then_inc(h_ready if ln else hn_ready, 1)

            for j in range(2, 4):
                high(0, j, True)
            with act.Fori(1, 4) as g:
                for j in range(4):
                    high(g, j, True)
            with act.Fori(4, 8) as g:
                for j in range(4):
                    high(g, j)
            for j in range(2):
                high(8, j)
            norm(0)

            def par(w, tile):
                return conv_par[:, bass.ds(w * 2 * FT + tile, 1)]

            def up_rows_copy(n, pairs):
                act.wait_ge(upt_done, n + 1)
                wait(act, upr_stored, 64 * n)
                copy(up_rows[:, 0:2 * pairs * P], bank[4][0:10, 0:2 * pairs * P]).then_inc(upt_read, 1)

            def up(n, pairs, first=False):
                for q in range(pairs):
                    wait(act, hid_ready, 2 * (n - 1) + q + 1)
                    for v in range(2):
                        t = 2 * q + v
                        tile = 2 * n + q + v * FT
                        high(n + 8, t + 2)
                        act.wait_ge(slot_done, OUT + 4 * n + t + 1)
                        act.activation(acc[t], bank[t][:, 0:N], ACT.Identity, scale=par(2, tile), bias=par(3, tile))
                        if t == 0:
                            wait(act, upt_done, n)
                        copy(up10[:, t * 10:(t + 1) * 10], bank[t][:, T - 2:N]).then_inc(tap0, 1)
                    if q == 0 and not first:
                        up_rows_copy(n - 1, 2)
                    act.wait_ge(tap_done, 4 * n + 2 * q + 1)
                    act.activation(th[q], acc[2 * q], ACT.Tanh, scale=0.5).then_inc(th_ready, 1)

            up(0, 2, True)
            with act.Fori(1, FT // 2) as n:
                up(n, 2)
            up(FT // 2, 1)
            up_rows_copy(FT // 2, 1)
            first = SPLIT_DOWN // 4

            def high_down(i, o):
                k0, k1 = DOWN_PARTS[o % 3]
                high(3 * i + first, SPLIT_DOWN % 4 + o, k_tiles=k1 - k0)

            with act.Fori(0, KT // 4 - 1) as i:
                for o in range(2, 14):
                    high_down(i, o)
            for o in range(2, 12):
                high_down(KT // 4 - 1, o)
            norm(1)

        @block.vector
        def _(dve):
            ch = Chain(dve, dve_c)

            def row(k):
                return yg[0:PAIRS, k * P:(k + 1) * P]

            def link(ins):
                ch.did(ins)
                ch.wait()

            a_re, a_im, t_re, t_im = row(0), row(1), row(2), row(3)
            turns, turns_abs, sin, cos = row(10), row(5), row(6), row(7)
            tmp, inv = row(8), row(4)
            mag, ab_re, ab_im, f_re, f_im, neg_im = row(9), row(11), row(12), row(13), row(14), row(15)
            dve.wait_ge(rows_in, 48)
            dve.wait_ge(s5_act, 1)
            dt = small[0:PAIRS, 2:4].unsqueeze(2).to_broadcast([PAIRS, 2, S])

            def g2(x):
                return x.rearrange("q (g s) -> q g s", g=2)

            ch.did(dve.tensor_tensor(g2(t_im), g2(a_im), dt, ALU.mult))
            dve.tensor_tensor(g2(t_re), g2(a_re), dt, ALU.mult).then_inc(s5_dve, 1)
            ch.wait()
            link(dve.tensor_scalar(t_im, t_im, 1.0 / (2 * PI), None, ALU.mult))
            whole = mm[0:PAIRS, KT * N - P:KT * N].bitcast(I32)
            link(dve.tensor_copy(whole, t_im))
            link(dve.tensor_copy(tmp, whole))
            link(dve.tensor_tensor(turns, t_im, tmp, ALU.subtract))
            dve.scalar_tensor_tensor(turns_abs, turns, -1.0, turns, ALU.mult, ALU.max).then_inc(s5_dve, 1)
            ch.did(dve.tensor_tensor(inv, a_re, a_re, ALU.mult))
            link(dve.tensor_tensor(tmp, a_im, a_im, ALU.mult))
            link(dve.tensor_tensor(inv, inv, tmp, ALU.add))
            link(dve.reciprocal(inv, inv))
            dve.wait_ge(s5_act, 4)
            ch.did(dve.tensor_tensor(ab_re, mag, cos, ALU.mult))
            link(dve.tensor_tensor(ab_im, mag, sin, ALU.mult))
            link(dve.tensor_scalar(t_re, ab_re, -1.0, None, ALU.add))
            ch.did(dve.tensor_tensor(f_re, t_re, a_re, ALU.mult))
            ch.did(dve.tensor_tensor(tmp, ab_im, a_im, ALU.mult))
            ch.did(dve.tensor_tensor(f_im, ab_im, a_re, ALU.mult))
            link(dve.tensor_tensor(t_im, t_re, a_im, ALU.mult))
            ch.did(dve.tensor_tensor(f_re, f_re, tmp, ALU.add))
            link(dve.tensor_tensor(f_im, f_im, t_im, ALU.subtract))
            ch.did(dve.tensor_scalar(neg_im, ab_im, -1.0, None, ALU.mult))
            ch.did(dve.tensor_tensor(f_re, f_re, inv, ALU.mult))
            link(dve.tensor_tensor(f_im, f_im, inv, ALU.mult))
            dve.tensor_copy(small[0:PAIRS, 7:8], small[0:PAIRS, 4:5]).then_inc(s5_dve, 1)

            dve.wait_ge(s5_tr, 1)
            dve.tensor_copy(x0[:, :], bank[4][:, :]).then_inc(s5_used, 1)
            dve.wait_ge(mt_zero, 1)
            for k in range(4):
                dve.wait_ge(s5_tr, 2 + k)
                src = bank[4 + (1 + k) % 4][:, :].rearrange("p (t r q g c) -> p t r q g c", t=2, r=2, q=4, g=2)
                dst = MT[:, 2 * k:2 * k + 2, 256:512].rearrange("p t (r q g c) -> p t r q g c", r=2, q=4, g=2)
                for t in range(2):
                    for g in range(2):
                        rows = slice(64 * g, 64 * g + 64)
                        for r in range(2):
                            last = dve.tensor_scalar(dst[rows, t, r, :, g, :], src[rows, t, r, :, g, :],
                                                     1.0 - 2.0 * r, None, ALU.mult)
                last.then_inc(s5_used, 1)
            dve.wait_ge(s5_tr, 6)
            dve.tensor_copy(scan_par[:, :], bank[5][:, 0:7 * PAIRS]).then_inc(s5_used, 1)
            dve.wait_ge(s5_used, 6)
            dve.wait_ge(b_in, 32)
            dve.wait_ge(bpad_zero, 1)
            b_re, b_im, w0, w1 = (att[:, k * 512:(k + 1) * 512].rearrange("p (q c) -> p q c", c=C) for k in range(4))
            fr, fi = (scan_par[:, k * PAIRS:(k + 1) * PAIRS].unsqueeze(2).to_broadcast([P, PAIRS, C]) for k in (4, 5))
            for r, ((x, y), op) in enumerate((((fr, fi), ALU.subtract), ((fi, fr), ALU.add))):
                ch.did(dve.tensor_tensor(w0, b_re, x, ALU.mult))
                link(dve.tensor_tensor(w1, b_im, y, ALU.mult))
                for g in range(2):
                    rows = slice(64 * g, 64 * g + 64)
                    dst = kv_new[rows, r * 1024:(r + 1) * 1024].rearrange("p (q c) -> p q c", c=2 * C)[:, :, g * C:(g + 1) * C]
                    last = dve.tensor_tensor(dst, w0[rows], w1[rows], op)
                    if r == 1 and g == 1:
                        last.then_inc(s5_dve, 1)
                    else:
                        ch.did(last)
                ch.wait()
            for k in range(4):
                dve.wait_ge(s5_tr, 7 + k)
                dve.tensor_copy(MT[:, 2 * k:2 * k + 2, 0:256],
                                bank[4 + (6 + k) % 4][:, :].rearrange("p (t c) -> p t c", t=2)).then_inc(s5_used, 1)
            dve.wait_ge(par_in, 12 * 16)
            lam = small[:, 64:64 + 4 * HD].rearrange("p (m k d) -> p m k d", m=2, k=2)
            prod = small[:, 352:480].rearrange("p (m d) -> p m d", m=2)
            link(dve.tensor_tensor(prod, lam[:, :, 0, :], lam[:, :, 1, :], ALU.mult))
            dve.tensor_reduce(small[:, 26:28], prod, AX.X, ALU.add).then_inc(s5_dve, 2)
            dve.wait_ge(lam_exp, 1)
            link(dve.tensor_tensor(small[:, 25:26], small[:, 29:30], small[:, 28:29], ALU.subtract))
            link(dve.tensor_scalar(small[:, 25:26], small[:, 25:26], -LAM_INIT, None, ALU.add))
            ch.did(dve.tensor_scalar(small[:, 30:31], small[:, 24:25], 1.0 - LAM_INIT, None, ALU.mult))
            dve.wait_ge(mult_ready, 1)
            dve.wait_ge(s5_dve, 6)
            v, f = att[:, 0:1024], att[:, 1024:2048]
            turn_q = scan_par[:, PAIRS:2 * PAIRS].unsqueeze(2).to_broadcast([P, PAIRS, 32])
            times = small[:, 320:352].unsqueeze(1).to_broadcast([P, PAIRS, 32])
            link(dve.tensor_tensor(v.rearrange("p (q e) -> p q e", e=32), turn_q, times, ALU.mult))
            link(dve.tensor_copy(c_rows[:, 0:1024].bitcast(I32), v))
            link(dve.tensor_copy(f, c_rows[:, 0:1024].bitcast(I32)))
            link(dve.tensor_tensor(v, v, f, ALU.subtract))
            dve.scalar_tensor_tensor(f, v, -1.0, v, ALU.mult, ALU.max).then_inc(s5_dve, 1)

            dve.wait_ge(toep_in, 32)
            bias3 = bias.rearrange("p (h x) -> p h x", h=H)
            x04 = x0[:, :].rearrange("p (r b q) -> p r b q", r=2, b=B)

            def states(t, p):
                n = 4 * t + p
                q = bass.ds(n, 1)

                def par(k):
                    return scan_par[:, bass.ds(k * PAIRS + n, 1)]

                def old(r):
                    return x04[:, r, :, q].rearrange("p b o -> p (b o)")

                cos, sin = tab[p % 2][:, 0:256], tab[p % 2][:, 256:512]
                re, im = bank[6], bank[7]
                x_re, x_im = x_st[p % 2][:, 0:N], x_st[p % 2][:, N:2 * N]
                s_re, s_im = small[:, 400:408], small[:, 408:416]
                dve.wait_ge(tab_ready, n + 1)
                dve.wait_ge(b_done, n + 1)
                wait(dve, xs_ready, n)
                ch.did(dve.tensor_tensor(rot[0], re[:, 0:T], cos, ALU.mult))
                n1 = ch.did(dve.tensor_tensor(rot[1], im[:, 0:T], sin, ALU.mult))
                ch.did(dve.tensor_tensor(rot[2], im[:, 0:T], cos, ALU.mult))
                n2 = ch.did(dve.tensor_tensor(rot[3], re[:, 0:T], sin, ALU.mult))
                ch.did(dve.scalar_tensor_tensor(s_re, old(0), par(2), re[:, T:N], ALU.mult, ALU.add))
                dve.scalar_tensor_tensor(s_im, old(1), par(2), im[:, T:N], ALU.mult, ALU.add).then_inc(b_read, 1)
                ch.wait(n1)
                n1 = ch.did(dve.tensor_tensor(z_re, rot[0], rot[1], ALU.add))
                ch.wait(n2)
                n2 = ch.did(dve.tensor_tensor(z_im, rot[2], rot[3], ALU.subtract))
                decay = par(0).to_broadcast([P, T])
                ch.wait(n1)
                n1 = ch.did(dve.tensor_tensor_scan(y_re, decay, z_re, 0.0, ALU.mult, ALU.add))
                ch.wait(n2)
                n2 = ch.did(dve.tensor_tensor_scan(y_im, decay, z_im, 0.0, ALU.mult, ALU.add))
                wait(dve, c_done, n - 1)
                wait(dve, xf_read, n - 1)
                dve.wait_ge(b_read, n + 1)
                ch.did(dve.scalar_tensor_tensor(x_re[:, T:N], old(1), par(6), s_re, ALU.mult, ALU.add))
                ch.did(dve.scalar_tensor_tensor(x_im[:, T:N], old(0), par(3), s_im, ALU.mult, ALU.add))
                ch.wait(n1)
                ch.did(dve.tensor_tensor(rot[0], y_re, cos, ALU.mult))
                ch.did(dve.tensor_tensor(rot[2], y_re, sin, ALU.mult))
                ch.wait(n2)
                n1 = ch.did(dve.tensor_tensor(rot[1], y_im, sin, ALU.mult))
                n2 = ch.did(dve.tensor_tensor(rot[3], y_im, cos, ALU.mult))
                ch.wait(n1)
                ch.did(dve.tensor_tensor(x_re[:, 0:T], rot[0], rot[1], ALU.subtract))
                ch.wait(n2)
                dve.tensor_tensor(x_im[:, 0:T], rot[2], rot[3], ALU.add).then_inc(xs_ready, 1)

            def maxima(i):
                dve.wait_ge(sc_done, i + 1)
                wait(dve, exp_done, i)
                for j in range(2):
                    n1 = ch.did(dve.scalar_tensor_tensor(
                        s_sb[:, 384 * j:384 * (j + 1)], bank[4 + j][:, 0:384], HD ** -0.5,
                        bias3[:, bass.ds(i, 1), :].rearrange("p o x -> p (o x)"), ALU.mult, ALU.add))
                ch.wait(n1)
                s3 = s_sb.rearrange("p (j x) -> p j x", j=2)
                ch.did(dve.tensor_reduce(small[:, 420:422], s3[:, :, 0:256], AX.X, ALU.max, negate=True))
                dve.tensor_reduce(small[:, 422:424], s3[:, :, 256:384], AX.X, ALU.max, negate=True).then_inc(max_ready, 1)

            def differences(i):
                dve.wait_ge(exp_done, i + 1)
                wait(dve, pdt_done, i)
                link(dve.reciprocal(small[:, 428:432], small[:, 424:428]))
                second = small[:, 428:432].rearrange("p (k j) -> p k j", j=2)[:, :, 1]
                n1 = ch.did(dve.tensor_scalar(second, second, small[:, 25:26], None, ALU.mult))
                ch.did(dve.tensor_scalar(p_diff[:, 0:256], p_sb[:, 0:256], small[:, 428:429], None, ALU.mult))
                n2 = ch.did(dve.tensor_scalar(p_diff[:, 256:384], p_sb[:, 256:384], small[:, 430:431], None, ALU.mult))
                ch.wait(n2)
                ch.did(dve.scalar_tensor_tensor(p_diff[:, 0:256], p_sb[:, 384:640], small[:, 429:430],
                                                p_diff[:, 0:256], ALU.mult, ALU.add))
                dve.scalar_tensor_tensor(p_diff[:, 256:384], p_sb[:, 640:768], small[:, 431:432],
                                         p_diff[:, 256:384], ALU.mult, ALU.add).then_inc(pd_ready, 1)

            def y_out(t):
                dve.wait_ge(c_done, 4 * t + 4)
                dve.scalar_tensor_tensor(yg[:, bass.ds(t * N, N)], u_all[:, bass.ds(t * N, N)],
                                         small[:, bass.ds(16 + t, 1)], bank[3][:, 0:N], ALU.mult, ALU.add
                                         ).then_inc(y_ready, 1)

            def head(i, first=False):
                t = i - 1
                if not first:
                    states(t - 1, 3)
                    y_out(t - 1)
                states(t, 0)
                maxima(i - 1)
                states(t, 1)
                differences(i - 1)
                states(t, 2)

            head(1, first=True)
            with dve.Fori(2, H + 1) as i:
                ch.enter(i, 2, 4 * 16 + 3 + 5)
                head(i)
            ch.leave(H - 1)
            def diag(b):
                wait(dve, qb_done, b)
                query = q_s[:, :].rearrange("p (h b) -> p h b", h=H)[:, :, bass.ds(b, 1)].to_broadcast([P, H, P])
                dve.tensor_tensor(diag_q.rearrange("p (h m) -> p h m", h=H),
                                  ident[:, :].unsqueeze(1).to_broadcast([P, H, P]), query, ALU.mult).then_inc(dq_ready, 1)

            dve.wait_ge(mst_ready, HT)
            dve.wait_ge(z_read, L1)
            diag(0)
            states(HT - 1, 3)
            y_out(HT - 1)
            gelu_t = mm[:, H * N:2 * H * N]
            dve.wait_ge(gelu_act, 1)
            link(dve.tensor_scalar(gelu_t, gelu_t, 0.044715, 1.0, ALU.mult, ALU.add))
            dve.tensor_tensor(gelu_t, gelu_t, yg[:, :], ALU.mult).then_inc(gelu_dve, 1)
            dve.wait_ge(gelu_act, 2)
            dve.scalar_tensor_tensor(yg[:, :], gelu_t, 1.0, yg[:, :], ALU.add, ALU.mult).then_inc(gelu_dve, 1)

            def weights(b):
                dve.wait_ge(lsum_done, b + 1)
                wait(dve, ocomb_done, b)
                link(dve.reciprocal(small[:, 560:576], bank[7][:, 0:16]))
                link(dve.tensor_tensor(small[:, 560:576], small[:, 560:576], small[:, 352:368], ALU.mult))
                dve.tensor_reduce(small[:, 576:584], small[:, 560:576].rearrange("p (h j) -> p h j", j=2), AX.X,
                                  ALU.add).then_inc(w_ready, 1)

            def sample_out(b):
                dve.wait_ge(ocomb_done, b + 1)
                dst = att[:, :].rearrange("p (h n) -> p h n", h=H)[:, :, bass.ds(T + b, 1)].rearrange("p h o -> p (h o)")
                dve.tensor_copy(dst, bank[6][:, 0:H]).then_inc(o_read, 1)

            def decode(b, summed, more=True):
                if summed:
                    weights(b - 1)
                if more:
                    diag(b + 1)
                for p in range(PAGES + 1):
                    dve.wait_ge(kq_ready, 17 * b + p + 1)
                    dve.tensor_reduce(score[:, p * 16:(p + 1) * 16], kq[p % 2].rearrange("p (m d) -> p m d", d=HD),
                                      AX.X, ALU.add).then_inc(kq_read, 1)
                dve.wait_ge(kq_read, 17 * b + 17)
                s4 = score.rearrange("p (g h j) -> p g h j", h=H, j=2)
                for j in range(2):
                    ch.did(dve.tensor_tensor(s4[:, 0:PAGES, :, j], s4[:, 0:PAGES, :, j],
                                             bias_pg[:, :].rearrange("p (g h) -> p g h", h=H), ALU.add))
                    ch.did(dve.tensor_tensor(s4[:, PAGES, :, j], s4[:, PAGES, :, j],
                                             bias_nw[:, bass.ds(b * H, H)], ALU.add))
                ch.wait()
                dve.tensor_reduce(small[:, 512:528], score.rearrange("p (g c) -> p c g", c=16), AX.X,
                                  ALU.max).then_inc(smax_ready, 1)
                dve.wait_ge(gmax_ready, b + 1)
                s3 = score.rearrange("p (g c) -> p g c", c=16)
                dve.tensor_tensor(s3, s3, small[:, 528:544].unsqueeze(1).to_broadcast([P, PAGES + 1, 16]),
                                  ALU.subtract).then_inc(ssub_ready, 1)
                if summed:
                    sample_out(b - 1)
                dve.wait_ge(sexp_ready, b + 1)
                wait(dve, lsum_done, b)
                dve.tensor_reduce(small[:, 544:560], prob.rearrange("p (g c) -> p c g", c=16), AX.X,
                                  ALU.add).then_inc(lsum_ready, 1)

            signs = small[:, 352:368].rearrange("p (g h j) -> p g h j", g=4, j=2)
            for g in range(4):
                pick = ident[:, 36 * g:36 * g + 4].rearrange("p (h j) -> p h j", j=2)
                ch.did(dve.tensor_scalar(signs[:, g, :, 0], pick[:, :, 0], 1.0, None, ALU.mult))
                ch.did(dve.tensor_scalar(signs[:, g, :, 1], pick[:, :, 1], small[:, 25:26], None, ALU.mult))
            ch.wait()
            decode(0, False)
            dve.wait_ge(root_ready, 4)
            link(dve.reciprocal(sq_prompt, sq_prompt))
            link(dve.scalar_tensor_tensor(att3[:, :, 0:T], att3[:, :, 0:T], small[:, 30:31],
                                     sq_prompt.rearrange("p (h n) -> p h n", h=H), ALU.mult, ALU.mult))
            dve.memset(o_rows, 0.0).then_inc(att_ready, 1)
            with dve.Fori(1, B - 1) as b:
                ch.enter(b, 1, 6)
                decode(b, True)
            ch.leave(B - 2)
            decode(B - 1, True, False)
            weights(B - 1)
            dve.wait_ge(out_stored, 9 * 16)
            dve.wait_ge(z_read, GLU + HT)
            link(dve.scalar_tensor_tensor(glu, glu, 1.0, yg[:, :], ALU.add, ALU.mult))
            link(dve.tensor_copy(s_hi[:, :].bitcast(F32R), glu))
            dve.tensor_tensor(s_lo[:, :].bitcast(F32R), glu, s_hi[:, :], ALU.subtract).then_inc(ssm_ready, 1)

            def split_att(cols):
                hi, lo = (t[:, :].rearrange("p (h n) -> p h n", h=H)[:, :, cols] for t in (a_hi, a_lo))
                link(dve.tensor_copy(hi.bitcast(F32R), att3[:, :, cols]))
                return dve.tensor_tensor(lo.bitcast(F32R), att3[:, :, cols], hi, ALU.subtract)

            ch.did(split_att(slice(0, T)))
            sample_out(B - 1)
            dve.wait_ge(root_ready, 5)
            link(dve.reciprocal(root_sample, root_sample))
            link(dve.scalar_tensor_tensor(att3[:, :, T:N], att3[:, :, T:N], small[:, 30:31],
                                          root_sample.rearrange("p (h b) -> p h b", h=H), ALU.mult, ALU.mult))
            split_att(slice(T, N)).then_inc(att_ready, 1)

            def merge(i):
                for j in range(4):
                    n = 4 * i + j
                    one, two = (yg[:, k * 2 * N + (j % 2) * N:k * 2 * N + (j % 2 + 1) * N] for k in range(2))
                    wait(dve, merged_ready, n - 1)
                    dve.wait_ge(slot_done, PROJ0 + n + 1)
                    n1 = ch.did(dve.scalar_tensor_tensor(one, gate[:, bass.ds(n * N, N)], 1.0, bank[j % 2][:, 0:N],
                                                         ALU.add, ALU.mult))
                    dve.scalar_tensor_tensor(two, gate[:, bass.ds((KT + n) * N, N)], 1.0, bank[2 + j % 2][:, 0:N],
                                             ALU.add, ALU.mult).then_inc(zv_read, 1)
                    ch.wait(n1)
                    dve.wait_ge(zv_read, n + 1)
                    link(dve.scalar_tensor_tensor(one, two, 0.25, one, ALU.mult, ALU.add))
                    link(dve.tensor_copy(m_hi[:, bass.ds(n * N, N)].bitcast(F32R), one))
                    dve.tensor_tensor(m_lo[:, bass.ds(n * N, N)].bitcast(F32R), one, m_hi[:, bass.ds(n * N, N)],
                                      ALU.subtract).then_inc(merged_ready, 1)

            merge(0)
            with dve.Fori(1, 4) as i:
                ch.enter(i, 1, 12)
                merge(i)
            ch.leave(3)

            def residual(n, j, count):
                dve.wait_ge(slot_done, count)
                tile = xt[:, bass.ds(n * N, N)]
                dve.scalar_tensor_tensor(tile, tile, 2 * ALPHA, bank[j % 2][:, 0:N], ALU.mult, ALU.add).then_inc(zv_read, 1)

            def norm(ln):
                dve.wait_ge(mean_done, ln + 1)
                for g in range(4):
                    c3 = x3[:, 4 * g:4 * g + 4, :]
                    dve.tensor_tensor(c3, c3, bank[6][:, 0:N].unsqueeze(1).to_broadcast([P, 4, N]),
                                      ALU.subtract).then_inc(cent_ready, 1)
                dve.wait_ge(std_ready, ln + 1)
                link(dve.reciprocal(std_sb, std_sb))
                for g in range(4):
                    c3 = x3[:, 4 * g:4 * g + 4, :]
                    dve.tensor_tensor(c3, c3, std_sb.unsqueeze(1).to_broadcast([P, 4, N]), ALU.mult).then_inc(norm_ready, 1)

            with dve.Fori(0, KT // 4) as n:
                for j in range(4):
                    residual(4 * n + j, j, PROJ + 4 * n + j + 1)
            norm(0)
            for k in range(KT):
                dve.wait_ge(hn_ready, k + 1)
                cols = slice(k * N, (k + 1) * N)
                link(dve.tensor_copy(h_hi[:, cols].bitcast(F32R), h_tmp[k % 4]))
                dve.tensor_tensor(h_lo[:, cols].bitcast(F32R), h_tmp[k % 4], h_hi[:, cols], ALU.subtract).then_inc(h_ready, 1)

            state3 = conv_state[:, :].rearrange("p (t b i) -> p t b i", b=B, i=2)

            def up(n, pairs):
                for q in range(pairs):
                    for v in range(2):
                        t = 2 * q + v
                        tile = 2 * n + q + v * FT
                        y, ps = acc[t], bank[t]

                        def par(w):
                            return conv_par[:, bass.ds(w * 2 * FT + tile, 1)]

                        def old(i):
                            return state3[:, bass.ds(tile, 1), :, i].rearrange("p o b -> p (o b)")

                        dve.wait_ge(tap0, 4 * n + t + 1)
                        n1 = ch.did(dve.scalar_tensor_tensor(y[:, 1:T], ps[:, 0:T - 1], par(1), y[:, 1:T], ALU.mult, ALU.add))
                        n2 = ch.did(dve.scalar_tensor_tensor(y[:, T:N], old(1), par(1), y[:, T:N], ALU.mult, ALU.add))
                        ch.wait(n1)
                        dve.scalar_tensor_tensor(y[:, 2:T], ps[:, 0:T - 2], par(0), y[:, 2:T], ALU.mult, ALU.add
                                                 ).then_inc(zv_read, 1)
                        ch.wait(n2)
                        dve.scalar_tensor_tensor(y[:, T:N], old(0), par(0), y[:, T:N], ALU.mult, ALU.add
                                                 ).then_inc(tap_done, 1)
                    dve.wait_ge(th_ready, 2 * n + q + 1)
                    link(dve.scalar_tensor_tensor(th[q], th[q], 1.0, acc[2 * q], ALU.add, ALU.mult))
                    dve.wait_ge(tap_done, 4 * n + 2 * q + 2)
                    hidden = bass.ds((2 * n + q) * N, N)
                    link(dve.tensor_tensor(th[q], th[q], acc[2 * q + 1], ALU.mult))
                    link(dve.tensor_copy(hid_hi[:, hidden].bitcast(F32R), th[q]))
                    dve.tensor_tensor(hid_lo[:, hidden].bitcast(F32R), th[q], hid_hi[:, hidden], ALU.subtract
                                      ).then_inc(hid_ready, 1)

            up(0, 2)
            with dve.Fori(1, FT // 2) as n:
                ch.enter(n, 1, 14)
                up(n, 2)
            ch.leave(FT // 2 - 1)
            up(FT // 2, 1)
            with dve.Fori(0, KT // 4) as n:
                ch.enter(n, 0, 4)
                for j in range(4):
                    tile = bass.ds(4 * n * N + j * N, N)
                    dve.wait_ge(slot_done, 12 * n + UP + 3 * j + 3)
                    link(dve.scalar_tensor_tensor(xt[:, tile], h_hi[:, tile], 2 * ALPHA, bank[j % 2][:, 0:N], ALU.mult, ALU.add))
                    dve.scalar_tensor_tensor(xt[:, tile], h_lo[:, tile], 2 * ALPHA, xt[:, tile], ALU.mult, ALU.add
                                             ).then_inc(zv_read, 1)
            ch.leave(KT // 4)
            norm(1)
            for c in range(3):
                rows = min(P, N - c * P)
                for g in range(4):
                    n = 4 * c + g
                    dve.wait_ge(yt_done, n + 1)
                    dve.tensor_copy(big[0:rows, c * D + g * 512:c * D + (g + 1) * 512], bank[n % 4][0:rows, :]
                                    ).then_inc(yt_read, 1)


_OUTS = [
    ("y_prompt", (T, D), (1, T, D)),
    ("y_sample", (B, D), (B, 1, D)),
    ("k_prompt", (T, KW), (1, 1, T, H, 2, HD)),
    ("v_prompt", (T, SW), (1, 1, T, H, P)),
    ("ssm_re_prompt", (PAIRS, P), (1, 1, G, S)),
    ("ssm_im_prompt", (PAIRS, P), (1, 1, G, S)),
    ("conv_prompt", (2, 2 * FF), (1, 1, 2, 2 * FF)),
    ("k_sample", (B, KW), (1, B, 1, H, 2, HD)),
    ("v_sample", (B, SW), (1, B, 1, H, P)),
    ("ssm_re_sample", (B * PAIRS, P), (1, B, G, S)),
    ("ssm_im_sample", (B * PAIRS, P), (1, B, G, S)),
    ("conv_sample", (1, B, 2, 2 * FF), (1, B, 2, 2 * FF)),
]


def kernel(**inputs):
    import concourse.bacc as _bacc
    from concourse.bass_utils import run_bass_kernel_spmd as _run

    nc = _bacc.Bacc("TRN2", target_bir_lowering=False, num_devices=1)
    arrays, args, outs = {}, {}, {}
    named = {name: np.ascontiguousarray(array) for name, array in inputs.items()}
    named["buckets"] = bucket_table()
    for name, array in named.items():
        arrays[f"in_{name}"] = array
        args[name] = nc.dram_tensor(f"in_{name}", array.shape, mybir.dt.from_np(array.dtype), kind="ExternalInput").ap()
    for name, shape, _ in _OUTS:
        outs[name] = nc.dram_tensor(f"out_{name}", shape, F32, kind="ExternalOutput").ap()
    scratch = nc.dram_tensor("toeplitz_rows", (H, P, 384), F32, kind="Internal").ap()
    build(nc, args, outs, scratch)
    r = _run(nc, [arrays], core_ids=[0])
    return tuple(np.asarray(r.results[0][f"out_{name}"]).reshape(shape) for name, _, shape in _OUTS)
```
